# Optimizing a Trainium2 kernel written in Bass

```python
import jax
import jax.numpy as jnp
from jax import lax
import numpy as np
import math
import jax, jax.numpy as jnp

D_MODEL = 1024
BATCH = 1
SEQ = 512
DEPTH = 1

GRID_W = 64
CTX_LEN = 256
RET_HEADS = 4
RET_DK = 128
RET_DV = 128
RET_CHUNK = 128
GLA_HEADS = 4
GLA_DK = 64
GLA_DV = 128
GLA_RANK = 16
GLA_TAU = 16.0
GLA_CHUNK = 64
RET_WIDTH = RET_HEADS * RET_DV
GLA_WIDTH = GLA_HEADS * GLA_DV
D_MIX = RET_WIDTH + GLA_WIDTH
D_FF = 2816
N_MOD = 9
ROPE_BASE = 10000.0
EPS = 1e-6
IN_WIDTHS = (RET_HEADS * RET_DK, RET_HEADS * RET_DK, RET_WIDTH, RET_WIDTH,
             GLA_HEADS * GLA_DK, GLA_HEADS * GLA_DK, GLA_WIDTH, GLA_WIDTH, GLA_RANK, GLA_RANK)
IN_COLS = sum(IN_WIDTHS)
IN_SPLITS = tuple(int(v) for v in np.cumsum(IN_WIDTHS)[:-1])


def rms_norm(x, w):
    xf = x.astype(jnp.float32)
    y = xf * lax.rsqrt(jnp.mean(xf * xf, axis=-1, keepdims=True) + EPS)
    return (y * w.astype(jnp.float32)).astype(x.dtype)

def modulate(h, shift, scale):
    return h * (1.0 + scale[:, None, :]) + shift[:, None, :]

def swiglu(h, w1, w3, w2):
    return (jax.nn.silu(h @ w1) * (h @ w3)) @ w2

def split_heads(t, n_heads):
    b, n, _ = t.shape
    return t.reshape(b, n, n_heads, -1).transpose(0, 2, 1, 3).astype(jnp.float32)

def merge_heads(t):
    b, h, n, d = t.shape
    return t.transpose(0, 2, 1, 3).reshape(b, n, h * d)

def rotate(x, ang):
    x1, x2 = jnp.split(x, 2, axis=-1)
    cos, sin = jnp.cos(ang), jnp.sin(ang)
    return jnp.concatenate([x1 * cos - x2 * sin, x1 * sin + x2 * cos], axis=-1)

def grid_rope(x, n_tok):
    rows = n_tok // GRID_W
    row = jnp.repeat(jnp.arange(rows, dtype=jnp.float32), GRID_W)
    col = jnp.tile(jnp.arange(GRID_W, dtype=jnp.float32), rows)
    n_freq = x.shape[-1] // 4
    freqs = ROPE_BASE ** (-jnp.arange(n_freq, dtype=jnp.float32) / n_freq)
    xr, xc = jnp.split(x, 2, axis=-1)
    return jnp.concatenate([rotate(xr, row[:, None] * freqs), rotate(xc, col[:, None] * freqs)], axis=-1)

def to_chunks(t, c):
    b, h, n, d = t.shape
    return t.reshape(b, h, n // c, c, d).transpose(2, 0, 1, 3, 4)

def from_chunks(t):
    nc, b, h, c, d = t.shape
    return t.transpose(1, 2, 0, 3, 4).reshape(b, h, nc * c, d)

def retention_chunked(q, k, v, s0, log_gamma):
    c = RET_CHUNK
    pos = jnp.arange(c, dtype=jnp.float32)
    diff = pos[:, None] - pos[None, :]
    lg = log_gamma[:, None, None]
    decay = jnp.exp(jnp.where(diff >= 0, diff * lg, -jnp.inf))
    q_dec = jnp.exp((pos + 1.0) * log_gamma[:, None])[..., None]
    k_dec = jnp.exp((c - 1.0 - pos) * log_gamma[:, None])[..., None]
    chunk_dec = jnp.exp(c * log_gamma)[:, None, None]

    def step(s, xs):
        qc, kc, vc = xs
        scores = jnp.einsum('bhid,bhjd->bhij', qc, kc) * decay
        o = jnp.einsum('bhij,bhje->bhie', scores, vc) + jnp.einsum('bhid,bhde->bhie', qc * q_dec, s)
        s = chunk_dec * s + jnp.einsum('bhjd,bhje->bhde', kc * k_dec, vc)
        return s, o

    s_fin, o = lax.scan(step, s0, (to_chunks(q, c), to_chunks(k, c), to_chunks(v, c)))
    return from_chunks(o), s_fin

def gla_chunked(q, k, v, g, s0):
    c = GLA_CHUNK
    tri = jnp.tril(jnp.ones((c, c), dtype=bool))

    def step(s, xs):
        qc, kc, vc, gc = xs
        b = jnp.cumsum(gc, axis=-2)
        rel = b[:, :, :, None, :] - b[:, :, None, :, :]
        rel = jnp.exp(jnp.where(tri[:, :, None], rel, -jnp.inf))
        scores = jnp.einsum('bhid,bhjd,bhijd->bhij', qc, kc, rel)
        o = jnp.einsum('bhij,bhje->bhie', scores, vc) + jnp.einsum('bhid,bhde->bhie', qc * jnp.exp(b), s)
        b_last = b[:, :, -1:, :]
        s = jnp.exp(b_last[:, :, 0, :])[..., None] * s + jnp.einsum('bhjd,bhje->bhde', kc * jnp.exp(b_last - b), vc)
        return s, o

    s_fin, o = lax.scan(step, s0, (to_chunks(q, c), to_chunks(k, c), to_chunks(v, c), to_chunks(g, c)))
    return from_chunks(o), s_fin

def bidir_prefix(scan_f, scan_b, lat_f, lat_b, ctx_f, ctx_b):
    flip = lambda ts: tuple(t[:, :, ::-1] for t in ts)
    q0, v0 = ctx_f[0], ctx_f[2]
    s0 = jnp.zeros(q0.shape[:2] + (q0.shape[-1], v0.shape[-1]), jnp.float32)
    o_cf, s_f = scan_f(*ctx_f, s0)
    o_cb, s_b = scan_b(*flip(ctx_b), s0)
    o_lf, _ = scan_f(*lat_f, s_f)
    o_lb, _ = scan_b(*flip(lat_b), s_b)
    return o_lf + o_lb[:, :, ::-1], o_cf + o_cb[:, :, ::-1]

def retention_inputs(p, n_tok):
    q = split_heads(p[0], RET_HEADS) * (RET_DK ** -0.5)
    k = split_heads(p[1], RET_HEADS)
    if n_tok is not None:
        q, k = grid_rope(q, n_tok), grid_rope(k, n_tok)
    return (q, k, split_heads(p[2], RET_HEADS))

def gla_inputs(p, w_f, b_f, w_b, b_b):
    q = split_heads(p[4], GLA_HEADS) * (GLA_DK ** -0.5)
    k = split_heads(p[5], GLA_HEADS)
    v = split_heads(p[6], GLA_HEADS)
    g_f = split_heads(jax.nn.log_sigmoid((p[8] @ w_f + b_f).astype(jnp.float32)), GLA_HEADS) / GLA_TAU
    g_b = split_heads(jax.nn.log_sigmoid((p[9] @ w_b + b_b).astype(jnp.float32)), GLA_HEADS) / GLA_TAU
    return (q, k, v, g_f), (q, k, v, g_b)

def merge_outputs(o_ret, o_gla, p, ret_norm_w, gla_norm_w, w_out, dtype):
    mu = jnp.mean(o_ret, axis=-1, keepdims=True)
    var = jnp.mean(jnp.square(o_ret - mu), axis=-1, keepdims=True)
    r = merge_heads((o_ret - mu) * lax.rsqrt(var + EPS)) * ret_norm_w * jax.nn.silu(p[3].astype(jnp.float32))
    gl = merge_heads(o_gla * lax.rsqrt(jnp.mean(o_gla * o_gla, axis=-1, keepdims=True) + EPS))
    gl = gl * gla_norm_w * jax.nn.silu(p[7].astype(jnp.float32))
    return jnp.concatenate([r, gl], axis=-1).astype(dtype) @ w_out

def token_mixing(h_lat, h_ctx, w_in, ret_decay_f, ret_decay_b, ret_norm_w,
                 gla_gate_w_f, gla_gate_b_f, gla_gate_w_b, gla_gate_b_b, gla_norm_w, w_out, with_ctx):
    n_lat = h_lat.shape[1]
    p_lat = jnp.split(h_lat @ w_in, IN_SPLITS, axis=-1)
    p_ctx = jnp.split(h_ctx @ w_in, IN_SPLITS, axis=-1)
    lg_f = jax.nn.log_sigmoid(ret_decay_f.astype(jnp.float32))
    lg_b = jax.nn.log_sigmoid(ret_decay_b.astype(jnp.float32))
    ret_lat = retention_inputs(p_lat, n_lat)
    ret_ctx = retention_inputs(p_ctx, None)
    o_ret_l, o_ret_c = bidir_prefix(lambda q, k, v, s: retention_chunked(q, k, v, s, lg_f),
                                    lambda q, k, v, s: retention_chunked(q, k, v, s, lg_b),
                                    ret_lat, ret_lat, ret_ctx, ret_ctx)
    gla_lat_f, gla_lat_b = gla_inputs(p_lat, gla_gate_w_f, gla_gate_b_f, gla_gate_w_b, gla_gate_b_b)
    gla_ctx_f, gla_ctx_b = gla_inputs(p_ctx, gla_gate_w_f, gla_gate_b_f, gla_gate_w_b, gla_gate_b_b)
    o_gla_l, o_gla_c = bidir_prefix(gla_chunked, gla_chunked, gla_lat_f, gla_lat_b, gla_ctx_f, gla_ctx_b)
    y_lat = merge_outputs(o_ret_l, o_gla_l, p_lat, ret_norm_w, gla_norm_w, w_out, h_lat.dtype)
    y_ctx = None
    if with_ctx:
        y_ctx = merge_outputs(o_ret_c, o_gla_c, p_ctx, ret_norm_w, gla_norm_w, w_out, h_ctx.dtype)
    return y_lat, y_ctx

def first_inputs(seed: int = 0) -> dict:
    key = jax.random.key(seed)
    ks = jax.random.split(key, 32)
    f32 = jnp.float32

    def nrm(k, shape, scale):
        return jax.random.normal(k, shape, f32) * scale

    def gain(k, shape):
        return 1.0 + 0.05 * jax.random.normal(k, shape, f32)

    decay_logit = jnp.log(2.0 ** (5.0 + jnp.arange(RET_HEADS, dtype=f32)) - 1.0)
    return {
        "x": nrm(ks[0], (BATCH, SEQ, D_MODEL), 1.0),
        "c": nrm(ks[1], (BATCH, D_MODEL), 1.0),
        "ctx": nrm(ks[2], (BATCH, CTX_LEN, D_MODEL), 1.0),
        "c_ctx": nrm(ks[3], (D_MODEL,), 1.0),
        "ada_w": nrm(ks[4], (DEPTH, D_MODEL, N_MOD * D_MODEL), 0.5 * D_MODEL ** -0.5),
        "ada_b": nrm(ks[5], (DEPTH, N_MOD * D_MODEL), 0.02),
        "norm1_w": gain(ks[6], (DEPTH, D_MODEL)),
        "ffn1_w1": nrm(ks[7], (DEPTH, D_MODEL, D_FF), D_MODEL ** -0.5),
        "ffn1_w3": nrm(ks[8], (DEPTH, D_MODEL, D_FF), D_MODEL ** -0.5),
        "ffn1_w2": nrm(ks[9], (DEPTH, D_FF, D_MODEL), D_FF ** -0.5),
        "norm2_w": gain(ks[10], (DEPTH, D_MODEL)),
        "w_in": nrm(ks[11], (DEPTH, D_MODEL, IN_COLS), D_MODEL ** -0.5),
        "ret_decay_f": decay_logit + 0.1 * jax.random.normal(ks[12], (DEPTH, RET_HEADS), f32),
        "ret_decay_b": decay_logit + 0.1 * jax.random.normal(ks[13], (DEPTH, RET_HEADS), f32),
        "ret_norm_w": gain(ks[14], (DEPTH, RET_WIDTH)),
        "gla_gate_w_f": nrm(ks[15], (DEPTH, GLA_RANK, GLA_HEADS * GLA_DK), GLA_RANK ** -0.5),
        "gla_gate_b_f": 1.0 + 0.5 * jax.random.normal(ks[16], (DEPTH, GLA_HEADS * GLA_DK), f32),
        "gla_gate_w_b": nrm(ks[17], (DEPTH, GLA_RANK, GLA_HEADS * GLA_DK), GLA_RANK ** -0.5),
        "gla_gate_b_b": 1.0 + 0.5 * jax.random.normal(ks[18], (DEPTH, GLA_HEADS * GLA_DK), f32),
        "gla_norm_w": gain(ks[19], (DEPTH, GLA_WIDTH)),
        "w_out": nrm(ks[20], (DEPTH, D_MIX, D_MODEL), D_MIX ** -0.5),
        "norm3_w": gain(ks[21], (DEPTH, D_MODEL)),
        "ffn2_w1": nrm(ks[22], (DEPTH, D_MODEL, D_FF), D_MODEL ** -0.5),
        "ffn2_w3": nrm(ks[23], (DEPTH, D_MODEL, D_FF), D_MODEL ** -0.5),
        "ffn2_w2": nrm(ks[24], (DEPTH, D_FF, D_MODEL), D_FF ** -0.5),
        "final_norm_w": gain(ks[25], (D_MODEL,)),
    }

def first_block(x, c, ctx, c_ctx, ada_w, ada_b, norm1_w, ffn1_w1, ffn1_w3, ffn1_w2, norm2_w, w_in,
              ret_decay_f, ret_decay_b, ret_norm_w, gla_gate_w_f, gla_gate_b_f, gla_gate_w_b, gla_gate_b_b,
              gla_norm_w, w_out, norm3_w, ffn2_w1, ffn2_w3, ffn2_w2, final_norm_w):
    cond_lat = jax.nn.silu(c)
    cond_ctx = jax.nn.silu(c_ctx)[None, :]
    for i in range(DEPTH):
        update_ctx = i < DEPTH - 1
        m_l = jnp.split(cond_lat @ ada_w[i] + ada_b[i], N_MOD, axis=-1)
        m_c = jnp.split(cond_ctx @ ada_w[i] + ada_b[i], N_MOD, axis=-1)
        x = x + 0.5 * m_l[2][:, None, :] * swiglu(modulate(rms_norm(x, norm1_w[i]), m_l[0], m_l[1]),
                                                    ffn1_w1[i], ffn1_w3[i], ffn1_w2[i])
        ctx = ctx + 0.5 * m_c[2][:, None, :] * swiglu(modulate(rms_norm(ctx, norm1_w[i]), m_c[0], m_c[1]),
                                                        ffn1_w1[i], ffn1_w3[i], ffn1_w2[i])
        y_l, y_c = token_mixing(modulate(rms_norm(x, norm2_w[i]), m_l[3], m_l[4]),
                                modulate(rms_norm(ctx, norm2_w[i]), m_c[3], m_c[4]),
                                w_in[i], ret_decay_f[i], ret_decay_b[i], ret_norm_w[i],
                                gla_gate_w_f[i], gla_gate_b_f[i], gla_gate_w_b[i], gla_gate_b_b[i],
                                gla_norm_w[i], w_out[i], update_ctx)
        x = x + m_l[5][:, None, :] * y_l
        x = x + 0.5 * m_l[8][:, None, :] * swiglu(modulate(rms_norm(x, norm3_w[i]), m_l[6], m_l[7]),
                                                    ffn2_w1[i], ffn2_w3[i], ffn2_w2[i])
        if update_ctx:
            ctx = ctx + m_c[5][:, None, :] * y_c
            ctx = ctx + 0.5 * m_c[8][:, None, :] * swiglu(modulate(rms_norm(ctx, norm3_w[i]), m_c[6], m_c[7]),
                                                            ffn2_w1[i], ffn2_w3[i], ffn2_w2[i])
    return rms_norm(x, final_norm_w)


N_ATTN_HEADS = 8
HEAD_DIM = 64
ATTN_WIDTH = N_ATTN_HEADS * HEAD_DIM
N_RG_BLOCKS = 8
RG_WIDTH = 512
RG_BLOCK = RG_WIDTH // N_RG_BLOCKS
MIX_WIDTH = ATTN_WIDTH + RG_WIDTH
IN_COLS_2 = 3 * ATTN_WIDTH + 2 * RG_WIDTH
DILATED_PATTERNS = ((128, 1), (512, 4), (2048, 16))
BAND_BLOCK = 64
ROPE_THETA = 10000.0
CONV_WIDTH = 4
CONV_PAD_LEFT = 2
CONV_PAD_RIGHT = 1
RG_C = 8.0
N_MEM = 256
N_CROSS_HEADS = 4
CROSS_HEAD_DIM = 128
CROSS_WIDTH = N_CROSS_HEADS * CROSS_HEAD_DIM
D_FF_2 = 4 * D_MODEL
NORM_EPS = 1e-6
NEG_BIG = -1e30


def rmsnorm(x, g):
    xf = x.astype(jnp.float32)
    return xf * lax.rsqrt(jnp.mean(xf * xf, axis=-1, keepdims=True) + NORM_EPS) * g.astype(jnp.float32)

def rope(t, positions):
    half = t.shape[-1] // 2
    inv_freq = ROPE_THETA ** (-jnp.arange(half, dtype=jnp.float32) / half)
    ang = positions.astype(jnp.float32)[..., None] * inv_freq
    cos = jnp.cos(ang)[:, :, None, :]
    sin = jnp.sin(ang)[:, :, None, :]
    t1, t2 = t[..., :half], t[..., half:]
    return jnp.concatenate([t1 * cos - t2 * sin, t1 * sin + t2 * cos], axis=-1)

def banded_window_attention(q, k, v, radius):
    L, dh = q.shape[-2], q.shape[-1]
    blk = BAND_BLOCK
    nb = -(-L // blk)
    Lp = nb * blk
    lead = q.shape[:-2]
    nlead = len(lead)
    qb = jnp.pad(q, [(0, 0)] * nlead + [(0, Lp - L), (0, 0)]).reshape(*lead, nb, blk, dh)
    pad_both = [(0, 0)] * nlead + [(blk, Lp - L + blk), (0, 0)]
    kb = jnp.pad(k, pad_both).reshape(*lead, nb + 2, blk, dh)
    vb = jnp.pad(v, pad_both).reshape(*lead, nb + 2, blk, dh)
    kn = jnp.concatenate([kb[..., :-2, :, :], kb[..., 1:-1, :, :], kb[..., 2:, :, :]], axis=-2)
    vn = jnp.concatenate([vb[..., :-2, :, :], vb[..., 1:-1, :, :], vb[..., 2:, :, :]], axis=-2)
    s = jnp.einsum('...nqd,...nkd->...nqk', qb, kn) * (dh ** -0.5)
    qpos = jnp.arange(nb)[:, None] * blk + jnp.arange(blk)[None, :]
    kpos = (jnp.arange(nb)[:, None] - 1) * blk + jnp.arange(3 * blk)[None, :]
    dist = qpos[:, :, None] - kpos[:, None, :]
    valid = (jnp.abs(dist) <= radius) & (kpos[:, None, :] >= 0) & (kpos[:, None, :] < L)
    s = jnp.where(valid, s, NEG_BIG)
    m = jnp.max(s, axis=-1, keepdims=True)
    p = jnp.exp(s - m)
    denom = jnp.sum(p, axis=-1, keepdims=True)
    o = jnp.einsum('...nqk,...nkd->...nqd', p, vn) / denom
    lse = (m + jnp.log(denom))[..., 0]
    o = o.reshape(*lead, Lp, dh)[..., :L, :]
    lse = lse.reshape(*lead, Lp)[..., :L]
    return o, lse

def dilated_mixture_attention(q, k, v):
    B, S, H, dh = q.shape
    outs, lses = [], []
    for window, dil in DILATED_PATTERNS:
        L = S // dil

        def to_classes(t):
            return t.reshape(B, L, dil, H, dh).transpose(0, 2, 3, 1, 4)

        o, lse = banded_window_attention(to_classes(q), to_classes(k), to_classes(v), window // (2 * dil))
        outs.append(o.transpose(0, 3, 1, 2, 4).reshape(B, S, H, dh))
        lses.append(lse.transpose(0, 3, 1, 2).reshape(B, S, H))
    w = jax.nn.softmax(jnp.stack(lses, axis=0), axis=0)
    return jnp.sum(w[..., None] * jnp.stack(outs, axis=0), axis=0)

def centred_depthwise_conv(u, w, b):
    out = lax.conv_general_dilated(
        u, w[:, None, :].astype(u.dtype), window_strides=(1,),
        padding=[(CONV_PAD_LEFT, CONV_PAD_RIGHT)],
        dimension_numbers=('NWC', 'WIO', 'NWC'),
        feature_group_count=u.shape[-1])
    return out + b

def _linear_recurrence_combine(c1, c2):
    a1, b1 = c1
    a2, b2 = c2
    return a1 * a2, a2 * b1 + b2

def bidirectional_rglru(u, a_w, a_b, x_w, x_b, lam):
    B, S, _ = u.shape
    ug = u.reshape(B, S, N_RG_BLOCKS, RG_BLOCK)
    r = jax.nn.sigmoid(jnp.einsum('bsgi,zgij->zbsgj', ug, a_w) + a_b[:, None, None]).reshape(2, B, S, RG_WIDTH)
    i = jax.nn.sigmoid(jnp.einsum('bsgi,zgij->zbsgj', ug, x_w) + x_b[:, None, None]).reshape(2, B, S, RG_WIDTH)
    log_a = -RG_C * r * jax.nn.softplus(-lam.astype(jnp.float32))[:, None, None, :]
    a = jnp.exp(log_a)
    b = jnp.sqrt(-jnp.expm1(2.0 * log_a)) * (i * u[None])
    _, h_f = lax.associative_scan(_linear_recurrence_combine, (a[0], b[0]), axis=1)
    _, h_b = lax.associative_scan(_linear_recurrence_combine, (a[1], b[1]), axis=1, reverse=True)
    return h_f + h_b

def memory_cross_attention(xn, memn, wq, wk, wv, wo):
    B, S, _ = xn.shape
    M = memn.shape[1]
    q = (xn @ wq).reshape(B, S, N_CROSS_HEADS, CROSS_HEAD_DIM)
    k = (memn @ wk).reshape(B, M, N_CROSS_HEADS, CROSS_HEAD_DIM)
    v = (memn @ wv).reshape(B, M, N_CROSS_HEADS, CROSS_HEAD_DIM)
    s = jnp.einsum('bshd,bmhd->bhsm', q, k) * (CROSS_HEAD_DIM ** -0.5)
    p = jax.nn.softmax(s, axis=-1)
    o = jnp.einsum('bhsm,bmhd->bshd', p, v).reshape(B, S, CROSS_WIDTH)
    return o @ wo

def second_inputs(seed: int = 0) -> dict:
    key = jax.random.key(seed)
    ks = jax.random.split(key, 24)
    f32 = jnp.float32

    def nrm(k, shape, scale):
        return jax.random.normal(k, shape, f32) * scale

    def gain(k, shape):
        return 1.0 + 0.05 * jax.random.normal(k, shape, f32)

    lam_u = jax.random.uniform(ks[11], (DEPTH, 2, RG_WIDTH), f32, minval=0.9, maxval=0.999)
    a0 = lam_u ** (1.0 / RG_C)
    rg_lambda = jnp.log(a0) - jnp.log1p(-a0)
    return {
        "x": nrm(ks[0], (BATCH, SEQ, D_MODEL), 1.0),
        "mem": nrm(ks[1], (BATCH, N_MEM, D_MODEL), 1.0),
        "positions": jnp.broadcast_to(jnp.arange(SEQ, dtype=jnp.int32), (BATCH, SEQ)),
        "norm_mix_g": gain(ks[2], (DEPTH, D_MODEL)),
        "w_in": nrm(ks[3], (DEPTH, D_MODEL, IN_COLS_2), D_MODEL ** -0.5),
        "conv_w": nrm(ks[4], (DEPTH, CONV_WIDTH, RG_WIDTH), CONV_WIDTH ** -0.5),
        "conv_b": nrm(ks[5], (DEPTH, RG_WIDTH), 0.01),
        "rg_a_w": nrm(ks[6], (DEPTH, 2, N_RG_BLOCKS, RG_BLOCK, RG_BLOCK), RG_BLOCK ** -0.5),
        "rg_a_b": nrm(ks[7], (DEPTH, 2, N_RG_BLOCKS, RG_BLOCK), 0.01),
        "rg_x_w": nrm(ks[8], (DEPTH, 2, N_RG_BLOCKS, RG_BLOCK, RG_BLOCK), RG_BLOCK ** -0.5),
        "rg_x_b": nrm(ks[9], (DEPTH, 2, N_RG_BLOCKS, RG_BLOCK), 0.01),
        "rg_lambda": rg_lambda,
        "w_out": nrm(ks[10], (DEPTH, MIX_WIDTH, D_MODEL), MIX_WIDTH ** -0.5),
        "norm_cross_g": gain(ks[12], (DEPTH, D_MODEL)),
        "norm_mem_g": gain(ks[13], (DEPTH, D_MODEL)),
        "w_cq": nrm(ks[14], (DEPTH, D_MODEL, CROSS_WIDTH), D_MODEL ** -0.5),
        "w_ck": nrm(ks[15], (DEPTH, D_MODEL, CROSS_WIDTH), D_MODEL ** -0.5),
        "w_cv": nrm(ks[16], (DEPTH, D_MODEL, CROSS_WIDTH), D_MODEL ** -0.5),
        "w_co": nrm(ks[17], (DEPTH, CROSS_WIDTH, D_MODEL), CROSS_WIDTH ** -0.5),
        "norm_mlp_g": gain(ks[18], (DEPTH, D_MODEL)),
        "w_mlp_in": nrm(ks[19], (DEPTH, D_MODEL, D_FF_2), D_MODEL ** -0.5),
        "w_mlp_out": nrm(ks[20], (DEPTH, D_FF_2, D_MODEL), D_FF_2 ** -0.5),
        "norm_final_g": gain(ks[21], (D_MODEL,)),
    }

def second_block(x, mem, positions, norm_mix_g, w_in, conv_w, conv_b, rg_a_w, rg_a_b, rg_x_w, rg_x_b,
              rg_lambda, w_out, norm_cross_g, norm_mem_g, w_cq, w_ck, w_cv, w_co,
              norm_mlp_g, w_mlp_in, w_mlp_out, norm_final_g):
    B, S, _ = x.shape
    h = x.astype(jnp.float32)
    memf = mem.astype(jnp.float32)
    for l in range(DEPTH):
        xn = rmsnorm(h, norm_mix_g[l])
        proj = xn @ w_in[l]
        q, k, v, u, y = jnp.split(proj, [ATTN_WIDTH, 2 * ATTN_WIDTH, 3 * ATTN_WIDTH,
                                         3 * ATTN_WIDTH + RG_WIDTH], axis=-1)
        q = rope(q.reshape(B, S, N_ATTN_HEADS, HEAD_DIM), positions)
        k = rope(k.reshape(B, S, N_ATTN_HEADS, HEAD_DIM), positions)
        v = v.reshape(B, S, N_ATTN_HEADS, HEAD_DIM)
        attn = dilated_mixture_attention(q, k, v).reshape(B, S, ATTN_WIDTH)
        uc = centred_depthwise_conv(u, conv_w[l], conv_b[l])
        rec = bidirectional_rglru(uc, rg_a_w[l], rg_a_b[l], rg_x_w[l], rg_x_b[l], rg_lambda[l]) * jax.nn.gelu(y)
        h = h + jnp.concatenate([attn, rec], axis=-1) @ w_out[l]
        h = h + memory_cross_attention(rmsnorm(h, norm_cross_g[l]), rmsnorm(memf, norm_mem_g[l]),
                                       w_cq[l], w_ck[l], w_cv[l], w_co[l])
        hid = jnp.square(jax.nn.relu(rmsnorm(h, norm_mlp_g[l]) @ w_mlp_in[l]))
        h = h + hid @ w_mlp_out[l]
    return rmsnorm(h, norm_final_g).astype(x.dtype)


def setup_inputs(seed=0):
    out = dict(first_inputs(seed))
    for name, value in second_inputs(seed + 1).items():
        if name != "x":
            out[name + "_2"] = value
    return out


def reference(
    x, c, ctx, c_ctx, ada_w, ada_b, norm1_w, ffn1_w1, ffn1_w3, ffn1_w2, norm2_w, w_in,
    ret_decay_f, ret_decay_b, ret_norm_w, gla_gate_w_f, gla_gate_b_f, gla_gate_w_b,
    gla_gate_b_b, gla_norm_w, w_out, norm3_w, ffn2_w1, ffn2_w3, ffn2_w2, final_norm_w, mem_2,
    positions_2, norm_mix_g_2, w_in_2, conv_w_2, conv_b_2, rg_a_w_2, rg_a_b_2, rg_x_w_2,
    rg_x_b_2, rg_lambda_2, w_out_2, norm_cross_g_2, norm_mem_g_2, w_cq_2, w_ck_2, w_cv_2,
    w_co_2, norm_mlp_g_2, w_mlp_in_2, w_mlp_out_2, norm_final_g_2,
):
    x = first_block(
        x, c, ctx, c_ctx, ada_w, ada_b, norm1_w, ffn1_w1, ffn1_w3, ffn1_w2, norm2_w, w_in,
        ret_decay_f, ret_decay_b, ret_norm_w, gla_gate_w_f, gla_gate_b_f, gla_gate_w_b,
        gla_gate_b_b, gla_norm_w, w_out, norm3_w, ffn2_w1, ffn2_w3, ffn2_w2, final_norm_w,
    )
    return second_block(
        x, mem_2, positions_2, norm_mix_g_2, w_in_2, conv_w_2, conv_b_2, rg_a_w_2, rg_a_b_2,
        rg_x_w_2, rg_x_b_2, rg_lambda_2, w_out_2, norm_cross_g_2, norm_mem_g_2, w_cq_2, w_ck_2,
        w_cv_2, w_co_2, norm_mlp_g_2, w_mlp_in_2, w_mlp_out_2, norm_final_g_2,
    )


_drawn_inputs = setup_inputs


def setup_inputs(seed=0):
    import zlib

    import numpy as np

    out = dict(_drawn_inputs(seed))
    spreads = {}
    factors = {'norm1_w': 5.843,
     'ret_norm_w': 6.61,
     'gla_norm_w': 6.976,
     'norm3_w': 6.271,
     'rg_a_b_2': 8.0,
     'rg_x_b_2': 8.0,
     'norm_cross_g_2': 8.0,
     'norm_mem_g_2': 6.988,
     'norm_mlp_g_2': 5.491}
    for name, (base, spread) in spreads.items():
        noise = np.random.default_rng([zlib.crc32(name.encode()), seed]).standard_normal(out[name].shape)
        drawn = base * np.exp(spread * noise) if base else spread * noise
        out[name] = jnp.asarray(drawn.astype(out[name].dtype))
    for name, factor in factors.items():
        out[name] = (out[name] * factor).astype(out[name].dtype)
    return out
```

```python
import math
from contextlib import ExitStack

import numpy as np
import concourse.bass as bass
from concourse import mybir

P = 128
D = 1024
KC = D // P
LAT, CTX = 512, 256
TOK = LAT + CTX
HALF = TOK // 2
DFF = 2816
FF = DFF // P
FF_GROUPS = (8, 8, 6)
assert sum(FF_GROUPS) == FF
DFF2 = 4096
NMOD = 9
EPS = 1e-6
RING = 4
PANEL = KC * P
ADA_RING = 3
ADA_FIRST = 18
ADA_PER_PAIR = (3, 6, 6)
ADA_ROWS = (2, 2, 1)
assert ADA_FIRST + sum(n * g // 2 for n, g in zip(ADA_PER_PAIR, FF_GROUPS)) == NMOD * KC

N_FFN = sum(2 * g + KC for g in FF_GROUPS)
P_FFN1 = 0
P_WIN = P_FFN1 + N_FFN
P_WOUT = P_WIN + 28
P_FFN2 = P_WOUT + 8
P_WIN2 = P_FFN2 + N_FFN
P_WOUT2 = P_WIN2 + 28
P_CQ = P_WOUT2 + 8
P_CO = P_CQ + 4
P_MLP = P_CO + 4
N_PANELS = P_MLP + 2 * DFF2 // P
assert all(p % RING == 0 for p in (P_WIN, P_WOUT, P_FFN2, P_WIN2, P_WOUT2, P_CQ, P_CO, P_MLP, N_PANELS))

VEC_WIDTHS = dict(norm1_w=8, norm2_w=8, norm3_w=8, final_norm_w=8, norm_mix_g_2=8, norm_cross_g_2=8, norm_mem_g_2=8,
                  norm_mlp_g_2=8, norm_final_g_2=8, ada_b=72, ret_norm_w=4, gla_norm_w=4, gla_gate_b_f=2,
                  gla_gate_b_b=2, conv_b_2=4, conv_w_2=16, rg_a_b_2=8, rg_x_b_2=8, rg_lambda_2=8)
VEC_AT, _n = {}, 0
for _k, _w in VEC_WIDTHS.items():
    VEC_AT[_k] = _n
    _n += _w
N_VEC = _n


WIN = [("rq", 0, 1), ("rq", 1, 1), ("rq", 2, 1), ("rq", 3, 1), ("rk", 4, 1), ("rk", 5, 1), ("rk", 6, 1), ("rk", 7, 1),
       ("rv", 8, 4), ("rg", 12, 1), ("rg", 13, 1), ("rg", 14, 1), ("rg", 15, 1), ("gq", 16, 1), ("gq", 17, 1),
       ("gk", 18, 1), ("gk", 19, 1), ("gv", 20, 4), ("gg", 24, 1), ("gg", 25, 1), ("gg", 26, 1), ("gg", 27, 1)]
WIN2 = [("q", 0, 1), ("q", 1, 1), ("q", 2, 1), ("q", 3, 1), ("k", 4, 1), ("k", 5, 1), ("k", 6, 1), ("k", 7, 1), ("v", 8, 4),
        ("u", 12, 1), ("u", 13, 1), ("u", 14, 1), ("u", 15, 1), ("y", 16, 1), ("y", 17, 1), ("y", 18, 1), ("y", 19, 1),
        ("ck", 20, 1), ("ck", 21, 1), ("ck", 22, 1), ("ck", 23, 1), ("cv", 24, 4)]
DH = 64
P_BUFS = 4
TWO_PI = (6.28125, round((2 * math.pi - 6.28125) * 2 ** 21) / 2 ** 21, 2 * math.pi - 6.28125 - round((2 * math.pi - 6.28125) * 2 ** 21) / 2 ** 21)
PI_IN = 3.1415925
ROUND = 1.5 * 2 ** 23
TILES = TOK // P
LT = LAT // P
HEADS = 4
UW = 896
LEVELS = (1, 2, 4, 8, 16, 32, 64)
UNITS = len(LEVELS) + 4
SWAP16 = [(i + 16) % 32 for i in range(32)]


def build(nc, x_t, ctx_t, cond, ada_t, vecs, panels, lr_w, gate_w, decays, rope_grid, u_tab, level_masks, diag2, ident_h,
          mem_t, positions, rope_pp_h, window_bias, rg_w, out):
    f32, f32r, bf16, i32 = mybir.dt.float32, mybir.dt.float32r, mybir.dt.bfloat16, mybir.dt.int32
    ACT, ALU, AX = mybir.ActivationFunctionType, mybir.AluOpType, mybir.AxisListType
    ds = bass.ds

    with ExitStack() as stack:
        KB = 1024
        origin = -(-nc.sbuf_base // 64) * 64

        def at(name, cols, offset, dt=f32, rows=P):
            return nc.alloc_sbuf_tensor_at(name, [rows, cols], dt, offset=origin + offset)

        R_RAW, R_HI, R_LO, R_XL, R_XC, R_H, R_G = 0, 16 * KB, 32 * KB, 48 * KB, 64 * KB, 72 * KB, 120 * KB
        R_TMP, R_ADA, R_VEC = 168 * KB, 180 * KB, 202 * KB

        raw = at("raw", RING * PANEL, R_RAW)
        whi = at("whi", RING * PANEL, R_HI, f32r)
        wlo = at("wlo", RING * PANEL, R_LO, f32r)
        x_lat = at("x_lat", KC * LAT, R_XL)
        x_ctx = at("x_ctx", KC * CTX, R_XC)
        h_hi = at("h_hi", KC * TOK, R_H, f32r)
        h_lo = at("h_lo", KC * TOK, R_H + 24 * KB, f32r)
        g_hi = at("g_hi", KC * TOK, R_G, f32r)
        g_lo = at("g_lo", KC * TOK, R_G + 24 * KB, f32r)
        rstd = at("rstd", TOK, R_G)
        act_a = at("act_a", 2 * TOK, R_TMP)
        prod = at("prod", 2 * TOK, R_TMP + 6 * KB)
        ada_w = at("ada_w", ADA_RING * D, R_ADA)
        cond_b = at("cond_b", 2 * D, R_ADA + 12 * KB)
        ada_prod = at("ada_prod", D, R_ADA + 20 * KB, bf16)
        vec = at("vec", N_VEC, R_VEC)
        mods = at("mods", 2 * NMOD * KC, R_VEC + 800)
        scales = at("scales", 5 * KC, R_VEC + 1408)
        gates = at("gates", 4 * KC, R_VEC + 1664)
        eps_t = at("eps_t", 1, R_VEC + 1792)
        ones_k = at("ones_k", P, R_VEC + 1824)

        lr_raw = at("lr_raw", KC * 32, R_VEC + 2368)
        gate_sb = at("gate_sb", 512, R_VEC + 3392, rows=16)
        ident = at("ident", P, R_VEC + 5440)
        rq = at("rq", HEADS * LAT, R_G)
        rk = at("rk", HEADS * TOK, R_G + 8 * KB)
        rg = at("rg", HEADS * LAT, R_G + 20 * KB)
        gg = at("gg", HEADS * LAT, R_G + 28 * KB)
        gf = at("gf", 2 * TOK, R_G + 36 * KB)
        gb = at("gb", 2 * TOK, R_G + 42 * KB)
        rv = at("rv", LT * 512, R_ADA)
        gv = at("gv", LT * 512, R_ADA + 8 * KB)
        gq = at("gq", 2 * LAT, R_ADA + 16 * KB)
        rv_c = at("rv_c", 2 * 512, R_XC)
        gv_c = at("gv_c", 2 * 512, R_XC + 4 * KB)
        gk = at("gk", 2 * TOK, R_TMP)
        rope_tmp = at("rope_tmp", LAT, R_TMP + 6 * KB)
        rope_cs = at("rope_cs", 2 * LAT, R_TMP + 8 * KB)
        lr_hi = at("lr_hi", KC * 32, R_G, f32r)
        lr_lo = at("lr_lo", KC * 32, R_G + KB, f32r)
        lr_sb = at("lr_sb", TILES * 32, R_G + 2 * KB)
        lr_t = [at(f"lr_t{d}", TOK, R_G + (3 + 3 * d) * KB, rows=16) for d in range(2)]
        gate_y = at("gate_y", TOK, R_G + 9 * KB)
        gate_e = at("gate_e", TOK, R_G + 12 * KB)
        o_hi = at("o_hi", KC * LAT, R_H, f32r)
        o_lo = at("o_lo", KC * LAT, R_H + 16 * KB, f32r)
        decay_f = at("decay_f", UW + 640, R_H + 32 * KB)
        decay_b = at("decay_b", UW + 640, R_H + 38 * KB)
        s_ring = at("s_ring", 2 * LAT, R_H + 44 * KB)
        u_sb = at("u_sb", UW, R_TMP + 8 * KB)
        o_sb = at("o_sb", LAT, R_TMP + 6 * KB)
        o_sq = at("o_sq", LAT, R_ADA + 20 * KB)
        s_gla = at("s_gla", 2 * TILES * LAT, R_G)
        ctx_k = at("ctx_k", 4 * CTX, R_G + 24 * KB)
        q_lv = at("q_lv", 2 * LAT, R_ADA)
        k_lv = at("k_lv", 2 * LAT, R_ADA + 4 * KB)
        d_lv = at("d_lv", 4 * LAT, R_H + 32 * KB)
        cum = at("cum", 4 * LAT, R_H + 40 * KB)
        suf = at("suf", LAT, R_TMP + 8 * KB)
        masks = at("masks", 7 * P, R_XC, i32)
        diag2_sb = at("diag2_sb", P, R_XC + 3584)
        lsig = at("lsig", 16, R_VEC + 1568)
        nlsig = at("nlsig", 4, R_VEC + 1632)
        zero_t = at("zero_t", 1, R_VEC + 2336)
        ls_tmp = at("ls_tmp", 4 * 16, R_TMP)

        aq = at("aq", 4 * LAT, R_G)
        ak = at("ak", 4 * LAT, R_G + 8 * KB)
        av = at("av", LT * 512, R_G + 16 * KB)
        ru = at("ru", 4 * LAT, R_G + 24 * KB)
        ry = at("ry", 4 * LAT, R_G + 32 * KB)
        ck = at("ck", HEADS * CTX, R_G + 40 * KB)
        cv = at("cv", 2 * 512, R_G + 44 * KB)
        pos_i = at("pos_i", LAT, R_TMP, i32)
        angle = at("angle", LAT, R_TMP + 2 * KB)
        turns = at("turns", LAT, R_TMP + 4 * KB)
        cs2 = at("cs2", 2 * LAT, R_TMP + 8 * KB)
        rope_pp = at("rope_pp", 2, R_VEC + 1376)
        bias_sb = at("bias_sb", LT * LAT, R_ADA)
        prob = at("prob", P_BUFS * LAT, R_ADA + 8 * KB)
        stat = at("stat", 3 * P_BUFS, R_ADA + 16 * KB)
        prob_t = at("prob_t", 2 * LT * LAT, R_H + 32 * KB)
        uc = at("uc", 4 * LAT, R_ADA)
        rg_sb = at("rg_sb", 16 * P, R_ADA + 8 * KB)
        rg_c = at("rg_c", 8, R_ADA + 16 * KB + 64)
        rg_r = at("rg_r", 2 * LAT, R_H + 32 * KB)
        rg_i = at("rg_i", 2 * LAT, R_H + 36 * KB)
        rg_a = at("rg_a", 2 * LAT, R_H + 40 * KB)
        rg_t = at("rg_t", 2 * LAT, R_H + 44 * KB)
        rg_h = at("rg_h", 2 * LAT, R_TMP)

        ps = stack.enter_context(nc.psum_tensor("ps", [P, 8 * 512], f32))

        def bank(b, n=512, c0=0):
            return ps[:, b * 512 + c0:b * 512 + c0 + n]

        sems = {}

        def sem(name):
            sems[name] = stack.enter_context(nc.semaphore(name))
            return sems[name]

        raw_ready = [sem(f"raw_ready{s}") for s in range(RING)]
        hi_done, lo_done, panel_done = sem("hi_done"), sem("lo_done"), sem("panel_done")
        ada_ready = [sem(f"ada_ready{s}") for s in range(ADA_RING)]
        ada_used = sem("ada_used")
        x_loaded, vec_loaded, cond_loaded, consts = sem("x_loaded"), sem("vec_loaded"), sem("cond_loaded"), sem("consts")
        cond_ready = sem("cond_ready")
        act_chain, dve_chain = sem("act_chain"), sem("dve_chain")
        mods_ready = sem("mods_ready")
        silu_done, up_evac, ghi_done, g_ready, down_evac = (sem(n) for n in ("silu_done", "up_evac", "ghi_done", "g_ready", "down_evac"))
        sq_ready, sq_used, root_ready, xn_ready, hhi_done, h_ready = (
            sem(n) for n in ("sq_ready", "sq_used", "root_ready", "xn_ready", "hhi_done", "h_ready"))
        out_done = sem("out_done")
        small_loaded = sem("small_loaded")
        mem_loaded, pos_loaded, win2_evac, cs_arg, cs_ready, rope2_done, bias_loaded, rg_loaded, cq_evac = (
            sem(n) for n in ("mem_loaded", "pos_loaded", "win2_evac", "cs_arg", "cs_ready", "rope2_done", "bias_loaded", "rg_loaded", "cq_evac"))
        a_scores, a_max, a_exp, a_prob, a_trans, a_copied, a_values = (
            sem(n) for n in ("a_scores", "a_max", "a_exp", "a_prob", "a_trans", "a_copied", "a_values"))
        rg_conv, rg_gates, rg_sig, rg_la, rg_exp, rg_v, rg_root, rg_hid = (
            sem(n) for n in ("rg_conv", "rg_gates", "rg_sig", "rg_la", "rg_exp", "rg_v", "rg_root", "rg_hid"))
        ls_exp, lsig_ready = sem("ls_exp"), sem("lsig_ready")
        lr_lo_done = sem("lr_lo_done")
        lr_split, lr_pe, lr_act, gate_act, gate_dve = (sem(n) for n in ("lr_split", "lr_pe", "lr_act", "gate_act", "gate_dve"))
        win_evac, rope_loaded, rope_done, u_loaded, masks_loaded = (
            sem(n) for n in ("win_evac", "rope_loaded", "rope_done", "u_loaded", "masks_loaded"))
        arg_ready, exp_ready, s_ready, s_evac, pv_done = (sem(n) for n in ("arg_ready", "exp_ready", "s_ready", "s_evac", "pv_done"))
        o_ready, o_copied, mean_ready, o_centred, osq_ready, var_ready, oroot_ready, o_scaled, ohi_done, mix_ready = (
            sem(n) for n in ("o_ready", "o_copied", "mean_ready", "o_centred", "osq_ready", "var_ready", "oroot_ready",
                             "o_scaled", "ohi_done", "mix_ready"))
        d_ready, x_ready, qk_ready, unit_ready, unit_dve, unit_act, ctx_arg, ctx_exp = (
            sem(n) for n in ("d_ready", "x_ready", "qk_ready", "unit_ready", "unit_dve", "unit_act", "ctx_arg", "ctx_exp"))
        block = stack.enter_context(nc.Block())

        def done(p):
            return p + RING + 1

        def token_cols(T):
            return [(0, 0, HALF), (1, HALF, HALF)] if T == TOK else [(0, 0, T)]

        def vcol(name, j=0, n=1):
            return vec[:, VEC_AT[name] + j:VEC_AT[name] + j + n]

        def mod(row, part):
            c = (row * NMOD + part) * KC
            return mods[:, c:c + KC]

        class Norm:
            def __init__(self, n, T, A, B, last=False):
                self.n, self.T, self.A, self.B, self.last = n, T, A, B, last

            def segs(self):
                s = [(x_lat, LAT, 0, 0)]
                return s + [(x_ctx, CTX, LAT, 1)] if self.T == TOK else s

        def sc(j):
            return lambda kc: scales[:, j * KC + kc:j * KC + kc + 1]

        def md(row, part):
            return lambda kc: mods[:, (row * NMOD + part) * KC + kc:(row * NMOD + part) * KC + kc + 1]

        def vc(name):
            return lambda kc: vcol(name, kc)

        norms = [Norm(0, TOK, (sc(0), sc(1)), (md(0, 0), md(1, 0))),
                 Norm(1, TOK, (sc(2), sc(3)), (md(0, 3), md(1, 3))),
                 Norm(2, LAT, (sc(4),), (md(0, 6),)),
                 Norm(3, LAT, (vc("final_norm_w"),), None, True),
                 Norm(4, TOK, (vc("norm_mix_g_2"), vc("norm_mem_g_2")), None),
                 Norm(5, LAT, (vc("norm_cross_g_2"),), None),
                 Norm(6, LAT, (vc("norm_mlp_g_2"),), None),
                 Norm(7, LAT, (vc("norm_final_g_2"),), None, True)]
        H_BEFORE = [sum(8 for m in norms[:n] if not m.last) for n in range(9)]

        def hidden_groups():
            f, rows = 0, []
            for layer, (p0, T, sizes, gated) in enumerate(((P_FFN1, TOK, FF_GROUPS, True), (P_FFN2, LAT, FF_GROUPS, True),
                                                        (P_MLP, LAT, (8,) * 4, False))):
                p, o = p0, (0, 4 * KC, 9 * KC)[layer]
                for n, g in enumerate(sizes):
                    n_up = (2 if gated else 1) * g
                    rows.append(dict(layer=layer, n=n, T=T, g=g, gated=gated, p_up=p, p_down=p + n_up, f0=f, o0=o, last=n == len(sizes) - 1))
                    p += n_up + KC
                    f += g
                    o += KC
            return rows

        GROUPS = hidden_groups()

        def ada_before(n):
            return ADA_FIRST + sum(ADA_PER_PAIR[m] * FF_GROUPS[m] // 2 for m in range(n))

        def ada_rows(n, k):
            k0 = ada_before(n)
            return sum(r * (ada_before(m + 1) - ada_before(m)) for m, r in enumerate(ADA_ROWS[:n])) + 2 * ADA_FIRST + ADA_ROWS[n] * (k - k0)

        def x_final(n):
            return {1: 3, 2: 4, 3: 7, 5: 8, 6: 9, 7: 13}[n] * KC

        def attention_items(heads, q, k, v, dk, keys, n0, p0, s0):
            return dict(heads=heads, q=q, k=k, v=v, dk=dk, keys=keys, n0=n0, h0=p0, s0=s0, n=heads * LT)

        SELF = attention_items(8, aq, ak, av, DH, LAT, 0, 0, 8)
        CROSS = attention_items(HEADS, aq, ck, cv, P, CTX, 8 * LT, 8, 16)

        V_BANKS = {"v": (0, 1, 2, 3), "cv": (0, 1), "rv": (0, 1, 2, 3, 4, 5), "gv": (0, 1, 2, 3, 4, 5)}

        def unit_bank(u, a):
            return 4 * (u % 2) + 2 * a

        @block.sync
        def _(sp):
            sp.dma_start(vec[:, :], vecs).then_inc(vec_loaded, 16)
            sp.dma_start(cond_b[:, :], cond.partition_broadcast(P)).then_inc(cond_loaded, 16)
            sp.dma_start(lsig[:, 0:8], decays.partition_broadcast(P)).then_inc(small_loaded, 16)
            sp.dma_start(lr_raw[:, :], lr_w).then_inc(small_loaded, 16)
            sp.dma_start(gate_sb[:, :], gate_w).then_inc(small_loaded, 16)
            sp.dma_start(ident[:, :], ident_h).then_inc(small_loaded, 16)
            sp.dma_start(rope_pp[:, :], rope_pp_h).then_inc(small_loaded, 16)
            for k in range(ADA_RING):
                sp.dma_start(ada_w[:, k * D:(k + 1) * D], ada_t[k]).then_inc(ada_ready[k], 16)
            sp.dma_start(x_lat[:, :], x_t).then_inc(x_loaded, 16)
            sp.dma_start(x_ctx[:, :], ctx_t).then_inc(x_loaded, 16)
            for k in range(ADA_RING, ADA_FIRST):
                sp.wait_ge(ada_used, 2 * (k - ADA_RING + 1))
                s = k % ADA_RING
                sp.dma_start(ada_w[:, s * D:(s + 1) * D], ada_t[k]).then_inc(ada_ready[s], 16)
                if k < ADA_RING + RING:
                    s = k - ADA_RING
                    sp.dma_start(raw[:, s * PANEL:(s + 1) * PANEL], panels[s]).then_inc(raw_ready[s], 16)
            with sp.Fori(1, N_PANELS // RING) as i:
                for s in range(RING):
                    sp.wait_ge(lo_done, (i - 1) * RING + s + 1)
                    sp.dma_start(raw[:, s * PANEL:(s + 1) * PANEL],
                                 panels[ds(i * RING + s, 1)].rearrange("a p n -> (a p) n")).then_inc(raw_ready[s], 16)
            for kc in range(KC):
                sp.wait_ge(xn_ready, 7 * KC + kc + 1)
                sp.dma_start(out[0, :, kc * LAT:(kc + 1) * LAT], x_lat[:, kc * LAT:(kc + 1) * LAT]).then_inc(out_done, 16)
            sp.wait_ge(out_done, 16 * KC)

        @block.gpsimd
        def _(pool):
            pool.memset(ones_k[:, :], 1.0 / D).then_inc(consts, 1)
            pool.memset(eps_t[:, :], EPS).then_inc(consts, 1)
            pool.memset(zero_t[:, :], 0.0).then_inc(consts, 1)
            with pool.Fori(0, N_PANELS // RING) as i:
                for s in range(RING):
                    pool.wait_ge(hi_done, i * RING + s + 1)
                    sl = slice(s * PANEL, (s + 1) * PANEL)
                    pool.tensor_tensor(wlo[:, sl], raw[:, sl], whi[:, sl].bitcast(f32), ALU.subtract).then_inc(lo_done, 1)

        @block.scalar
        def _(act):
            chain = [0]

            def link(ins):
                chain[0] += 1
                ins.then_inc(act_chain, 1)
                act.wait_ge(act_chain, chain[0])

            def round_panel(s, turn, p_done=None):
                act.wait_ge(raw_ready[s], turn * 16)
                if p_done is not None:
                    act.wait_ge(panel_done, done(p_done))
                sl = slice(s * PANEL, (s + 1) * PANEL)
                act.activation(whi[:, sl], raw[:, sl], ACT.Copy).then_inc(hi_done, 1)

            def round_ahead(p0, i, c):
                q = p0 + c + 2
                round_panel(q % RING, i + (q // RING + 1), i * RING + (q - RING))

            def norm(m):
                cols = token_cols(m.T)
                for kc in range(KC):
                    if m.n == 0:
                        if kc == 0:
                            act.wait_ge(x_loaded, 32)
                    elif m.n == 4:
                        if kc == 0:
                            act.wait_ge(mem_loaded, 16)
                        act.wait_ge(xn_ready, 3 * KC + kc + 1)
                    else:
                        act.wait_ge(down_evac, x_final(m.n) + kc + 1)
                    if kc >= 2:
                        act.wait_ge(sq_used, m.n * KC + kc - 1)
                    b = (kc % 2) * TOK
                    for xs, n, c0, _ in m.segs():
                        ins = act.activation(act_a[:, b + c0:b + c0 + n], xs[:, kc * n:(kc + 1) * n], ACT.Square)
                    ins.then_inc(sq_ready, 1)
                act.wait_ge(sq_used, m.n * KC + KC)
                for b, c0, n in cols:
                    ins = act.activation(rstd[:, c0:c0 + n], bank(b, n), ACT.Sqrt, bias=eps_t[:, :])
                ins.then_inc(root_ready, 1)
                if m.last:
                    return
                for kc in range(KC):
                    act.wait_ge(xn_ready, m.n * KC + kc + 1)
                    b = (kc % 2) * TOK
                    for j, (_, n, c0, _) in enumerate(m.segs()):
                        o = h_hi[:, kc * TOK + c0:kc * TOK + c0 + n]
                        if m.B is None:
                            ins = act.activation(o, prod[:, b + c0:b + c0 + n], ACT.Copy)
                        else:
                            ins = act.activation(o, prod[:, b + c0:b + c0 + n], ACT.Identity, bias=m.B[j](kc))
                    ins.then_inc(hhi_done, 1)

            def hidden_up(G):
                T, cols = G["T"], token_cols(G["T"])
                per_f = 2 if G["gated"] else 1
                f_per = RING // per_f
                with act.Fori(0, G["g"] // f_per) as i:
                    for u in range(f_per):
                        if G["layer"] == 0 and (u == 0 or ADA_PER_PAIR[G["n"]] == 6):
                            for j in range(ADA_RING):
                                k = ada_before(G["n"]) + i * ADA_PER_PAIR[G["n"]] + u * ADA_RING + j
                                act.wait_ge(ada_used, ada_rows(G["n"], k - ADA_RING + 1))
                                act.dma_start(ada_w[:, j * D:(j + 1) * D],
                                              ada_t[ds(k, 1)].rearrange("a p n -> (a p) n")).then_inc(ada_ready[j], 16)
                        for c in range(per_f):
                            round_ahead(G["p_up"], i, u * per_f + c)
                        f = G["f0"] + i * f_per + u
                        b = (u % 2) * TOK
                        act.wait_ge(panel_done, done(G["p_up"] + i * RING + u * per_f))
                        act.wait_ge(up_evac, f + 1)
                        b0 = 2 * u * per_f
                        src = ps[:, b0 * 512:b0 * 512 + 1024].rearrange("p (b n) -> p b n", b=2)[:, 0:len(cols), 0:cols[0][2]]
                        dst = act_a[:, b:b + T].rearrange("p (b n) -> p b n", b=len(cols))
                        act.activation(dst, src, ACT.Silu if G["gated"] else ACT.Relu).then_inc(silu_done, 1)
                        act.wait_ge(up_evac, f + 3)
                        fo = (i * f_per + u) * TOK
                        act.activation(g_hi[:, ds(fo, T)], prod[:, b:b + T], ACT.Copy).then_inc(ghi_done, 1)

            def hidden_down(G):
                if G["p_down"] + KC == N_PANELS:
                    for q in range(G["p_down"] + 2, N_PANELS):
                        round_panel(q % RING, q // RING + 1, q - RING)
                    return
                with act.Fori(0, KC // RING) as i:
                    for c in range(RING):
                        round_ahead(G["p_down"], i, c)

            def head_norm(j, gated_only):
                act.wait_ge(o_ready, j + 1)
                if j:
                    act.wait_ge(mix_ready, j)
                act.activation(o_sb[:, :], bank(2), ACT.Copy).then_inc(o_copied, 1)
                if gated_only:
                    act.wait_ge(o_copied, j + 1)
                else:
                    act.wait_ge(o_centred, j + 1)
                act.activation(o_sq[:, :], o_sb[:, :], ACT.Square).then_inc(osq_ready, 1)
                act.wait_ge(var_ready, j + 1)
                act.activation(o_sq[:, :], bank(4), ACT.Sqrt, bias=eps_t[:, :], scale=float(D // P)).then_inc(oroot_ready, 1)
                act.wait_ge(o_scaled, j + 1)
                act.activation(o_hi[:, j * LAT:(j + 1) * LAT], o_sb[:, :], ACT.Copy).then_inc(ohi_done, 1)

            def residual(p0):
                with act.Fori(0, KC // RING) as i:
                    for c in range(RING):
                        round_ahead(p0, i, c)

            def gates_of_gla():
                act.wait_ge(small_loaded, 80)
                act.activation(lr_hi[:, :], lr_raw[:, :], ACT.Copy).then_inc(lr_split, 1)
                act.wait_ge(lr_pe, 1)
                act.activation(lr_sb[:, :], bank(6, TILES * 32), ACT.Copy).then_inc(lr_act, 1)
                act.wait_ge(lr_pe, 2)
                for d in range(2):
                    for b in range(2):
                        ins = act.activation(lr_t[d][:, b * HALF:(b + 1) * HALF], ps[0:16, (4 + 2 * d + b) * 512:(4 + 2 * d + b) * 512 + HALF], ACT.Copy)
                ins.then_inc(lr_act, 1)
                for n in range(4):
                    d, hp = divmod(n, 2)
                    act.wait_ge(lr_pe, 3 + n)
                    if n:
                        act.wait_ge(gate_dve, n)
                    src = ps[:, 2 * n * 512:2 * n * 512 + 1024].rearrange("p (b n) -> p b n", b=2)[:, :, 0:HALF]
                    y = gate_y[:, :].rearrange("p (b n) -> p b n", b=2)
                    link(act.activation(y, src, ACT.Identity, bias=vcol(("gla_gate_b_f", "gla_gate_b_b")[d], hp)))
                    link(act.activation(gate_e[:, :], gate_y[:, :], ACT.Abs))
                    link(act.activation(gate_e[:, :], gate_e[:, :], ACT.Exp, scale=-1.0))
                    act.activation(gate_e[:, :], gate_e[:, :], ACT.Ln, bias=1.0).then_inc(gate_act, 1)

            def input_projection():
                act.wait_ge(h_ready, H_BEFORE[2])
                act.dma_start(rope_cs[:, :], rope_grid).then_inc(rope_loaded, 16)
                gates_of_gla()
                act.wait_ge(gate_dve, 4)
                for n, (kind, first, n_p) in enumerate(WIN):
                    for c in range(n_p):
                        q = P_WIN + first + c + 2
                        round_panel(q % RING, q // RING + 1, q - RING)
                    act.wait_ge(panel_done, done(P_WIN + first + n_p - 1))
                    j = first % 4
                    b = 2 * (first % RING)
                    two = ps[:, b * 512:b * 512 + 1024].rearrange("p (b n) -> p b n", b=2)[:, :, 0:HALF]
                    if kind == "rq":
                        act.activation(rq[:, j * LAT:(j + 1) * LAT], bank(b), ACT.Copy, scale=P ** -0.5).then_inc(win_evac, 1)
                    elif kind in ("rk", "gk"):
                        j = first - 18 if kind == "gk" else j
                        dst = (rk if kind == "rk" else gk)[:, j * TOK:(j + 1) * TOK].rearrange("p (b n) -> p b n", b=2)
                        act.activation(dst, two, ACT.Copy).then_inc(win_evac, 1)
                    elif kind == "gq":
                        act.activation(gq[:, j * LAT:(j + 1) * LAT], bank(b), ACT.Copy, scale=64 ** -0.5).then_inc(win_evac, 1)
                    elif kind in ("rg", "gg"):
                        dst = (rg if kind == "rg" else gg)[:, j * LAT:(j + 1) * LAT]
                        act.activation(dst, bank(b), ACT.Silu).then_inc(win_evac, 1)
                    else:
                        lat, ctx = (rv, rv_c) if kind == "rv" else (gv, gv_c)
                        for t in range(TILES):
                            dst = lat[:, t * 512:(t + 1) * 512] if t < LT else ctx[:, (t - LT) * 512:(t - LT + 1) * 512]
                            ins = act.activation(dst, bank(V_BANKS[kind][t]), ACT.Copy)
                        ins.then_inc(win_evac, 1)

            def retention():
                act.wait_ge(rope_done, 8)
                act.dma_start(u_sb[:, :], u_tab).then_inc(u_loaded, 16)
                for j in range(HEADS):
                    act.wait_ge(arg_ready, j + 1)
                    act.activation(decay_f[:, :], decay_f[:, :], ACT.Exp)
                    act.activation(decay_b[:, :], decay_b[:, :], ACT.Exp).then_inc(exp_ready, 1)
                    head_norm(j, False)

            def gla():
                act.wait_ge(pv_done, 6 * HEADS)
                act.dma_start(masks[:, :], level_masks).then_inc(masks_loaded, 16)
                act.dma_start(diag2_sb[:, :], diag2).then_inc(masks_loaded, 16)
                for hp in range(2):
                    act.wait_ge(ctx_arg, hp + 1)
                    act.activation(ctx_k[:, 0:2 * CTX], ctx_k[:, 0:2 * CTX], ACT.Exp).then_inc(ctx_exp, 1)
                    for u in range(1, UNITS):
                        n = hp * (UNITS - 1) + u
                        act.wait_ge(d_ready, n)
                        b = (u % 2) * 2 * LAT
                        if u < UNITS - 1:
                            h = 2 ** (u - 1)
                            v = d_lv[:, b:b + 2 * LAT].rearrange("p (n t h) -> p n t h", t=2, h=h)
                            act.activation(v[:, :, 0, :], v[:, :, 0, :], ACT.Exp, scale=-1.0)
                            act.activation(v[:, :, 1, :], v[:, :, 1, :], ACT.Exp).then_inc(x_ready, 1)
                        else:
                            act.activation(d_lv[:, b:b + 2 * LAT], d_lv[:, b:b + 2 * LAT], ACT.Exp).then_inc(x_ready, 1)
                        if u - 1 >= len(LEVELS) + 1:
                            unit_copy(hp, u - 1)
                    unit_copy(hp, UNITS - 1)
                    for a in range(2):
                        head_norm(HEADS + 2 * hp + a, True)

            def unit_copy(hp, u):
                act.wait_ge(unit_ready, hp * UNITS + u + 1)
                for a in range(2):
                    S = s_gla[:, a * TILES * LAT:(a + 1) * TILES * LAT].rearrange("p (j i) -> p j i", j=TILES)
                    b = unit_bank(u, a)
                    if u == UNITS - 3:
                        for t in range(LT):
                            o = (t ^ 1) * P
                            ins = act.activation(S[:, t, o:o + P], bank(b, P, t * P), ACT.Copy)
                    elif u == UNITS - 2:
                        for half in range(2):
                            ins = act.activation(S[:, 2 * half:2 * half + 2, (1 - half) * 256:(2 - half) * 256],
                                                 bank(b + half).rearrange("p (j i) -> p j i", j=2), ACT.Copy)
                    else:
                        ins = act.activation(S[:, LT:TILES, :], ps[:, b * 512:(b + 2) * 512].rearrange("p (j i) -> p j i", j=2), ACT.Copy)
                ins.then_inc(unit_act, 1)

            def input_projection2():
                act.wait_ge(h_ready, H_BEFORE[5])
                act.dma_start(pos_i[:, :], positions.partition_broadcast(P)).then_inc(pos_loaded, 16)
                act.dma_start(bias_sb[:, :], window_bias).then_inc(bias_loaded, 16)
                for n, (kind, first, n_p) in enumerate(WIN2):
                    for c in range(n_p):
                        q = P_WIN2 + first + c + 2
                        round_panel(q % RING, q // RING + 1, q - RING)
                    act.wait_ge(panel_done, done(P_WIN2 + first + n_p - 1))
                    j = first % 4
                    b = 2 * (first % RING)
                    if kind in ("q", "k", "u"):
                        dst = {"q": aq, "k": ak, "u": ru}[kind]
                        act.activation(dst[:, j * LAT:(j + 1) * LAT], bank(b), ACT.Copy).then_inc(win2_evac, 1)
                    elif kind == "y":
                        act.activation(ry[:, j * LAT:(j + 1) * LAT], bank(b), ACT.Gelu_apprx_tanh).then_inc(win2_evac, 1)
                    elif kind == "ck":
                        act.activation(ck[:, j * CTX:(j + 1) * CTX], bank(b, CTX), ACT.Copy).then_inc(win2_evac, 1)
                    else:
                        dst = av if kind == "v" else cv
                        for t, vb in enumerate(V_BANKS[kind]):
                            ins = act.activation(dst[:, t * 512:(t + 1) * 512], bank(vb), ACT.Copy)
                        ins.then_inc(win2_evac, 1)
                    if n == 1:
                        act.wait_ge(cs_arg, 1)
                        act.activation(cs2[:, :], cs2[:, :], ACT.Sin).then_inc(cs_ready, 1)

            def attention(A):
                for n in range(A["n"] + 2):
                    if n < A["n"]:
                        N = A["n0"] + n
                        sl = N % P_BUFS
                        act.wait_ge(a_max, N + 1)
                        row = prob[:, sl * LAT:sl * LAT + A["keys"]]
                        act.activation(row, row, ACT.Exp, bias=stat[:, sl:sl + 1], scale=float(A["dk"]) ** -0.5,
                                       accum_out=stat[:, P_BUFS + sl:P_BUFS + sl + 1]).then_inc(a_exp, 1)
                    if n >= 2:
                        m = n - 2
                        hd, it = divmod(m, LT)
                        act.wait_ge(a_trans, A["n0"] + m + 1)
                        H = A["h0"] + hd
                        if it == 0 and H >= 2:
                            act.wait_ge(a_values, H - 1)
                        kt = A["keys"] // P
                        dst = prob_t[:, (hd % 2) * LT * LAT:(hd % 2 + 1) * LT * LAT].rearrange("p (j i) -> p j i", j=LT)
                        act.activation(dst[:, 0:kt, it * P:(it + 1) * P], bank(2 + m % 2, kt * P).rearrange("p (j i) -> p j i", j=kt),
                                       ACT.Copy).then_inc(a_copied, 1)
                        if it == LT - 1 and (A["dk"] == P or hd % 2):
                            act.wait_ge(a_values, H + 1)
                            c = hd if A["dk"] == P else hd // 2
                            act.activation(o_hi[:, c * LAT:(c + 1) * LAT], bank(4 + c % 2), ACT.Copy).then_inc(ohi_done, 1)

            def rg_lru():
                act.wait_ge(a_prob, SELF["n"])
                act.wait_ge(a_trans, SELF["n"])
                act.dma_start(rg_sb[:, :], rg_w).then_inc(rg_loaded, 16)
                for c in range(4):
                    act.wait_ge(rg_gates, c + 1)
                    if c:
                        act.wait_ge(rg_hid, c)
                    b0 = 4 * (c % 2)
                    for z in range(2):
                        sl = slice(z * LAT, (z + 1) * LAT)
                        act.activation(rg_r[:, sl], bank(b0 + 2 * z), ACT.Sigmoid, bias=vcol("rg_a_b_2", 4 * z + c))
                        ins = act.activation(rg_i[:, sl], bank(b0 + 2 * z + 1), ACT.Sigmoid, bias=vcol("rg_x_b_2", 4 * z + c))
                    ins.then_inc(rg_sig, 1)
                    act.wait_ge(rg_la, c + 1)
                    act.activation(rg_t[:, :], rg_r[:, :], ACT.Tanh)
                    act.activation(rg_a[:, :], rg_r[:, :], ACT.Exp, scale=-1.0).then_inc(rg_exp, 1)
                    act.wait_ge(rg_v, c + 1)
                    act.activation(rg_t[:, :], rg_t[:, :], ACT.Sqrt).then_inc(rg_root, 1)
                    act.wait_ge(rg_hid, c + 1)
                    act.activation(o_hi[:, (4 + c) * LAT:(5 + c) * LAT], rg_h[:, 0:LAT], ACT.Copy).then_inc(ohi_done, 1)

            def cross_queries():
                for j in range(4):
                    q = P_CQ + j + 2
                    round_panel(q % RING, q // RING + 1, q - RING)
                    act.wait_ge(panel_done, done(P_CQ + j))
                    act.activation(aq[:, j * LAT:(j + 1) * LAT], bank(2 * j), ACT.Copy).then_inc(cq_evac, 1)

            act.wait_ge(vec_loaded, 16)
            act.wait_ge(small_loaded, 80)
            link(act.activation(lsig[:, 8:16], vcol("rg_lambda_2", 0, 8), ACT.Copy))
            link(act.activation(ls_tmp[:, 0:16], lsig[:, :], ACT.Abs))
            act.activation(ls_tmp[:, 0:16], ls_tmp[:, 0:16], ACT.Exp, scale=-1.0).then_inc(ls_exp, 1)
            act.wait_ge(cond_loaded, 16)
            act.activation(cond_b[:, :], cond_b[:, :], ACT.Silu).then_inc(cond_ready, 1)
            round_panel(0, 1)
            round_panel(1, 1)
            act.wait_ge(consts, 3)
            norm(norms[0])
            for G in GROUPS[0:3]:
                hidden_up(G)
                hidden_down(G)
            norm(norms[1])
            input_projection()
            retention()
            gla()
            residual(P_WOUT)
            norm(norms[2])
            for G in GROUPS[3:6]:
                hidden_up(G)
                hidden_down(G)
            act.wait_ge(o_ready, 8)
            act.dma_start(x_ctx[:, :], mem_t).then_inc(mem_loaded, 16)
            norm(norms[3])
            norm(norms[4])
            input_projection2()
            attention(SELF)
            rg_lru()
            residual(P_WOUT2)
            norm(norms[5])
            cross_queries()
            attention(CROSS)
            for q in range(P_CO + 2, P_CO + 6):
                round_panel(q % RING, q // RING + 1, q - RING)
            norm(norms[6])
            for G in GROUPS[6:10]:
                hidden_up(G)
                hidden_down(G)
            norm(norms[7])

        @block.vector
        def _(dve):
            chain = [0]

            def link(ins):
                chain[0] += 1
                ins.then_inc(dve_chain, 1)
                dve.wait_ge(dve_chain, chain[0])

            def ada_chunk(k, s, turn, rows, rows_done, first=False):
                dve.wait_ge(ada_ready[s], turn * 16)
                for r in range(rows):
                    if r or not first:
                        dve.wait_ge(ada_used, rows_done + r)
                    ins = dve.scalar_tensor_tensor(out=ada_prod[:, :], in0=ada_w[:, s * D:(s + 1) * D], scalar=1.0,
                                                   in1=cond_b[:, r * D:(r + 1) * D], op0=ALU.mult, op1=ALU.mult,
                                                   accum_out=mods[:, ds(r * NMOD * KC + k, 1)])
                    ins.then_inc(ada_used, 1)

            def add_bias(parts, rows):
                n = (parts[1] - parts[0]) * KC
                for r in range(rows):
                    c = (r * NMOD + parts[0]) * KC
                    link(dve.tensor_tensor(mods[:, c:c + n], mods[:, c:c + n], vcol("ada_b", parts[0] * KC, n), ALU.add))

            def norm_scale(j, row, part, w):
                link(dve.scalar_tensor_tensor(scales[:, j * KC:(j + 1) * KC], mod(row, part), 1.0, vcol(w, 0, KC), ALU.add, ALU.mult))

            def norm(m):
                cols = token_cols(m.T)
                dve.wait_ge(root_ready, m.n + 1)
                link(dve.reciprocal(rstd[:, 0:m.T], rstd[:, 0:m.T]))
                for kc in range(KC + 1):
                    if kc < KC:
                        b = (kc % 2) * TOK
                        for j, (xs, n, c0, _) in enumerate(m.segs()):
                            o = xs[:, kc * n:(kc + 1) * n] if m.last else prod[:, b + c0:b + c0 + n]
                            ins = dve.scalar_tensor_tensor(o, xs[:, kc * n:(kc + 1) * n], m.A[j](kc), rstd[:, c0:c0 + n],
                                                           ALU.mult, ALU.mult)
                        ins.then_inc(xn_ready, 1)
                    if kc > 0 and not m.last:
                        k = kc - 1
                        b = (k % 2) * TOK
                        dve.wait_ge(hhi_done, H_BEFORE[m.n] + k + 1)
                        dve.wait_ge(xn_ready, m.n * KC + k + 1)
                        for j, (_, n, c0, _) in enumerate(m.segs()):
                            sl = slice(k * TOK + c0, k * TOK + c0 + n)
                            src = prod[:, b + c0:b + c0 + n]
                            if m.B is None:
                                ins = dve.tensor_tensor(h_lo[:, sl], src, h_hi[:, sl].bitcast(f32), ALU.subtract)
                            else:
                                ins = dve.scalar_tensor_tensor(h_lo[:, sl], src, m.B[j](k), h_hi[:, sl].bitcast(f32),
                                                               ALU.add, ALU.subtract)
                        ins.then_inc(h_ready, 1)
                        dve.wait_ge(h_ready, H_BEFORE[m.n] + k + 1)

            def hidden_up(G):
                T, cols = G["T"], token_cols(G["T"])
                per_f = 2 if G["gated"] else 1
                f_per = RING // per_f
                with dve.Fori(0, G["g"] // f_per) as i:
                    for u in range(f_per):
                        if G["layer"] == 0 and (u == 0 or ADA_PER_PAIR[G["n"]] == 6):
                            npp = ADA_PER_PAIR[G["n"]]
                            for j in range(ADA_RING):
                                k = ada_before(G["n"]) + i * npp + u * ADA_RING + j
                                ada_chunk(k, j, (ada_before(G["n"]) // ADA_RING) + i * (npp // ADA_RING) + u + 1, ADA_ROWS[G["n"]],
                                          ada_rows(G["n"], k))
                        f = G["f0"] + i * f_per + u
                        b = (u % 2) * TOK
                        dve.wait_ge(panel_done, done(G["p_up"] + i * RING + (u + 1) * per_f - 1))
                        dve.wait_ge(silu_done, f + 1)
                        dve.wait_ge(g_ready, f + 1)
                        if G["gated"]:
                            src = ps[:, (4 * u + 2) * 512:(4 * u + 2) * 512 + 1024].rearrange("p (b n) -> p b n", b=2)[:, 0:len(cols), 0:cols[0][2]]
                            a = act_a[:, b:b + T].rearrange("p (b n) -> p b n", b=len(cols))
                            o = prod[:, b:b + T].rearrange("p (b n) -> p b n", b=len(cols))
                            dve.tensor_tensor(o, a, src, ALU.mult).then_inc(up_evac, 1)
                        else:
                            dve.tensor_tensor(prod[:, b:b + T], act_a[:, b:b + T], act_a[:, b:b + T], ALU.mult).then_inc(up_evac, 1)
                        dve.wait_ge(ghi_done, f + 1)
                        fo = (i * f_per + u) * TOK
                        dve.tensor_tensor(g_lo[:, ds(fo, T)], prod[:, b:b + T], g_hi[:, ds(fo, T)].bitcast(f32), ALU.subtract)\
                            .then_inc(g_ready, 1)

            def hidden_down(G):
                T = G["T"]
                with dve.Fori(0, KC // RING) as i:
                    for c in range(RING):
                        dve.wait_ge(panel_done, done(G["p_down"] + i * RING + c))
                        dve.wait_ge(down_evac, G["o0"] + i * RING + c + 1)
                        o = i * RING + c
                        def add(dst, src, gate):
                            return dve.scalar_tensor_tensor(dst, src, gate, dst, ALU.mult, ALU.add)
                        if T == TOK:
                            add(x_lat[:, ds(o * LAT, HALF)], bank(2 * c, HALF), gates[:, ds(o, 1)])
                            add(x_lat[:, ds(o * LAT + HALF, LAT - HALF)], bank(2 * c + 1, LAT - HALF), gates[:, ds(o, 1)])
                            ins = add(x_ctx[:, ds(o * CTX, CTX)], bank(2 * c + 1, CTX, LAT - HALF), gates[:, ds(o + KC, 1)])
                        elif G["gated"]:
                            ins = add(x_lat[:, ds(o * LAT, LAT)], bank(2 * c), gates[:, ds(o + 3 * KC, 1)])
                        else:
                            dst = x_lat[:, ds(o * LAT, LAT)]
                            ins = dve.tensor_tensor(dst, bank(2 * c), dst, ALU.add)
                        ins.then_inc(down_evac, 1)

            def log_sigmoids():
                z, w, w2, p = (ls_tmp[:, j * 16:(j + 1) * 16] for j in range(4))
                dve.wait_ge(ls_exp, 1)
                link(dve.tensor_scalar(w, z, 2.0, None, ALU.add))
                link(dve.reciprocal(w, w))
                link(dve.tensor_tensor(w, w, z, ALU.mult))
                link(dve.tensor_tensor(w2, w, w, ALU.mult))
                link(dve.tensor_scalar(p, w2, 1.0 / 17, 1.0 / 15, ALU.mult, ALU.add))
                for k in (13, 11, 9, 7, 5, 3, 1):
                    link(dve.tensor_tensor(p, p, w2, ALU.mult))
                    link(dve.tensor_scalar(p, p, 1.0 / k, None, ALU.add))
                link(dve.scalar_tensor_tensor(p, p, 2.0, w, ALU.mult, ALU.mult))
                link(dve.scalar_tensor_tensor(lsig[:, :], lsig[:, :], 0.0, p, ALU.min, ALU.subtract))
                dve.tensor_scalar(nlsig[:, :], lsig[:, 4:8], -1.0, None, ALU.mult).then_inc(lsig_ready, 1)

            def residual(p0, o0, gate):
                with dve.Fori(0, KC // RING) as i:
                    for c in range(RING):
                        dve.wait_ge(panel_done, done(p0 + i * RING + c))
                        dve.wait_ge(down_evac, o0 + i * RING + c + 1)
                        o = i * RING + c
                        dst = x_lat[:, ds(o * LAT, LAT)]
                        if gate is None:
                            ins = dve.tensor_tensor(dst, bank(2 * c), dst, ALU.add)
                        else:
                            ins = dve.scalar_tensor_tensor(dst, bank(2 * c), gates[:, ds(o + gate * KC, 1)], dst, ALU.mult, ALU.add)
                        ins.then_inc(down_evac, 1)

            def head_norm(j, gated_only, w, gate):
                if not gated_only:
                    dve.wait_ge(mean_ready, j + 1)
                    dve.scalar_tensor_tensor(o_sb[:, :], bank(3), -float(D // P), o_sb[:, :], ALU.mult, ALU.add).then_inc(o_centred, 1)
                    dve.wait_ge(o_centred, j + 1)
                dve.wait_ge(oroot_ready, j + 1)
                link(dve.reciprocal(o_sq[:, :], o_sq[:, :]))
                link(dve.scalar_tensor_tensor(o_sb[:, :], o_sb[:, :], w, o_sq[:, :], ALU.mult, ALU.mult))
                dve.tensor_tensor(o_sb[:, :], o_sb[:, :], gate, ALU.mult).then_inc(o_scaled, 1)
                dve.wait_ge(ohi_done, j + 1)
                dve.wait_ge(o_scaled, j + 1)
                sl = slice(j * LAT, (j + 1) * LAT)
                dve.tensor_tensor(o_lo[:, sl], o_sb[:, :], o_hi[:, sl].bitcast(f32), ALU.subtract).then_inc(mix_ready, 1)

            def input_projection():
                dve.wait_ge(lr_split, 1)
                dve.tensor_tensor(lr_lo[:, :], lr_raw[:, :], lr_hi[:, :].bitcast(f32), ALU.subtract).then_inc(lr_lo_done, 1)
                for n in range(4):
                    d, hp = divmod(n, 2)
                    dve.wait_ge(gate_act, n + 1)
                    dst = (gf, gb)[d][:, hp * TOK:(hp + 1) * TOK]
                    link(dve.scalar_tensor_tensor(dst, gate_y[:, :], 0.0, gate_e[:, :], ALU.min, ALU.subtract))
                    dve.tensor_scalar(dst, dst, 1.0 / 16, None, ALU.mult).then_inc(gate_dve, 1)
                dve.wait_ge(rope_loaded, 16)
                for j in range(8):
                    dve.wait_ge(win_evac, j + 1)
                    dst = rq[:, j * LAT:(j + 1) * LAT] if j < 4 else rk[:, (j - 4) * TOK:(j - 4) * TOK + LAT]
                    if j:
                        dve.wait_ge(rope_done, j)
                    link(dve.stream_shuffle(rope_tmp[:, :], dst, SWAP16))
                    link(dve.tensor_tensor(rope_tmp[:, :], rope_tmp[:, :], rope_cs[:, LAT:2 * LAT], ALU.mult))
                    link(dve.tensor_tensor(dst, dst, rope_cs[:, 0:LAT], ALU.mult))
                    dve.tensor_tensor(dst, dst, rope_tmp[:, :], ALU.add).then_inc(rope_done, 1)

            def retention():
                dve.wait_ge(win_evac, len(WIN))
                dve.wait_ge(u_loaded, 16)
                dve.wait_ge(lsig_ready, 1)
                for j in range(HEADS):
                    lg_f, nlg_b = lsig[:, j:j + 1], nlsig[:, j:j + 1]
                    if j:
                        dve.wait_ge(s_evac, 6 * j)
                    dve.tensor_scalar(decay_f[:, 0:UW], u_sb[:, :], 0.0, lg_f, ALU.max, ALU.mult)
                    dve.tensor_scalar(decay_b[:, 0:UW], u_sb[:, :], 0.0, nlg_b, ALU.min, ALU.mult)
                    dve.tensor_scalar(decay_f[:, UW:], u_sb[:, 256:], float(CTX), lg_f, ALU.add, ALU.mult)
                    dve.tensor_scalar(decay_b[:, UW:], u_sb[:, 256:], -float(LAT), nlg_b, ALU.add, ALU.mult).then_inc(arg_ready, 1)
                    dve.wait_ge(exp_ready, j + 1)
                    dve.scalar_tensor_tensor(decay_f[:, 0:UW], u_sb[:, :], 0.0, decay_f[:, 0:UW], ALU.is_ge, ALU.mult)
                    link(dve.scalar_tensor_tensor(decay_b[:, 0:UW], u_sb[:, :], 0.0, decay_b[:, 0:UW], ALU.is_le, ALU.mult))
                    link(dve.tensor_tensor(decay_f[:, :], decay_f[:, :], decay_b[:, :], ALU.add))
                    for t in range(TILES):
                        n = j * TILES + t
                        dve.wait_ge(s_ready, n + 1)
                        if n >= 2:
                            dve.wait_ge(pv_done, n - 1)
                        c = 384 - P * t if t < LT else UW + P - P * (t - LT)
                        dve.tensor_tensor(s_ring[:, (n % 2) * LAT:(n % 2 + 1) * LAT], bank(n % 2), decay_f[:, c:c + LAT], ALU.mult)\
                            .then_inc(s_evac, 1)
                    head_norm(j, False, vcol("ret_norm_w", j), rg[:, j * LAT:(j + 1) * LAT])

            def gla():
                dve.wait_ge(masks_loaded, 32)
                zero = zero_t[:, :].to_broadcast([P, LAT])
                C = [cum[:, j * LAT:(j + 1) * LAT] for j in range(4)]
                for hp in range(2):
                    q, k = gq[:, hp * LAT:(hp + 1) * LAT], gk[:, hp * TOK:(hp + 1) * TOK]
                    f, b = gf[:, hp * TOK:(hp + 1) * TOK], gb[:, hp * TOK:(hp + 1) * TOK]
                    if hp:
                        dve.wait_ge(o_ready, HEADS + 2)
                    def scan(dst, src, n):
                        return dve.tensor_tensor_scan(dst, src, zero_t[:, :].to_broadcast([P, n]), 0.0, ALU.add, ALU.add)
                    for t in range(LT):
                        sl = slice(t * P, (t + 1) * P)
                        scan(C[0][:, sl], f[:, sl], P)
                        scan(C[1][:, sl], b[:, sl], P)
                    scan(C[2], f[:, 0:LAT], LAT)
                    scan(C[3], b[:, 0:LAT], LAT)
                    scan(suf[:, ::-1], b[:, 0:LAT][:, ::-1], LAT)
                    kf, kb = ctx_k[:, 0:CTX], ctx_k[:, CTX:2 * CTX]
                    scan(kf[:, ::-1], f[:, LAT:TOK][:, ::-1], CTX)
                    link(scan(kb, b[:, LAT:TOK], CTX))
                    dve.tensor_tensor(C[1], C[1], b[:, 0:LAT], ALU.subtract)
                    dve.tensor_tensor(C[3], C[3], b[:, 0:LAT], ALU.subtract)
                    dve.tensor_tensor(kf, kf, f[:, LAT:TOK], ALU.subtract)
                    dve.tensor_tensor(kb, kb, b[:, LAT:TOK], ALU.subtract).then_inc(ctx_arg, 1)
                    dve.wait_ge(ctx_arg, hp + 1)
                    dve.wait_ge(ctx_exp, hp + 1)
                    link(dve.tensor_tensor(kf, kf, k[:, LAT:TOK], ALU.mult))
                    link(dve.tensor_tensor(kb, kb, k[:, LAT:TOK], ALU.mult))

                    def distances(u):
                        n = hp * (UNITS - 1) + u
                        if n > 2:
                            dve.wait_ge(qk_ready, hp * UNITS + u - 1 if u > 2 else hp * UNITS)
                        o = (u % 2) * 2 * LAT
                        if u == UNITS - 1:
                            dve.tensor_copy(d_lv[:, o:o + LAT], C[2])
                            dve.tensor_copy(d_lv[:, o + LAT:o + 2 * LAT], suf[:, :]).then_inc(d_ready, 1)
                            return
                        h = 2 ** (u - 1)
                        for d in range(2):
                            src = C[d if h < P else 2 + d].rearrange("p (n h) -> p n h", h=2 * h)
                            ref = src[:, :, h - 1 + d:h + d].broadcast_to([P, LAT // (2 * h), 2 * h])
                            dst = d_lv[:, o + d * LAT:o + (d + 1) * LAT].rearrange("p (n h) -> p n h", h=2 * h)
                            ins = dve.tensor_tensor(dst, src, ref, ALU.subtract)
                        ins.then_inc(d_ready, 1)

                    def scaled(u):
                        m = hp * UNITS + u
                        dve.wait_ge(x_ready, hp * (UNITS - 1) + u)
                        if m >= 2:
                            dve.wait_ge(unit_ready, m - 1)
                        o = (u % 2) * LAT
                        ql, kl = q_lv[:, o:o + LAT], k_lv[:, o:o + LAT]
                        xf, xb = d_lv[:, 2 * o:2 * o + LAT], d_lv[:, 2 * o + LAT:2 * o + 2 * LAT]
                        if u == UNITS - 1:
                            dve.tensor_tensor(ql, q, xf, ALU.mult)
                            dve.tensor_tensor(kl, q, xb, ALU.mult).then_inc(qk_ready, 1)
                            return
                        h = 2 ** (u - 1)
                        v = lambda a: a.rearrange("p (n t h) -> p n t h", t=2, h=h)
                        kk = k[:, 0:LAT]
                        dve.tensor_tensor(v(ql)[:, :, 0], v(q)[:, :, 0], v(xb)[:, :, 0], ALU.mult)
                        dve.tensor_tensor(v(ql)[:, :, 1], v(q)[:, :, 1], v(xf)[:, :, 1], ALU.mult)
                        dve.tensor_tensor(v(kl)[:, :, 0], v(kk)[:, :, 0], v(xf)[:, :, 0], ALU.mult)
                        dve.tensor_tensor(v(kl)[:, :, 1], v(kk)[:, :, 1], v(xb)[:, :, 1], ALU.mult).then_inc(qk_ready, 1)

                    def masked(u):
                        dve.wait_ge(unit_ready, hp * UNITS + u + 1)
                        if u:
                            dve.wait_ge(unit_dve, hp * (len(LEVELS) + 1) + u)
                        for a in range(2):
                            c0 = a * TILES * LAT
                            diagonal = [s_gla[:, c0 + t * (LAT + P):c0 + t * (LAT + P) + P] for t in range(LT)]
                            for t in range(LT):
                                src = bank(unit_bank(u, a), P, t * P)
                                if u == 0:
                                    ins = dve.tensor_tensor(diagonal[t], src, diag2_sb[:, :], ALU.mult)
                                else:
                                    ins = dve.copy_predicated(diagonal[t], masks[:, (u - 1) * P:u * P], src)
                        ins.then_inc(unit_dve, 1)

                    dve.tensor_copy(q_lv[:, 0:LAT], q)
                    dve.tensor_copy(k_lv[:, 0:LAT], k[:, 0:LAT]).then_inc(qk_ready, 1)
                    distances(1)
                    for u in range(1, UNITS):
                        if u + 1 < UNITS:
                            distances(u + 1)
                        scaled(u)
                        if u - 1 <= len(LEVELS):
                            masked(u - 1)
                    for a in range(2):
                        j = 2 * hp + a
                        head_norm(HEADS + j, True, vcol("gla_norm_w", j), gg[:, j * LAT:(j + 1) * LAT])

            def input_projection2():
                dve.wait_ge(pos_loaded, 16)
                link(dve.tensor_copy(angle[:, :], pos_i[:, :]))
                link(dve.tensor_scalar(angle[:, :], angle[:, :], rope_pp[:, 0:1], None, ALU.mult))
                link(dve.tensor_scalar(turns[:, :], angle[:, :], 1.0 / (2 * math.pi), ROUND, ALU.mult, ALU.add))
                link(dve.tensor_scalar(turns[:, :], turns[:, :], ROUND, None, ALU.subtract))
                for part in TWO_PI:
                    link(dve.scalar_tensor_tensor(angle[:, :], turns[:, :], -part, angle[:, :], ALU.mult, ALU.add))
                cos_a, sin_a = cs2[:, 0:LAT], cs2[:, LAT:2 * LAT]
                link(dve.tensor_scalar(cos_a, angle[:, :], math.pi / 2, None, ALU.add))
                link(dve.tensor_scalar(turns[:, :], cos_a, math.pi, -2 * math.pi, ALU.is_gt, ALU.mult))
                link(dve.tensor_tensor(cos_a, cos_a, turns[:, :], ALU.add))
                link(dve.tensor_copy(sin_a, angle[:, :]))
                dve.tensor_scalar(cs2[:, :], cs2[:, :], PI_IN, -PI_IN, ALU.min, ALU.max).then_inc(cs_arg, 1)
                dve.wait_ge(cs_ready, 1)
                link(dve.tensor_scalar(sin_a, sin_a, rope_pp[:, 1:2], None, ALU.mult))
                for j in range(8):
                    dve.wait_ge(win2_evac, j + 1)
                    dst = (aq if j < 4 else ak)[:, (j % 4) * LAT:(j % 4 + 1) * LAT]
                    if j:
                        dve.wait_ge(rope2_done, j)
                    link(dve.stream_shuffle(rope_tmp[:, :], dst, SWAP16))
                    link(dve.tensor_tensor(rope_tmp[:, :], rope_tmp[:, :], sin_a, ALU.mult))
                    link(dve.tensor_tensor(dst, dst, cos_a, ALU.mult))
                    dve.tensor_tensor(dst, dst, rope_tmp[:, :], ALU.add).then_inc(rope2_done, 1)

            def attention(A):
                if A is SELF:
                    dve.wait_ge(bias_loaded, 16)
                scale = float(A["dk"]) ** -0.5
                for n in range(A["n"] + 1):
                    N = A["n0"] + n
                    if n < A["n"]:
                        sl = N % P_BUFS
                        row = prob[:, sl * LAT:sl * LAT + A["keys"]]
                        top = stat[:, sl:sl + 1]
                        dve.wait_ge(a_scores, N + 1)
                        if N >= P_BUFS:
                            dve.wait_ge(a_trans, N - P_BUFS + 1)
                        if A is SELF:
                            it = n % LT
                            link(dve.tensor_tensor_reduce(out=row, in0=bank(n % 2), in1=bias_sb[:, it * LAT:(it + 1) * LAT], scale=1.0,
                                                          scalar=-3e38, op0=ALU.add, op1=ALU.max, accum_out=top))
                        else:
                            dve.tensor_copy(row, bank(n % 2, A["keys"]))
                            link(dve.tensor_reduce(out=top, in_=bank(n % 2, A["keys"]), axis=AX.X, op=ALU.max))
                        dve.tensor_scalar(top, top, -scale, None, ALU.mult).then_inc(a_max, 1)
                    if n >= 1:
                        sl = (N - 1) % P_BUFS
                        row = prob[:, sl * LAT:sl * LAT + A["keys"]]
                        total, inv = stat[:, P_BUFS + sl:P_BUFS + sl + 1], stat[:, 2 * P_BUFS + sl:2 * P_BUFS + sl + 1]
                        dve.wait_ge(a_exp, N)
                        link(dve.reciprocal(inv, total))
                        dve.tensor_scalar(row, row, inv, None, ALU.mult).then_inc(a_prob, 1)
                        hd, it = divmod(n - 1, LT)
                        if it == LT - 1 and (A["dk"] == P or hd % 2):
                            c = hd if A["dk"] == P else hd // 2
                            pending.append(c)
                    while pending and (n == A["n"] or n % LT == 3):
                        c = pending.pop(0)
                        dve.wait_ge(ohi_done, A["s0"] + c + 1)
                        sl = slice(c * LAT, (c + 1) * LAT)
                        dve.tensor_tensor(o_lo[:, sl], bank(4 + c % 2), o_hi[:, sl].bitcast(f32), ALU.subtract).then_inc(mix_ready, 1)

            pending = []

            def rg_lru():
                link(dve.tensor_scalar(rg_c[:, :], lsig[:, 8:16], -8.0, None, ALU.mult))
                dve.wait_ge(a_trans, SELF["n"])
                for c in range(4):
                    u_in, o = ru[:, c * LAT:(c + 1) * LAT], uc[:, c * LAT:(c + 1) * LAT]
                    w = [vcol("conv_w_2", 4 * k + c) for k in range(4)]
                    link(dve.tensor_scalar(o, u_in, w[2], vcol("conv_b_2", c), ALU.mult, ALU.add))
                    link(dve.scalar_tensor_tensor(o[:, 1:], u_in[:, :LAT - 1], w[1], o[:, 1:], ALU.mult, ALU.add))
                    link(dve.scalar_tensor_tensor(o[:, 2:], u_in[:, :LAT - 2], w[0], o[:, 2:], ALU.mult, ALU.add))
                    dve.scalar_tensor_tensor(o[:, :LAT - 1], u_in[:, 1:], w[3], o[:, :LAT - 1], ALU.mult, ALU.add).then_inc(rg_conv, 1)
                dve.wait_ge(rg_conv, 4)
                for c in range(4):
                    dve.wait_ge(rg_sig, c + 1)
                    for z in range(2):
                        sl = slice(z * LAT, (z + 1) * LAT)
                        dve.tensor_tensor(rg_i[:, sl], rg_i[:, sl], uc[:, c * LAT:(c + 1) * LAT], ALU.mult)
                        ins = dve.tensor_scalar(rg_r[:, sl], rg_r[:, sl], rg_c[:, 4 * z + c:4 * z + c + 1], None, ALU.mult)
                    ins.then_inc(rg_la, 1)
                    dve.wait_ge(rg_la, c + 1)
                    dve.wait_ge(rg_exp, c + 1)
                    link(dve.tensor_tensor(rg_r[:, :], rg_a[:, :], rg_a[:, :], ALU.mult))
                    dve.scalar_tensor_tensor(rg_t[:, :], rg_r[:, :], 1.0, rg_t[:, :], ALU.add, ALU.mult).then_inc(rg_v, 1)
                    dve.wait_ge(rg_root, c + 1)
                    link(dve.tensor_tensor(rg_i[:, :], rg_i[:, :], rg_t[:, :], ALU.mult))
                    if c:
                        dve.wait_ge(ohi_done, 8 + 4 + c)
                    dve.tensor_tensor_scan(rg_h[:, 0:LAT], rg_a[:, 0:LAT], rg_i[:, 0:LAT], 0.0, ALU.mult, ALU.add)
                    link(dve.tensor_tensor_scan(rg_h[:, LAT:][:, ::-1], rg_a[:, LAT:][:, ::-1], rg_i[:, LAT:][:, ::-1], 0.0, ALU.mult, ALU.add))
                    link(dve.tensor_tensor(rg_h[:, 0:LAT], rg_h[:, 0:LAT], rg_h[:, LAT:], ALU.add))
                    dve.tensor_tensor(rg_h[:, 0:LAT], rg_h[:, 0:LAT], ry[:, c * LAT:(c + 1) * LAT], ALU.mult).then_inc(rg_hid, 1)
                    dve.wait_ge(rg_hid, c + 1)
                    dve.wait_ge(ohi_done, 8 + 4 + c + 1)
                    sl = slice((4 + c) * LAT, (5 + c) * LAT)
                    dve.tensor_tensor(o_lo[:, sl], rg_h[:, 0:LAT], o_hi[:, sl].bitcast(f32), ALU.subtract).then_inc(mix_ready, 1)
                    dve.wait_ge(mix_ready, 8 + 4 + c + 1)

            dve.sem_inc(up_evac, 2)
            dve.sem_inc(g_ready, 2)
            dve.sem_inc(down_evac, KC)
            log_sigmoids()
            dve.wait_ge(cond_ready, 1)
            for k in range(ADA_FIRST):
                ada_chunk(k, k % ADA_RING, k // ADA_RING + 1, 2, 2 * k, first=k == 0)
            dve.wait_ge(vec_loaded, 16)
            dve.wait_ge(small_loaded, 80)
            dve.wait_ge(ada_used, 2 * ADA_FIRST)
            add_bias((0, 2), 2)
            norm_scale(0, 0, 1, "norm1_w")
            norm_scale(1, 1, 1, "norm1_w")
            norm(norms[0])
            for G in GROUPS[0:3]:
                hidden_up(G)
                if G["n"] == 0:
                    dve.wait_ge(ada_used, ada_rows(0, ada_before(1)))
                    add_bias((2, 3), 2)
                    for r in range(2):
                        link(dve.tensor_scalar(gates[:, r * KC:(r + 1) * KC], mod(r, 2), 0.5, None, ALU.mult))
                hidden_down(G)
            dve.wait_ge(ada_used, ada_rows(2, ada_before(3)))
            add_bias((3, 9), 1)
            link(dve.tensor_tensor(mods[:, 72 + 24:72 + 40], mods[:, 72 + 24:72 + 40], vcol("ada_b", 24, 16), ALU.add))
            norm_scale(2, 0, 4, "norm2_w")
            norm_scale(3, 1, 4, "norm2_w")
            norm_scale(4, 0, 7, "norm3_w")
            link(dve.tensor_copy(gates[:, 2 * KC:3 * KC], mod(0, 5)))
            link(dve.tensor_scalar(gates[:, 3 * KC:4 * KC], mod(0, 8), 0.5, None, ALU.mult))
            norm(norms[1])
            input_projection()
            retention()
            gla()
            residual(P_WOUT, 3 * KC, 2)
            norm(norms[2])
            for G in GROUPS[3:6]:
                hidden_up(G)
                hidden_down(G)
            norm(norms[3])
            norm(norms[4])
            input_projection2()
            attention(SELF)
            rg_lru()
            residual(P_WOUT2, 7 * KC, None)
            norm(norms[5])
            attention(CROSS)
            for o in range(KC):
                dve.wait_ge(panel_done, done(P_CO + o // 2))
                dve.wait_ge(down_evac, 8 * KC + o + 1)
                dst = x_lat[:, o * LAT:(o + 1) * LAT]
                dve.tensor_tensor(dst, bank(o), dst, ALU.add).then_inc(down_evac, 1)
            norm(norms[6])
            for G in GROUPS[6:10]:
                hidden_up(G)
                hidden_down(G)
            norm(norms[7])

        @block.tensor
        def _(pe):
            def product3(out, lhs, rhs, first, last):
                pe.matmul(out, lhs[0], rhs[0], start=first, stop=False)
                pe.matmul(out, lhs[0], rhs[1], start=False, stop=False)
                return pe.matmul(out, lhs[1], rhs[0], start=False, stop=last)

            def panel_product(s, banks, act_hi, act_lo, cols, n_k=KC, ready=None, off=0, stride=TOK):
                for kc in range(n_k):
                    if ready is not None:
                        pe.wait_ge(*ready(kc))
                    w = slice(s * PANEL + (off + kc) * P, s * PANEL + (off + kc + 1) * P)
                    order = ((whi, act_hi), (whi, act_lo), (wlo, act_hi))
                    for j, (wt, a) in enumerate(order):
                        for b, c0, n in cols:
                            ins = pe.matmul(bank(banks + b, n), wt[:, w], a[:, kc * stride + c0:kc * stride + c0 + n],
                                            start=kc == 0 and j == 0, stop=kc == n_k - 1 and j == 2)
                return ins

            def norm(m):
                cols = token_cols(m.T)
                if m.n == 0:
                    pe.wait_ge(consts, 3)
                elif m.n == 4:
                    pe.wait_ge(root_ready, 4)
                else:
                    pe.wait_ge(down_evac, x_final(m.n) + RING + 1)
                for kc in range(KC):
                    pe.wait_ge(sq_ready, m.n * KC + kc + 1)
                    for b, c0, n in cols:
                        o = (kc % 2) * TOK + c0
                        ins = pe.matmul(bank(b, n), ones_k[:, :], act_a[:, o:o + n], start=kc == 0, stop=kc == KC - 1)
                    ins.then_inc(sq_used, 1)

            def hidden_up(G, h_base):
                cols = token_cols(G["T"])
                per_f = 2 if G["gated"] else 1
                f_per = RING // per_f
                if G["n"] == 0:
                    pe.wait_ge(root_ready, (0, 2, 6)[G["layer"]] + 1)
                with pe.Fori(0, G["g"] // f_per) as i:
                    for u in range(f_per):
                        pe.wait_ge(up_evac, G["f0"] + i * f_per + u + 1)
                        pe.wait_ge(down_evac, G["o0"] + KC - (2 if u == 0 else 0))
                        for c in range(per_f):
                            s = u * per_f + c
                            pe.wait_ge(lo_done, G["p_up"] + i * RING + s + 1)
                            ready = (lambda kc: (h_ready, h_base + kc + 1)) if G["n"] == 0 and s == 0 else None
                            panel_product(s, 2 * s, h_hi, h_lo, cols, ready=ready).then_inc(panel_done, 1)

            def hidden_down(G):
                cols = token_cols(G["T"])
                f_end = G["f0"] + G["g"] + 2
                with pe.Fori(0, KC // RING) as i:
                    for c in range(RING):
                        pe.wait_ge(up_evac, f_end - (1 if c < 2 else 0))
                        pe.wait_ge(down_evac, G["o0"] + i * RING + c + RING + 1)
                        pe.wait_ge(lo_done, G["p_down"] + i * RING + c + 1)
                        ready = (lambda kc: (g_ready, G["f0"] + 2 + kc + 1)) if c == 0 else None
                        panel_product(c, 2 * c, g_hi, g_lo, cols, n_k=G["g"], ready=ready).then_inc(panel_done, 1)

            def panel_rows(s, k, banks, tiles=TILES, t0=0, first=False, last=False):
                for c in range(2):
                    for t in range(tiles):
                        a = slice((k + c) * TOK + (t0 + t) * P, (k + c) * TOK + (t0 + t + 1) * P)
                        w = slice(s * PANEL + c * 512, s * PANEL + (c + 1) * 512)
                        ins = product3(bank(banks[t]), (h_hi[:, a], h_lo[:, a]), (whi[:, w], wlo[:, w]),
                                       first and c == 0, last and c == 1)
                return ins

            def input_projection():
                pe.wait_ge(lr_lo_done, 1)
                pe.wait_ge(h_ready, H_BEFORE[2])
                pe.wait_ge(down_evac, 4 * KC)
                for t in range(TILES):
                    for kc in range(KC):
                        a, w = slice(kc * TOK + t * P, kc * TOK + (t + 1) * P), slice(kc * 32, (kc + 1) * 32)
                        ins = product3(bank(6, 32, t * 32), (h_hi[:, a], h_lo[:, a]), (lr_hi[:, w], lr_lo[:, w]), kc == 0, kc == KC - 1)
                ins.then_inc(lr_pe, 1)
                pe.wait_ge(lr_act, 1)
                for d in range(2):
                    for t in range(TILES):
                        b = 4 + 2 * d + t // 3
                        ins = pe.transpose(ps[0:16, b * 512 + (t % 3) * P:b * 512 + (t % 3 + 1) * P], lr_sb[:, t * 32 + d * 16:t * 32 + d * 16 + 16],
                                           ident[:, :])
                ins.then_inc(lr_pe, 1)
                pe.wait_ge(lr_act, 2)
                for n in range(4):
                    d, hp = divmod(n, 2)
                    for b in range(2):
                        ins = pe.matmul(bank(2 * n + b, HALF), gate_sb[:, d * 256 + hp * P:d * 256 + (hp + 1) * P],
                                        lr_t[d][:, b * HALF:(b + 1) * HALF], start=True, stop=True)
                    ins.then_inc(lr_pe, 1)
                pe.wait_ge(gate_act, 4)
                last_use = {}
                for n, (kind, first, n_p) in enumerate(WIN):
                    T = TOK if kind in ("rk", "gk") else LAT
                    b0 = 2 * (first % RING)
                    banks = V_BANKS[kind] if kind in V_BANKS else [b0 + b for b, _, _ in token_cols(T)]
                    free = max(last_use.get(b, 0) for b in banks)
                    if free:
                        pe.wait_ge(win_evac, free)
                    for b in banks:
                        last_use[b] = n + 1
                    for c in range(n_p):
                        p = P_WIN + first + c
                        pe.wait_ge(lo_done, p + 1)
                        if kind in V_BANKS:
                            panel_rows(p % RING, 2 * c, banks, first=c == 0, last=c == n_p - 1).then_inc(panel_done, 1)
                        else:
                            panel_product(p % RING, b0, h_hi, h_lo, token_cols(T)).then_inc(panel_done, 1)

            def head_stats(j, gated_only):
                if not gated_only:
                    pe.wait_ge(o_copied, j + 1)
                    pe.matmul(bank(3), ones_k[:, :], o_sb[:, :], start=True, stop=True).then_inc(mean_ready, 1)
                pe.wait_ge(osq_ready, j + 1)
                pe.matmul(bank(4), ones_k[:, :], o_sq[:, :], start=True, stop=True).then_inc(var_ready, 1)

            def retention():
                pe.wait_ge(win_evac, len(WIN))
                pe.wait_ge(rope_done, 8)
                for j in range(HEADS):
                    def scores(t):
                        n = j * TILES + t
                        if n >= 2:
                            pe.wait_ge(s_evac, n - 1)
                        pe.matmul(bank(n % 2), rk[:, j * TOK + t * P:j * TOK + (t + 1) * P], rq[:, j * LAT:(j + 1) * LAT],
                                  start=True, stop=True).then_inc(s_ready, 1)

                    def values(t):
                        n = j * TILES + t
                        pe.wait_ge(s_evac, n + 1)
                        v = rv[:, t * 512 + j * P:t * 512 + (j + 1) * P] if t < LT else rv_c[:, (t - LT) * 512 + j * P:(t - LT) * 512 + (j + 1) * P]
                        return pe.matmul(bank(2), v, s_ring[:, (n % 2) * LAT:(n % 2 + 1) * LAT], start=t == 0, stop=t == TILES - 1)
                    scores(0)
                    for t in range(1, TILES):
                        scores(t)
                        values(t - 1).then_inc(pv_done, 1)
                    values(TILES - 1).then_inc(pv_done, 1)
                    pe.wait_ge(pv_done, TILES * (j + 1))
                    pe.sem_inc(o_ready, 1)
                    head_stats(j, False)

            def gla():
                pe.wait_ge(oroot_ready, HEADS)
                for hp in range(2):
                    if hp:
                        pe.wait_ge(oroot_ready, HEADS + 2)
                    for u in range(UNITS):
                        m = hp * UNITS + u
                        pe.wait_ge(qk_ready, m + 1)
                        if u >= 2:
                            v = u - 2
                            if v <= len(LEVELS):
                                pe.wait_ge(unit_dve, hp * (len(LEVELS) + 1) + v + 1)
                            else:
                                pe.wait_ge(unit_act, hp * 3 + v - len(LEVELS))
                        o = (u % 2) * LAT
                        for a in range(2):
                            r = slice(64 * a, 64 * a + 64)
                            b = unit_bank(u, a)
                            ql, kl = q_lv[r, o:o + LAT], k_lv[r, o:o + LAT]
                            if u <= len(LEVELS) + 1:
                                for t in range(LT):
                                    i = t if u <= len(LEVELS) else t ^ 1
                                    ins = pe.matmul(bank(b, P, t * P), kl[:, t * P:(t + 1) * P], ql[:, i * P:(i + 1) * P], start=True, stop=True)
                            elif u == UNITS - 2:
                                for t in range(LT):
                                    i = (1 - t // 2) * 256
                                    ins = pe.matmul(bank(b + t // 2, 256, (t % 2) * 256), kl[:, t * P:(t + 1) * P], ql[:, i:i + 256], start=True, stop=True)
                            else:
                                for t in range(2):
                                    for d, qq in enumerate((ql, kl)):
                                        ins = pe.matmul(bank(b + t), ctx_k[r, d * CTX + t * P:d * CTX + (t + 1) * P], qq, start=d == 0, stop=d == 1)
                        ins.then_inc(unit_ready, 1)
                    pe.wait_ge(unit_dve, (hp + 1) * (len(LEVELS) + 1))
                    pe.wait_ge(unit_act, 3 * (hp + 1))
                    for a in range(2):
                        j = 2 * hp + a
                        if a:
                            pe.wait_ge(o_copied, HEADS + j)
                        for t in range(TILES):
                            v = gv[:, t * 512 + j * P:t * 512 + (j + 1) * P] if t < LT else gv_c[:, (t - LT) * 512 + j * P:(t - LT) * 512 + (j + 1) * P]
                            S = s_gla[:, (a * TILES + t) * LAT:(a * TILES + t + 1) * LAT]
                            ins = pe.matmul(bank(2), v, S, start=t == 0, stop=t == TILES - 1)
                        ins.then_inc(o_ready, 1)
                        head_stats(HEADS + j, True)

            def input_projection2():
                last_use = {}
                pe.wait_ge(root_ready, 5)
                for n, (kind, first, n_p) in enumerate(WIN2):
                    cols = [(0, LAT, CTX)] if kind == "ck" else token_cols(LAT)
                    b0 = 2 * (first % RING)
                    banks = V_BANKS[kind] if kind in V_BANKS else [b0]
                    free = max(last_use.get(b, 0) for b in banks)
                    if free:
                        pe.wait_ge(win2_evac, free)
                    for b in banks:
                        last_use[b] = n + 1
                    for c in range(n_p):
                        p = P_WIN2 + first + c
                        pe.wait_ge(lo_done, p + 1)
                        if kind in V_BANKS:
                            t0, tiles = (0, LT) if kind == "v" else (LT, 2)
                            panel_rows(p % RING, 2 * c, banks, tiles=tiles, t0=t0, first=c == 0, last=c == n_p - 1)\
                                .then_inc(panel_done, 1)
                        else:
                            ready = (lambda kc: (h_ready, H_BEFORE[4] + kc + 1)) if n == 0 else None
                            panel_product(p % RING, b0, h_hi, h_lo, cols, ready=ready).then_inc(panel_done, 1)

            def attention(A):
                if A is SELF:
                    pe.wait_ge(win2_evac, len(WIN2))
                    pe.wait_ge(rope2_done, 8)
                dk, kt = A["dk"], A["keys"] // P
                for n in range(A["n"] + 2):
                    if n < A["n"]:
                        hd, it = divmod(n, LT)
                        j, r = (hd // 2, slice(64 * (hd % 2), 64 * (hd % 2) + 64)) if dk == DH else (hd, slice(0, P))
                        if n >= 2:
                            pe.wait_ge(a_max, A["n0"] + n - 1)
                        pe.matmul(bank(n % 2, A["keys"]), A["q"][r, j * LAT + it * P:j * LAT + (it + 1) * P],
                                  A["k"][r, j * A["keys"]:(j + 1) * A["keys"]], start=True, stop=True).then_inc(a_scores, 1)
                    if n >= 2:
                        m = n - 2
                        hd, it = divmod(m, LT)
                        N = A["n0"] + m
                        pe.wait_ge(a_prob, N + 1)
                        if m >= 2:
                            pe.wait_ge(a_copied, N - 1)
                        for t in range(kt):
                            ins = pe.transpose(bank(2 + m % 2, P, t * P), prob[:, (N % P_BUFS) * LAT + t * P:(N % P_BUFS) * LAT + (t + 1) * P], ident[:, :])
                        ins.then_inc(a_trans, 1)
                        if it == LT - 1:
                            c = hd if dk == P else hd // 2
                            if c >= 2 or A is not SELF:
                                pe.wait_ge(mix_ready, max(A["s0"] + c - 1, A["s0"]))
                            pe.wait_ge(a_copied, N + 1)
                            r = slice(0, P) if dk == P else slice(64 * (hd % 2), 64 * (hd % 2) + 64)
                            o = ps[r, (4 + c % 2) * 512:(5 + c % 2) * 512]
                            for t in range(kt):
                                v = A["v"][:, t * 512 + hd * dk:t * 512 + (hd + 1) * dk]
                                ins = pe.matmul(o, v, prob_t[:, ((hd % 2) * LT + t) * LAT:((hd % 2) * LT + t + 1) * LAT], start=t == 0, stop=t == kt - 1)
                            ins.then_inc(a_values, 1)

            def rg_lru():
                pe.wait_ge(rg_loaded, 16)
                pe.wait_ge(mix_ready, 8 + 4)
                for c in range(4):
                    pe.wait_ge(rg_conv, c + 1)
                    if c >= 2:
                        pe.wait_ge(rg_sig, c - 1)
                    for z in range(2):
                        for g in range(2):
                            w = ((2 * z + g) * 4 + c) * P
                            ins = pe.matmul(bank(4 * (c % 2) + 2 * z + g), rg_sb[:, w:w + P], uc[:, c * LAT:(c + 1) * LAT], start=True, stop=True)
                    ins.then_inc(rg_gates, 1)

            def cross_queries():
                pe.wait_ge(root_ready, 6)
                for j in range(4):
                    pe.wait_ge(lo_done, P_CQ + j + 1)
                    ready = (lambda kc: (h_ready, H_BEFORE[5] + kc + 1)) if j == 0 else None
                    panel_product(j, 2 * j, h_hi, h_lo, token_cols(LAT), ready=ready).then_inc(panel_done, 1)
                pe.wait_ge(cq_evac, 4)

            def cross_output():
                for c in range(RING):
                    pe.wait_ge(lo_done, P_CO + c + 1)
                    for e in range(2):
                        ready = (lambda kc: (mix_ready, 16 + kc + 1)) if c == 0 and e == 0 else None
                        ins = panel_product(c, 2 * c + e, o_hi, o_lo, token_cols(LAT), n_k=4, ready=ready, off=4 * e, stride=LAT)
                    ins.then_inc(panel_done, 1)

            def residual(p0, o0, a_hi, a_lo, n_k, stride, ready):
                with pe.Fori(0, KC // RING) as i:
                    for c in range(RING):
                        pe.wait_ge(down_evac, o0 + i * RING + c + RING + 1)
                        pe.wait_ge(lo_done, p0 + i * RING + c + 1)
                        panel_product(c, 2 * c, a_hi, a_lo, token_cols(LAT), n_k=n_k, ready=ready if c == 0 else None,
                                      stride=stride).then_inc(panel_done, 1)

            pe.sem_inc(panel_done, RING)
            norm(norms[0])
            for G in GROUPS[0:3]:
                hidden_up(G, 0)
                hidden_down(G)
            norm(norms[1])
            input_projection()
            retention()
            gla()
            residual(P_WOUT, 3 * KC, o_hi, o_lo, KC, LAT, lambda kc: (mix_ready, kc + 1))
            norm(norms[2])
            for G in GROUPS[3:6]:
                hidden_up(G, H_BEFORE[2])
                hidden_down(G)
            norm(norms[3])
            norm(norms[4])
            input_projection2()
            attention(SELF)
            rg_lru()
            pe.wait_ge(rg_sig, 4)
            residual(P_WOUT2, 7 * KC, o_hi, o_lo, KC, LAT, lambda kc: (mix_ready, 8 + kc + 1))
            norm(norms[5])
            cross_queries()
            attention(CROSS)
            cross_output()
            norm(norms[6])
            for G in GROUPS[6:10]:
                hidden_up(G, H_BEFORE[6])
                hidden_down(G)
            norm(norms[7])


def rotary_order(parts, n):
    order = []
    for part in range(parts):
        for f in range(0, n, 16):
            order += [part * 2 * n + f + j for j in range(16)] + [part * 2 * n + n + f + j for j in range(16)]
    return order


def shape_tables():
    tok = np.arange(LAT)
    freqs = 10000.0 ** (-np.arange(32) / 32)
    angle = np.zeros((P, LAT))
    sign = np.zeros((P, 1))
    for p, d in enumerate(rotary_order(2, 32)):
        pos = (tok // 64) if d < 64 else (tok % 64)
        angle[p] = pos * np.float32(freqs[d % 32])
        sign[p] = -1.0 if d % 64 < 32 else 1.0
    rope_grid = np.concatenate([np.cos(angle), sign * np.sin(angle)], axis=1)
    p = np.arange(P)[:, None]
    u_tab = np.arange(UW)[None, :] - 384 - p
    i = np.arange(P)[None, :]
    level_masks = np.concatenate([((p // (2 * h) == i // (2 * h)) & (p // h != i // h)) for h in LEVELS], axis=1)
    return {"rope_grid": rope_grid.astype(np.float32), "u_tab": u_tab.astype(np.float32),
            "level_masks": level_masks.astype(np.int32), "diag2": (2.0 * np.eye(P)).astype(np.float32),
            "ident": np.eye(P, dtype=np.float32)}


def window_tables():
    inv_freq = np.float32(10000.0) ** (-np.arange(32, dtype=np.float32) / np.float32(32))
    order = rotary_order(1, 32) * 2
    pp = np.array([[inv_freq[d % 32], -1.0 if d < 32 else 1.0] for d in order], np.float32)
    i, j = np.arange(LAT)[:, None], np.arange(LAT)[None, :]
    times = sum(((i - j) % dil == 0) & (abs(i - j) <= window // 2) for window, dil in ((128, 1), (512, 4), (2048, 16)))
    bias = np.where(times > 0, np.log(np.maximum(times, 1)) * DH ** 0.5, -1e30)
    bias = bias.reshape(LT, P, LAT).transpose(1, 0, 2).reshape(P, LT * LAT)
    return {"rope_pp_h": pp, "window_bias": bias.astype(np.float32)}


def kernel(**inputs):
    import concourse.bacc as bacc
    from concourse.bass_utils import run_bass_kernel_spmd

    def feature_major(a):
        return np.ascontiguousarray(a.reshape(a.shape[0], KC, P).transpose(2, 1, 0).reshape(P, -1))

    def columns(a):
        return a.reshape(-1, P).T

    a = {k: np.asarray(v) for k, v in inputs.items()}
    vecs = np.zeros((P, N_VEC), np.float32)
    for name, n in VEC_WIDTHS.items():
        v = a[name]
        if name == "conv_w_2":
            v = v.reshape(4, 4 * P)
        vecs[:, VEC_AT[name]:VEC_AT[name] + n] = columns(v)
    panels = np.zeros((N_PANELS, P, PANEL), np.float32)
    at = [0]

    def put(w, k0, n_k, c0):
        block = w[k0 * P:(k0 + n_k) * P, c0:c0 + P].reshape(n_k, P, P).transpose(1, 0, 2)
        panels[at[0], :, 0:n_k * P] = block.reshape(P, n_k * P)
        at[0] += 1

    def put_ffn(w1, w3, w2):
        f = 0
        for g in FF_GROUPS:
            for j in range(g):
                put(w1, 0, KC, (f + j) * P)
                put(w3, 0, KC, (f + j) * P)
            for o in range(KC):
                put(w2, f, g, o * P)
            f += g

    def put_rows(w, c0):
        for k in range(0, KC, 2):
            block = w[k * P:(k + 2) * P, c0:c0 + 512].reshape(2, P, 512).transpose(1, 0, 2)
            panels[at[0]] = block.reshape(P, PANEL)
            at[0] += 1

    put_ffn(a["ffn1_w1"][0], a["ffn1_w3"][0], a["ffn1_w2"][0])
    w = a["w_in"][0]
    assert at[0] == P_WIN
    for c0 in (0, 512):
        rot = w[:, c0:c0 + 512].reshape(D, HEADS, P)[:, :, rotary_order(2, 32)].reshape(D, 512)
        for j in range(HEADS):
            put(rot, 0, KC, j * P)
    put_rows(w, 1024)
    for c0 in (1536, 1536 + 128, 1536 + 256, 1536 + 384, 2048, 2048 + 128, 2304, 2304 + 128):
        put(w, 0, KC, c0)
    put_rows(w, 2560)
    for c0 in (3072, 3200, 3328, 3456):
        put(w, 0, KC, c0)
    assert at[0] == P_WOUT
    for o in range(KC):
        put(a["w_out"][0], 0, KC, o * P)
    put_ffn(a["ffn2_w1"][0], a["ffn2_w3"][0], a["ffn2_w2"][0])
    assert at[0] == P_WIN2
    w2 = a["w_in_2"][0]
    for c0 in (0, 512):
        rot = w2[:, c0:c0 + 512].reshape(D, 8, DH)[:, :, rotary_order(1, 32)].reshape(D, 512)
        for j in range(4):
            put(rot, 0, KC, j * P)
    put_rows(w2, 1024)
    for c0 in range(1536, 2560, P):
        put(w2, 0, KC, c0)
    for c0 in range(0, 512, P):
        put(a["w_ck_2"][0], 0, KC, c0)
    put_rows(a["w_cv_2"][0], 0)
    assert at[0] == P_WOUT2
    for o in range(KC):
        put(a["w_out_2"][0], 0, KC, o * P)
    for o in range(4):
        put(a["w_cq_2"][0], 0, KC, o * P)
    for o in range(0, KC, 2):
        for e in range(2):
            block = a["w_co_2"][0][:, (o + e) * P:(o + e + 1) * P].reshape(4, P, P).transpose(1, 0, 2)
            panels[at[0], :, e * 512:(e + 1) * 512] = block.reshape(P, 512)
        at[0] += 1
    assert at[0] == P_MLP
    for f in range(0, DFF2 // P, 8):
        for j in range(8):
            put(a["w_mlp_in_2"][0], 0, KC, (f + j) * P)
        for o in range(KC):
            put(a["w_mlp_out_2"][0], f, 8, o * P)
    assert at[0] == N_PANELS
    rg_w = np.zeros((P, 2, 2, 4, P), np.float32)
    for z in range(2):
        for g, name in enumerate(("rg_a_w_2", "rg_x_w_2")):
            for n in range(8):
                r = slice(64 * (n % 2), 64 * (n % 2) + 64)
                rg_w[r, z, g, n // 2, r] = a[name][0, z, n]
    arrays = {
        "x_t": feature_major(a["x"][0]),
        "ctx_t": feature_major(a["ctx"][0]),
        "cond": np.concatenate([a["c"][0], a["c_ctx"]]),
        "ada_t": np.ascontiguousarray(a["ada_w"][0].T.reshape(NMOD * KC, P, D)),
        "vecs": vecs,
        "panels": panels,
        "lr_w": np.ascontiguousarray(w[:, 3584:3616].reshape(KC, P, 32).transpose(1, 0, 2).reshape(P, KC * 32)),
        "gate_w": np.concatenate([a["gla_gate_w_f"][0], a["gla_gate_w_b"][0]], axis=1),
        "decays": np.concatenate([a["ret_decay_f"][0], a["ret_decay_b"][0]]),
        **shape_tables(),
        "mem_t": feature_major(a["mem_2"][0]),
        "positions": np.ascontiguousarray(a["positions_2"][0]),
        **window_tables(),
        "rg_w": rg_w.reshape(P, 16 * P),
    }
    nc = bacc.Bacc("TRN2", target_bir_lowering=False, num_devices=1)
    args = [nc.dram_tensor(n, v.shape, mybir.dt.from_np(v.dtype), kind="ExternalInput").ap() for n, v in arrays.items()]
    out = nc.dram_tensor("out", (1, P, KC * LAT), mybir.dt.float32, kind="ExternalOutput").ap()
    build(nc, *args, out)
    r = run_bass_kernel_spmd(nc, [arrays], core_ids=[0])
    got = r.results[0]["out"]
    return np.ascontiguousarray(got.reshape(P, KC, LAT).transpose(2, 1, 0).reshape(1, LAT, D))
```

```python
import math
from contextlib import ExitStack

import numpy as np
import concourse.bass as bass
from concourse import mybir

P = 128
D = 1024
KC = D // P
LAT, CTX = 512, 256
TOK = LAT + CTX
HALF = TOK // 2
DFF = 2816
FF = DFF // P
FF_GROUPS = (8, 8, 6)
assert sum(FF_GROUPS) == FF
DFF2 = 4096
NMOD = 9
EPS = 1e-6
RING = 4
PANEL = KC * P
ADA_RING = 3
ADA_FIRST = 18
ADA_PER_PAIR = (3, 6, 6)
ADA_PE = 9
ADA_ROWS = (2, 2, 1)
assert ADA_FIRST + sum(n * g // 2 for n, g in zip(ADA_PER_PAIR, FF_GROUPS)) == NMOD * KC

N_FFN = sum(2 * g + KC for g in FF_GROUPS)
P_FFN1 = 0
P_WIN = P_FFN1 + N_FFN
P_WOUT = P_WIN + 28
P_FFN2 = P_WOUT + 8
P_WIN2 = P_FFN2 + N_FFN
P_WOUT2 = P_WIN2 + 28
P_CQ = P_WOUT2 + 8
P_CO = P_CQ + 4
P_MLP = P_CO + 4
N_PANELS = P_MLP + 2 * DFF2 // P
assert all(p % RING == 0 for p in (P_WIN, P_WOUT, P_FFN2, P_WIN2, P_WOUT2, P_CQ, P_CO, P_MLP, N_PANELS))

VEC_WIDTHS = dict(norm1_w=8, norm2_w=8, norm3_w=8, final_norm_w=8, norm_mix_g_2=8, norm_cross_g_2=8, norm_mem_g_2=8,
                  norm_mlp_g_2=8, norm_final_g_2=8, ada_b=72, ret_norm_w=4, gla_norm_w=4, gla_gate_b_f=2,
                  gla_gate_b_b=2, conv_b_2=4, conv_w_2=16, rg_a_b_2=8, rg_x_b_2=8, rg_lambda_2=8)
VEC_AT, _n = {}, 0
for _k, _w in VEC_WIDTHS.items():
    VEC_AT[_k] = _n
    _n += _w
N_VEC = _n


WIN = [("rq", 0, 1), ("rq", 1, 1), ("rq", 2, 1), ("rq", 3, 1), ("rg", 4, 1), ("rg", 5, 1), ("rg", 6, 1), ("rg", 7, 1),
       ("rk", 8, 1), ("rk", 9, 1), ("rk", 10, 1), ("rk", 11, 1), ("rv", 12, 4), ("gv", 16, 4), ("gk", 20, 1), ("gk", 21, 1),
       ("gq", 22, 1), ("gq", 23, 1), ("gg", 24, 1), ("gg", 25, 1), ("gg", 26, 1), ("gg", 27, 1)]
WIN_ALONE = 16
FILL = ((16, 17), (18, 19), (20, None), (21, None))
WIN2 = [("u", 0, 1), ("u", 1, 1), ("u", 2, 1), ("u", 3, 1), ("y", 4, 1), ("y", 5, 1), ("y", 6, 1), ("y", 7, 1),
        ("q", 8, 1), ("q", 9, 1), ("q", 10, 1), ("q", 11, 1), ("k", 12, 1), ("k", 13, 1), ("k", 14, 1), ("k", 15, 1), ("v", 16, 4),
        ("ck", 20, 1), ("ck", 21, 1), ("ck", 22, 1), ("ck", 23, 1), ("cv", 24, 4)]
RG_AFTER = {5: 0, 8: 1, 11: 2, 14: 3}
DH = 64
P_BUFS = 4
TWO_PI = (6.28125, round((2 * math.pi - 6.28125) * 2 ** 21) / 2 ** 21, 2 * math.pi - 6.28125 - round((2 * math.pi - 6.28125) * 2 ** 21) / 2 ** 21)
PI_IN = 3.1415925
ROUND = 1.5 * 2 ** 23
TILES = TOK // P
LT = LAT // P
HEADS = 4
UW = 896
LEVELS = (1, 2, 4, 8, 16, 32, 64)
UNITS = len(LEVELS) + 4
SWAP16 = [(i + 16) % 32 for i in range(32)]


def build(nc, x_t, ctx_t, cond, ada_t, vecs, panels, lr_w, gate_w, decays, rope_grid, u_tab, level_masks, diag2, ident_h,
          ada_p, cond_t, mem_t, positions, rope_pp_h, window_bias, rg_w, out):
    f32, f32r, bf16, i32 = mybir.dt.float32, mybir.dt.float32r, mybir.dt.bfloat16, mybir.dt.int32
    ACT, ALU, AX = mybir.ActivationFunctionType, mybir.AluOpType, mybir.AxisListType
    ds = bass.ds

    with ExitStack() as stack:
        KB = 1024
        origin = -(-nc.sbuf_base // 64) * 64

        def at(name, cols, offset, dt=f32, rows=P):
            return nc.alloc_sbuf_tensor_at(name, [rows, cols], dt, offset=origin + offset)

        R_RAW, R_HI, R_LO, R_XL, R_XC, R_H, R_G = 0, 16 * KB, 32 * KB, 48 * KB, 64 * KB, 72 * KB, 120 * KB
        R_TMP, R_ADA, R_VEC = 168 * KB, 180 * KB, 202 * KB

        raw = at("raw", RING * PANEL, R_RAW)
        whi = at("whi", RING * PANEL, R_HI, f32r)
        wlo = at("wlo", RING * PANEL, R_LO, f32r)
        x_lat = at("x_lat", KC * LAT, R_XL)
        x_ctx = at("x_ctx", KC * CTX, R_XC)
        h_hi = at("h_hi", KC * TOK, R_H, f32r)
        h_lo = at("h_lo", KC * TOK, R_H + 24 * KB, f32r)
        g_hi = at("g_hi", KC * TOK, R_G, f32r)
        g_lo = at("g_lo", KC * TOK, R_G + 24 * KB, f32r)
        rdiag = at("rdiag", TOK, R_G)
        act_a = at("act_a", 2 * TOK, R_TMP)
        prod = at("prod", 2 * TOK, R_TMP + 6 * KB)
        ada_f = [at(f"ada_f{k}", PANEL, R_H + 4 * k * KB if k < 12 else R_G + (24 + 4 * (k - 12)) * KB) for k in range(ADA_FIRST)]
        ada_w = at("ada_w", ADA_RING * D, R_ADA)
        cond_b = at("cond_b", 2 * D, R_ADA + 12 * KB)
        cond_s = at("cond_s", 2 * KC, R_TMP + 10 * KB)
        ada_prod = at("ada_prod", D, R_ADA + 20 * KB, bf16)
        vec = at("vec", N_VEC, R_VEC)
        mods = at("mods", 2 * NMOD * KC, R_VEC + 800)
        scales = at("scales", 5 * KC, R_VEC + 1408)
        gates = at("gates", 4 * KC, R_VEC + 1664)
        eps_t = at("eps_t", 1, R_VEC + 1792)
        rms = at("rms", TILES, R_VEC + 5952)
        ones_k = at("ones_k", P, R_VEC + 1824)

        lr_raw = at("lr_raw", KC * 32, R_VEC + 2368)
        gate_sb = at("gate_sb", 512, R_VEC + 3392, rows=16)
        ident = at("ident", P, R_VEC + 5440)
        rq = at("rq", HEADS * LAT, R_G)
        rk = at("rk", HEADS * TOK, R_G + 8 * KB)
        rg = at("rg", HEADS * LAT, R_G + 20 * KB)
        gg = at("gg", HEADS * LAT, R_G + 28 * KB)
        gf = at("gf", 2 * TOK, R_G + 36 * KB)
        gb = at("gb", 2 * TOK, R_G + 42 * KB)
        rv = at("rv", LT * 512, R_ADA)
        gv = at("gv", LT * 512, R_ADA + 8 * KB)
        gq = at("gq", 2 * LAT, R_ADA + 16 * KB)
        rv_c = at("rv_c", 2 * 512, R_XC)
        gv_c = at("gv_c", 2 * 512, R_XC + 4 * KB)
        gk = at("gk", 2 * TOK, R_TMP)
        rope_tmp = at("rope_tmp", LAT, R_TMP + 6 * KB)
        rope_cs = at("rope_cs", 2 * LAT, R_TMP + 8 * KB)
        lr_hi = at("lr_hi", KC * 32, R_ADA, f32r)
        lr_lo = at("lr_lo", KC * 32, R_ADA + KB, f32r)
        lr_sb = at("lr_sb", TILES * 32, R_ADA + 2 * KB)
        lr_t = [at(f"lr_t{d}", TOK, R_ADA + (3 + 3 * d) * KB, rows=16) for d in range(2)]
        gate_y = at("gate_y", TOK, R_ADA + 9 * KB)
        gate_e = at("gate_e", TOK, R_ADA + 12 * KB)
        o_hi = at("o_hi", KC * LAT, R_H, f32r)
        o_lo = at("o_lo", KC * LAT, R_H + 16 * KB, f32r)
        decay_f = at("decay_f", UW + 640, R_H + 16 * KB)
        decay_b = at("decay_b", UW + 640, R_H + 40 * KB)
        s_ring = [at(f"s_ring{b}", LAT, R_H + (22 + 24 * b) * KB) for b in range(2)]
        u_sb = at("u_sb", UW, R_TMP + 8 * KB)
        o_sb = at("o_sb", LAT, R_TMP + 6 * KB)
        o_sq = at("o_sq", LAT, R_ADA + 20 * KB)
        s_gla = at("s_gla", 2 * TILES * LAT, R_G)
        ctx_k = at("ctx_k", 4 * CTX, R_G + 24 * KB)
        q_lv = at("q_lv", 2 * LAT, R_ADA)
        k_lv = at("k_lv", 2 * LAT, R_ADA + 4 * KB)
        d_lv = at("d_lv", 4 * LAT, R_H + 32 * KB)
        cum = at("cum", 4 * LAT, R_H + 40 * KB)
        suf = at("suf", LAT, R_TMP + 8 * KB)
        masks = at("masks", 7 * P, R_XC, i32)
        diag2_sb = at("diag2_sb", P, R_XC + 3584)
        lsig = at("lsig", 16, R_VEC + 1568)
        nlsig = at("nlsig", 4, R_VEC + 1632)
        zero_t = at("zero_t", 1, R_VEC + 2336)
        ls_tmp = at("ls_tmp", 4 * 16, R_TMP + 11 * KB)

        aq = at("aq", 4 * LAT, R_G)
        ak = at("ak", 4 * LAT, R_G + 8 * KB)
        av = at("av", LT * 512, R_G + 16 * KB)
        ru = at("ru", 4 * LAT, R_G + 24 * KB)
        ry = at("ry", 4 * LAT, R_G + 32 * KB)
        ck = at("ck", HEADS * CTX, R_G + 40 * KB)
        cv = at("cv", 2 * 512, R_G + 44 * KB)
        pos_i = at("pos_i", LAT, R_TMP, i32)
        angle = at("angle", LAT, R_TMP + 2 * KB)
        turns = at("turns", LAT, R_TMP + 4 * KB)
        cs2 = at("cs2", 2 * LAT, R_TMP + 8 * KB)
        rope_pp = at("rope_pp", 2, R_VEC + 1376)
        bias_sb = at("bias_sb", LT * LAT, R_ADA)
        prob = at("prob", P_BUFS * LAT, R_ADA + 8 * KB)
        stat = at("stat", 3 * P_BUFS, R_ADA + 16 * KB)
        prob_t = at("prob_t", 2 * LT * LAT, R_H + 32 * KB)
        uc = at("uc", 4 * LAT, R_ADA)
        rg_sb = at("rg_sb", 16 * P, R_ADA + 8 * KB)
        rg_c = at("rg_c", 8, R_ADA + 16 * KB + 64)
        rg_r = at("rg_r", 2 * LAT, R_XC)
        rg_i = at("rg_i", 2 * LAT, R_XC + 4 * KB)
        rg_t = at("rg_t", 2 * LAT, R_ADA + 17 * KB)
        rg_h = at("rg_h", 2 * LAT, R_TMP)

        ps = stack.enter_context(nc.psum_tensor("ps", [P, 8 * 512], f32))

        def bank(b, n=512, c0=0):
            return ps[:, b * 512 + c0:b * 512 + c0 + n]

        sems = {}

        def sem(name):
            sems[name] = stack.enter_context(nc.semaphore(name))
            return sems[name]

        raw_ready = [sem(f"raw_ready{s}") for s in range(RING)]
        hi_done, lo_done, panel_done = sem("hi_done"), sem("lo_done"), sem("panel_done")
        ada_ready = [sem(f"ada_ready{s}") for s in range(ADA_RING)]
        ada_used = sem("ada_used")
        x_loaded, vec_loaded, cond_loaded, consts = sem("x_loaded"), sem("vec_loaded"), sem("cond_loaded"), sem("consts")
        cond_ready = sem("cond_ready")
        ada_loaded = [sem(f"ada_loaded{g}") for g in range(ADA_FIRST)]
        condt_loaded, condt_ready, ada_mods = sem("condt_loaded"), sem("condt_ready"), sem("ada_mods")
        act_chain, dve_chain = sem("act_chain"), sem("dve_chain")
        mods_ready = sem("mods_ready")
        silu_done, up_evac, ghi_done, g_ready, down_evac = (sem(n) for n in ("silu_done", "up_evac", "ghi_done", "g_ready", "down_evac"))
        sq_ready, sum_done, stats_ready, root_ready, diag_ready, rstd_ready, xn_ready, hhi_done, h_ready = (
            sem(n) for n in ("sq_ready", "sum_done", "stats_ready", "root_ready", "diag_ready", "rstd_ready", "xn_ready", "hhi_done",
                             "h_ready"))
        out_done = sem("out_done")
        small_loaded = sem("small_loaded")
        mem_loaded, pos_loaded, win2_evac, cs_arg, cs_ready, rope2_done, bias_loaded, rg_loaded, cq_evac = (
            sem(n) for n in ("mem_loaded", "pos_loaded", "win2_evac", "cs_arg", "cs_ready", "rope2_done", "bias_loaded", "rg_loaded", "cq_evac"))
        a_scores, a_max, a_exp, a_prob, a_trans, a_copied, a_values = (
            sem(n) for n in ("a_scores", "a_max", "a_exp", "a_prob", "a_trans", "a_copied", "a_values"))
        rg_conv, rg_gates, rg_sig, rg_la, rg_exp, rg_v, rg_root, rg_hid = (
            sem(n) for n in ("rg_conv", "rg_gates", "rg_sig", "rg_la", "rg_exp", "rg_v", "rg_root", "rg_hid"))
        ls_exp, lsig_ready = sem("ls_exp"), sem("lsig_ready")
        lr_lo_done = sem("lr_lo_done")
        lr_split, lr_pe, lr_act, gate_act, gate_dve = (sem(n) for n in ("lr_split", "lr_pe", "lr_act", "gate_act", "gate_dve"))
        win_evac, rope_loaded, rope_done, u_loaded, masks_loaded = (
            sem(n) for n in ("win_evac", "rope_loaded", "rope_done", "u_loaded", "masks_loaded"))
        arg_ready, exp_ready, s_ready, s_evac, pv_done = (sem(n) for n in ("arg_ready", "exp_ready", "s_ready", "s_evac", "pv_done"))
        o_ready, o_copied, mean_ready, o_centred, osq_ready, var_ready, oroot_ready, o_scaled, ohi_done, mix_ready = (
            sem(n) for n in ("o_ready", "o_copied", "mean_ready", "o_centred", "osq_ready", "var_ready", "oroot_ready",
                             "o_scaled", "ohi_done", "mix_ready"))
        d_ready, x_ready, qk_ready, unit_ready, unit_dve, unit_act, ctx_arg, ctx_exp = (
            sem(n) for n in ("d_ready", "x_ready", "qk_ready", "unit_ready", "unit_dve", "unit_act", "ctx_arg", "ctx_exp"))
        block = stack.enter_context(nc.Block())

        def done(p):
            return p + RING + 1

        def token_cols(T):
            return [(0, 0, LAT), (1, LAT, CTX)] if T == TOK else [(0, 0, T)]

        def h_at(kc, token):
            return kc * LAT + token if token < LAT else KC * LAT + kc * CTX + token - LAT

        def merged_at(kc, token):
            return kc * LAT + token

        def hidden_at(kc, token):
            return kc * TOK + token

        def vcol(name, j=0, n=1):
            return vec[:, VEC_AT[name] + j:VEC_AT[name] + j + n]

        def mod(row, part):
            c = (row * NMOD + part) * KC
            return mods[:, c:c + KC]

        class Norm:
            def __init__(self, n, T, A, B, last=False):
                self.n, self.T, self.A, self.B, self.last = n, T, A, B, last

            def segs(self):
                s = [(x_lat, LAT, 0, 0)]
                return s + [(x_ctx, CTX, LAT, 1)] if self.T == TOK else s

        def sc(j):
            return lambda kc: scales[:, j * KC + kc:j * KC + kc + 1]

        def md(row, part):
            return lambda kc: mods[:, (row * NMOD + part) * KC + kc:(row * NMOD + part) * KC + kc + 1]

        def vc(name):
            return lambda kc: vcol(name, kc)

        norms = [Norm(0, TOK, (sc(0), sc(1)), (md(0, 0), md(1, 0))),
                 Norm(1, TOK, (sc(2), sc(3)), (md(0, 3), md(1, 3))),
                 Norm(2, LAT, (sc(4),), (md(0, 6),)),
                 Norm(3, LAT, (vc("final_norm_w"),), None, True),
                 Norm(4, TOK, (vc("norm_mix_g_2"), vc("norm_mem_g_2")), None),
                 Norm(5, LAT, (vc("norm_cross_g_2"),), None),
                 Norm(6, LAT, (vc("norm_mlp_g_2"),), None),
                 Norm(7, LAT, (vc("norm_final_g_2"),), None, True)]
        H_BEFORE = [sum(8 for m in norms[:n] if not m.last) for n in range(9)]

        def hidden_groups():
            f, rows = 0, []
            for layer, (p0, T, sizes, gated) in enumerate(((P_FFN1, TOK, FF_GROUPS, True), (P_FFN2, LAT, FF_GROUPS, True),
                                                        (P_MLP, LAT, (8,) * 4, False))):
                p, o = p0, (0, 4 * KC, 9 * KC)[layer]
                for n, g in enumerate(sizes):
                    n_up = (2 if gated else 1) * g
                    rows.append(dict(layer=layer, n=n, T=T, g=g, gated=gated, p_up=p, p_down=p + n_up, f0=f, o0=o, last=n == len(sizes) - 1))
                    p += n_up + KC
                    f += g
                    o += KC
            return rows

        GROUPS = hidden_groups()
        squares = [prod[:, 0:TOK], act_a[:, TOK:2 * TOK]]

        def ada_before(n):
            return ADA_FIRST + sum(ADA_PER_PAIR[m] * FF_GROUPS[m] // 2 for m in range(n))

        def ada_rows(n, k):
            k0 = ada_before(n)
            return sum(r * (ada_before(m + 1) - ada_before(m)) for m, r in enumerate(ADA_ROWS[:n])) + 2 * ADA_FIRST + ADA_ROWS[n] * (k - k0)

        def x_final(n):
            return {1: 3, 2: 4, 3: 7, 5: 8, 6: 9, 7: 13}[n] * KC

        def attention_items(heads, q, k, v, dk, keys, n0, p0, s0):
            return dict(heads=heads, q=q, k=k, v=v, dk=dk, keys=keys, n0=n0, h0=p0, s0=s0, n=heads * LT)

        SELF = attention_items(8, aq, ak, av, DH, LAT, 0, 0, 12)
        CROSS = attention_items(HEADS, aq, ck, cv, P, CTX, 8 * LT, 8, 16)

        V_BANKS = {"v": (0, 2, 4, 6), "cv": (0, 2), "rv": (0, 1, 2, 3, 4, 5), "gv": (0, 1, 2, 3, 4, 5)}

        FILL_BANK = 5

        def unit_bank(u, a):
            return 4 * (u % 2) + 2 * a

        @block.sync
        def _(sp):
            sp.dma_start(vec[:, :], vecs).then_inc(vec_loaded, 16)
            sp.dma_start(cond_s[:, :], cond_t).then_inc(condt_loaded, 16)
            sp.dma_start(cond_b[:, :], cond.partition_broadcast(P)).then_inc(cond_loaded, 16)
            sp.dma_start(lsig[:, 0:8], decays.partition_broadcast(P)).then_inc(small_loaded, 16)
            sp.dma_start(lr_raw[:, :], lr_w).then_inc(small_loaded, 16)
            sp.dma_start(gate_sb[:, :], gate_w).then_inc(small_loaded, 16)
            sp.dma_start(ident[:, :], ident_h).then_inc(small_loaded, 16)
            sp.dma_start(rope_pp[:, :], rope_pp_h).then_inc(small_loaded, 16)
            sp.dma_start(x_lat[:, :], x_t).then_inc(x_loaded, 16)
            sp.dma_start(x_ctx[:, :], ctx_t).then_inc(x_loaded, 16)
            for k in range(ADA_PE):
                sp.dma_start(ada_f[k][:, :], ada_p[k]).then_inc(ada_loaded[k], 16)
                sp.dma_start(ada_f[ADA_PE + k][:, :], ada_t[ADA_PE + k]).then_inc(ada_loaded[ADA_PE + k], 16)
            for s in range(RING):
                sp.dma_start(raw[:, s * PANEL:(s + 1) * PANEL], panels[s]).then_inc(raw_ready[s], 16)
            with sp.Fori(1, N_PANELS // RING) as i:
                for s in range(RING):
                    sp.wait_ge(lo_done, (i - 1) * RING + s + 1)
                    sp.dma_start(raw[:, s * PANEL:(s + 1) * PANEL],
                                 panels[ds(i * RING + s, 1)].rearrange("a p n -> (a p) n")).then_inc(raw_ready[s], 16)
            for kc in range(KC):
                sp.wait_ge(xn_ready, 7 * KC + kc + 1)
                sp.dma_start(out[0, :, kc * LAT:(kc + 1) * LAT], x_lat[:, kc * LAT:(kc + 1) * LAT]).then_inc(out_done, 16)
            sp.wait_ge(out_done, 16 * KC)

        @block.gpsimd
        def _(pool):
            pool.memset(ones_k[:, :], 1.0 / D).then_inc(consts, 1)
            pool.memset(eps_t[:, :], EPS).then_inc(consts, 1)
            pool.memset(zero_t[:, :], 0.0).then_inc(consts, 1)
            with pool.Fori(0, N_PANELS // RING) as i:
                for s in range(RING):
                    pool.wait_ge(hi_done, i * RING + s + 1)
                    sl = slice(s * PANEL, (s + 1) * PANEL)
                    pool.tensor_tensor(wlo[:, sl], raw[:, sl], whi[:, sl].bitcast(f32), ALU.subtract).then_inc(lo_done, 1)

        @block.scalar
        def _(act):
            chain = [0]

            def link(ins):
                chain[0] += 1
                ins.then_inc(act_chain, 1)
                act.wait_ge(act_chain, chain[0])

            def round_panel(s, turn, p_done=None):
                act.wait_ge(raw_ready[s], turn * 16)
                if p_done is not None:
                    act.wait_ge(panel_done, done(p_done))
                sl = slice(s * PANEL, (s + 1) * PANEL)
                act.activation(whi[:, sl], raw[:, sl], ACT.Copy).then_inc(hi_done, 1)

            def round_ahead(p0, i, c):
                q = p0 + c + 2
                round_panel(q % RING, i + (q // RING + 1), i * RING + (q - RING))

            def square(m, kc):
                if m.n == 0:
                    act.wait_ge(x_loaded, 32)
                elif m.n == 4:
                    act.wait_ge(mem_loaded, 16)
                    act.wait_ge(xn_ready, 3 * KC + kc + 1)
                else:
                    act.wait_ge(down_evac, x_final(m.n) + kc + 1)
                if kc >= 3:
                    act.wait_ge(sum_done, m.n * (KC - 1) + kc - 2)
                buf = act_a[:, 0:TOK] if kc == 0 else squares[kc % 2]
                for xs, n, c0, _ in m.segs():
                    ins = act.activation(buf[:, c0:c0 + n], xs[:, kc * n:(kc + 1) * n], ACT.Square)
                ins.then_inc(sq_ready, 1)

            def norm(m):
                act.wait_ge(stats_ready, m.n + 1)
                act.activation(rms[:, 0:m.T // P], bank(4, m.T // P), ACT.Sqrt, bias=eps_t[:, :]).then_inc(root_ready, 1)
                if m.n == 0:
                    round_panel(0, 1)
                    round_panel(1, 1)
                if m.last:
                    return
                for kc in range(KC):
                    act.wait_ge(xn_ready, m.n * KC + kc + 1)
                    b = (kc % 2) * TOK
                    for j, (_, n, c0, _) in enumerate(m.segs()):
                        o = h_hi[:, h_at(kc, c0):h_at(kc, c0) + n]
                        if m.B is None:
                            ins = act.activation(o, prod[:, b + c0:b + c0 + n], ACT.Copy)
                        else:
                            ins = act.activation(o, prod[:, b + c0:b + c0 + n], ACT.Identity, bias=m.B[j](kc))
                    ins.then_inc(hhi_done, 1)

            def hidden_up(G):
                T, cols = G["T"], token_cols(G["T"])
                per_f = 2 if G["gated"] else 1
                f_per = RING // per_f
                with act.Fori(0, G["g"] // f_per) as i:
                    for u in range(f_per):
                        if G["layer"] == 0 and (u == 0 or ADA_PER_PAIR[G["n"]] == 6):
                            for j in range(ADA_RING):
                                k = ada_before(G["n"]) + i * ADA_PER_PAIR[G["n"]] + u * ADA_RING + j
                                act.wait_ge(ada_used, ada_rows(G["n"], k - ADA_RING + 1))
                                act.dma_start(ada_w[:, j * D:(j + 1) * D],
                                              ada_t[ds(k, 1)].rearrange("a p n -> (a p) n")).then_inc(ada_ready[j], 16)
                        for c in range(per_f):
                            round_ahead(G["p_up"], i, u * per_f + c)
                        f = G["f0"] + i * f_per + u
                        b = (u % 2) * TOK
                        act.wait_ge(panel_done, done(G["p_up"] + i * RING + u * per_f))
                        act.wait_ge(up_evac, f + 1)
                        b0 = 2 * u * per_f
                        src, dst = bank(b0, T), act_a[:, b:b + T]
                        act.activation(dst, src, ACT.Silu if G["gated"] else ACT.Relu).then_inc(silu_done, 1)
                        act.wait_ge(up_evac, f + 3)
                        fo = (i * f_per + u) * TOK
                        act.activation(g_hi[:, ds(fo, T)], prod[:, b:b + T], ACT.Copy).then_inc(ghi_done, 1)

            def hidden_down(G):
                if G["last"]:
                    outputs_and_squares(G["p_down"], norms[(1, 3, 7)[G["layer"]]])
                    return
                with act.Fori(0, KC // RING) as i:
                    for c in range(RING):
                        round_ahead(G["p_down"], i, c)

            def outputs_and_squares(p0, m):
                for o in range(KC):
                    q = p0 + o + 2
                    if q < N_PANELS:
                        round_panel(q % RING, q // RING + 1, q - RING)
                    if o >= 2:
                        square(m, o - 2)
                square(m, KC - 2)
                square(m, KC - 1)

            def head_out(j):
                act.wait_ge(o_ready, j + 1)
                if j:
                    act.wait_ge(o_scaled, j)
                if j > HEADS:
                    act.wait_ge(mix_ready, j)
                act.activation(o_sb[:, :], bank(2), ACT.Copy).then_inc(o_copied, 1)

            def head_squares(j):
                if j < HEADS:
                    act.wait_ge(o_centred, j + 1)
                else:
                    act.wait_ge(o_copied, j + 1)
                act.activation(o_sq[:, :], o_sb[:, :], ACT.Square).then_inc(osq_ready, 1)

            def head_root(j):
                act.wait_ge(var_ready, j + 1)
                act.activation(o_sq[:, :], bank(4), ACT.Sqrt, bias=eps_t[:, :], scale=float(D // P)).then_inc(oroot_ready, 1)

            def head_hi(j):
                act.wait_ge(o_scaled, j + 1)
                if j < HEADS:
                    act.wait_ge(pv_done, 6 * HEADS)
                    act.wait_ge(panel_done, done(P_WOUT - 1))
                src = rg[:, j * LAT:(j + 1) * LAT] if j < HEADS else o_sb[:, :]
                act.activation(o_hi[:, j * LAT:(j + 1) * LAT], src, ACT.Copy).then_inc(ohi_done, 1)

            def gate_step(n):
                if n == 0:
                    act.wait_ge(lr_pe, 1)
                    act.activation(lr_sb[:, :], bank(7, TILES * 32), ACT.Copy).then_inc(lr_act, 1)
                elif n == 1:
                    act.wait_ge(lr_pe, 2)
                    for d in range(2):
                        for b in range(2):
                            c = (1 + 4 * d + 2 * b) * 512
                            ins = act.activation(lr_t[d][:, b * HALF:(b + 1) * HALF], ps[0:16, c:c + HALF], ACT.Copy)
                    ins.then_inc(lr_act, 1)
                elif n < 6:
                    d, hp = divmod(n - 2, 2)
                    act.wait_ge(lr_pe, 1 + n)
                    if n > 2:
                        act.wait_ge(gate_dve, n - 2)
                    for b in range(2):
                        ins = act.activation(gate_y[:, b * HALF:(b + 1) * HALF], bank(1 + 4 * hp + 2 * b, HALF), ACT.Identity,
                                             bias=vcol(("gla_gate_b_f", "gla_gate_b_b")[d], hp))
                    link(ins)
                    link(act.activation(gate_e[:, :], gate_y[:, :], ACT.Abs))
                    link(act.activation(gate_e[:, :], gate_e[:, :], ACT.Exp, scale=-1.0))
                    act.activation(gate_e[:, :], gate_e[:, :], ACT.Ln, bias=1.0).then_inc(gate_act, 1)

            def projected(n, b):
                kind, first, n_p = WIN[n]
                for c in range(n_p):
                    q = P_WIN + first + c + 2
                    round_panel(q % RING, q // RING + 1, q - RING)
                act.wait_ge(panel_done, done(P_WIN + first + n_p - 1))
                j = first % 4
                if kind == "rq":
                    act.activation(rq[:, j * LAT:(j + 1) * LAT], bank(b), ACT.Copy, scale=P ** -0.5).then_inc(win_evac, 1)
                elif kind in ("rk", "gk"):
                    j = first - 20 if kind == "gk" else j
                    dst = (rk if kind == "rk" else gk)[:, j * TOK:(j + 1) * TOK]
                    act.activation(dst, bank(b, TOK), ACT.Copy).then_inc(win_evac, 1)
                elif kind == "gq":
                    j = first - 22
                    act.activation(gq[:, j * LAT:(j + 1) * LAT], bank(b), ACT.Copy, scale=64 ** -0.5).then_inc(win_evac, 1)
                elif kind in ("rg", "gg"):
                    dst = (rg if kind == "rg" else gg)[:, j * LAT:(j + 1) * LAT]
                    act.activation(dst, bank(b), ACT.Silu).then_inc(win_evac, 1)
                else:
                    if kind == "rv":
                        act.wait_ge(gate_dve, 4)
                    lat, ctx = (rv, rv_c) if kind == "rv" else (gv, gv_c)
                    for t in range(TILES):
                        dst = lat[:, t * 512:(t + 1) * 512] if t < LT else ctx[:, (t - LT) * 512:(t - LT + 1) * 512]
                        ins = act.activation(dst, bank(V_BANKS[kind][t]), ACT.Copy)
                    ins.then_inc(win_evac, 1)

            def input_projection():
                act.wait_ge(h_ready, H_BEFORE[2])
                act.dma_start(rope_cs[:, :], rope_grid).then_inc(rope_loaded, 16)
                act.wait_ge(small_loaded, 80)
                act.activation(lr_hi[:, :], lr_raw[:, :], ACT.Copy).then_inc(lr_split, 1)
                for n in range(WIN_ALONE):
                    projected(n, 2 * (WIN[n][1] % RING))
                    gate_step(n)

            def retention():
                act.wait_ge(rope_done, 8)
                act.dma_start(u_sb[:, :], u_tab).then_inc(u_loaded, 16)

                def exponentials(j):
                    act.wait_ge(arg_ready, j + 1)
                    act.activation(decay_f[:, :], decay_f[:, :], ACT.Exp)
                    act.activation(decay_b[:, :], decay_b[:, :], ACT.Exp).then_inc(exp_ready, 1)

                exponentials(0)
                for j in range(HEADS):
                    head_out(j)
                    if j + 1 < HEADS:
                        exponentials(j + 1)
                    for half, step in enumerate((head_squares, head_root)):
                        if FILL[j][half]:
                            projected(FILL[j][half], FILL_BANK)
                        step(j)
                for j in range(HEADS):
                    head_hi(j)

            def gla():
                act.wait_ge(pv_done, 6 * HEADS)
                act.dma_start(masks[:, :], level_masks).then_inc(masks_loaded, 16)
                act.dma_start(diag2_sb[:, :], diag2).then_inc(masks_loaded, 16)
                for hp in range(2):
                    act.wait_ge(ctx_arg, hp + 1)
                    act.activation(ctx_k[:, 0:2 * CTX], ctx_k[:, 0:2 * CTX], ACT.Exp).then_inc(ctx_exp, 1)
                    for u in range(1, UNITS):
                        n = hp * (UNITS - 1) + u
                        act.wait_ge(d_ready, n)
                        b = (u % 2) * 2 * LAT
                        if u < UNITS - 1:
                            h = 2 ** (u - 1)
                            v = d_lv[:, b:b + 2 * LAT].rearrange("p (n t h) -> p n t h", t=2, h=h)
                            act.activation(v[:, :, 0, :], v[:, :, 0, :], ACT.Exp, scale=-1.0)
                            act.activation(v[:, :, 1, :], v[:, :, 1, :], ACT.Exp).then_inc(x_ready, 1)
                        else:
                            act.activation(d_lv[:, b:b + 2 * LAT], d_lv[:, b:b + 2 * LAT], ACT.Exp).then_inc(x_ready, 1)
                        if u - 1 >= len(LEVELS) + 1:
                            unit_copy(hp, u - 1)
                    unit_copy(hp, UNITS - 1)
                    for a in range(2):
                        for step in (head_out, head_squares, head_root, head_hi):
                            step(HEADS + 2 * hp + a)

            def unit_copy(hp, u):
                act.wait_ge(unit_ready, hp * UNITS + u + 1)
                for a in range(2):
                    S = s_gla[:, a * TILES * LAT:(a + 1) * TILES * LAT].rearrange("p (j i) -> p j i", j=TILES)
                    b = unit_bank(u, a)
                    if u == UNITS - 3:
                        for t in range(LT):
                            o = (t ^ 1) * P
                            ins = act.activation(S[:, t, o:o + P], bank(b, P, t * P), ACT.Copy)
                    elif u == UNITS - 2:
                        for half in range(2):
                            ins = act.activation(S[:, 2 * half:2 * half + 2, (1 - half) * 256:(2 - half) * 256],
                                                 bank(b + half).rearrange("p (j i) -> p j i", j=2), ACT.Copy)
                    else:
                        ins = act.activation(S[:, LT:TILES, :], ps[:, b * 512:(b + 2) * 512].rearrange("p (j i) -> p j i", j=2), ACT.Copy)
                ins.then_inc(unit_act, 1)

            def input_projection2():
                act.wait_ge(h_ready, H_BEFORE[5])
                act.dma_start(pos_i[:, :], positions.partition_broadcast(P)).then_inc(pos_loaded, 16)
                act.dma_start(rg_sb[:, :], rg_w).then_inc(rg_loaded, 16)
                for n, (kind, first, n_p) in enumerate(WIN2):
                    for c in range(n_p):
                        q = P_WIN2 + first + c + 2
                        round_panel(q % RING, q // RING + 1, q - RING)
                    act.wait_ge(panel_done, done(P_WIN2 + first + n_p - 1))
                    j = first % 4
                    b = 2 * (first % RING)
                    if kind in ("q", "k", "u"):
                        dst = {"q": aq, "k": ak, "u": ru}[kind]
                        act.activation(dst[:, j * LAT:(j + 1) * LAT], bank(b), ACT.Copy).then_inc(win2_evac, 1)
                    elif kind == "y":
                        act.activation(ry[:, j * LAT:(j + 1) * LAT], bank(b), ACT.Gelu_apprx_tanh).then_inc(win2_evac, 1)
                    elif kind == "ck":
                        act.activation(ck[:, j * CTX:(j + 1) * CTX], bank(b, CTX), ACT.Copy).then_inc(win2_evac, 1)
                    else:
                        dst = av if kind == "v" else cv
                        for t, vb in enumerate(V_BANKS[kind]):
                            ins = act.activation(dst[:, t * 512:(t + 1) * 512], bank(vb), ACT.Copy)
                        ins.then_inc(win2_evac, 1)
                    if n == 1:
                        act.wait_ge(cs_arg, 1)
                        act.activation(cs2[:, :], cs2[:, :], ACT.Sin).then_inc(cs_ready, 1)
                    for step, m in enumerate((n, n - 1, n - 2)):
                        if m in RG_AFTER:
                            rg_step(RG_AFTER[m], step)
                    if kind == "v":
                        act.wait_ge(rg_hid, 4)
                        act.dma_start(bias_sb[:, :], window_bias).then_inc(bias_loaded, 16)

            def rg_step(c, step):
                if step == 0:
                    act.wait_ge(rg_gates, c + 1)
                    if c:
                        act.wait_ge(rg_hid, c)
                    for z in range(2):
                        sl = slice(z * LAT, (z + 1) * LAT)
                        act.activation(rg_r[:, sl], bank(1 + 4 * z), ACT.Sigmoid, bias=vcol("rg_a_b_2", 4 * z + c))
                        ins = act.activation(rg_i[:, sl], bank(3 + 4 * z), ACT.Sigmoid, bias=vcol("rg_x_b_2", 4 * z + c))
                    ins.then_inc(rg_sig, 1)
                elif step == 1:
                    act.wait_ge(rg_la, c + 1)
                    link(act.activation(rg_t[:, :], rg_r[:, :], ACT.Tanh))
                    act.activation(rg_r[:, :], rg_r[:, :], ACT.Exp, scale=-1.0).then_inc(rg_exp, 1)
                else:
                    act.wait_ge(rg_v, c + 1)
                    act.activation(rg_t[:, :], rg_t[:, :], ACT.Sqrt).then_inc(rg_root, 1)

            def rg_split():
                act.wait_ge(panel_done, done(P_WOUT2 - 1))
                for c in range(4):
                    act.activation(o_hi[:, (4 + c) * LAT:(5 + c) * LAT], ru[:, c * LAT:(c + 1) * LAT], ACT.Copy).then_inc(ohi_done, 1)

            def attention(A):
                for n in range(A["n"] + 2):
                    if n < A["n"]:
                        N = A["n0"] + n
                        sl = N % P_BUFS
                        act.wait_ge(a_max, N + 1)
                        row = prob[:, sl * LAT:sl * LAT + A["keys"]]
                        act.activation(row, row, ACT.Exp, bias=stat[:, sl:sl + 1], scale=float(A["dk"]) ** -0.5,
                                       accum_out=stat[:, P_BUFS + sl:P_BUFS + sl + 1]).then_inc(a_exp, 1)
                    if n >= 2:
                        m = n - 2
                        hd, it = divmod(m, LT)
                        act.wait_ge(a_trans, A["n0"] + m + 1)
                        H = A["h0"] + hd
                        if it == 0 and H >= 2:
                            act.wait_ge(a_values, H - 1)
                        kt = A["keys"] // P
                        dst = prob_t[:, (hd % 2) * LT * LAT:(hd % 2 + 1) * LT * LAT].rearrange("p (j i) -> p j i", j=LT)
                        act.activation(dst[:, 0:kt, it * P:(it + 1) * P], bank(2 + m % 2, kt * P).rearrange("p (j i) -> p j i", j=kt),
                                       ACT.Copy).then_inc(a_copied, 1)
                        if it == LT - 1 and (A["dk"] == P or hd % 2):
                            act.wait_ge(a_values, H + 1)
                            c = hd if A["dk"] == P else hd // 2
                            act.activation(o_hi[:, c * LAT:(c + 1) * LAT], bank(4 + c % 2), ACT.Copy).then_inc(ohi_done, 1)

            def cross_queries():
                for j in range(4):
                    q = P_CQ + j + 2
                    round_panel(q % RING, q // RING + 1, q - RING)
                    act.wait_ge(panel_done, done(P_CQ + j))
                    act.activation(aq[:, j * LAT:(j + 1) * LAT], bank(2 * j), ACT.Copy).then_inc(cq_evac, 1)

            act.wait_ge(vec_loaded, 16)
            act.wait_ge(small_loaded, 80)
            link(act.activation(lsig[:, 8:16], vcol("rg_lambda_2", 0, 8), ACT.Copy))
            link(act.activation(ls_tmp[:, 0:16], lsig[:, :], ACT.Abs))
            act.activation(ls_tmp[:, 0:16], ls_tmp[:, 0:16], ACT.Exp, scale=-1.0).then_inc(ls_exp, 1)
            act.wait_ge(condt_loaded, 16)
            act.activation(cond_s[:, :], cond_s[:, :], ACT.Silu).then_inc(condt_ready, 1)
            act.wait_ge(cond_loaded, 16)
            act.activation(cond_b[:, :], cond_b[:, :], ACT.Silu).then_inc(cond_ready, 1)
            act.wait_ge(consts, 3)
            for kc in range(KC):
                square(norms[0], kc)
            norm(norms[0])
            for G in GROUPS[0:3]:
                hidden_up(G)
                hidden_down(G)
            norm(norms[1])
            input_projection()
            retention()
            gla()
            outputs_and_squares(P_WOUT, norms[2])
            norm(norms[2])
            for G in GROUPS[3:6]:
                hidden_up(G)
                hidden_down(G)
            act.wait_ge(o_ready, 8)
            act.dma_start(x_ctx[:, :], mem_t).then_inc(mem_loaded, 16)
            norm(norms[3])
            for kc in range(KC):
                square(norms[4], kc)
            norm(norms[4])
            input_projection2()
            rg_split()
            attention(SELF)
            outputs_and_squares(P_WOUT2, norms[5])
            norm(norms[5])
            cross_queries()
            attention(CROSS)
            for c, q in enumerate(range(P_CO + 2, P_CO + 6)):
                round_panel(q % RING, q // RING + 1, q - RING)
                if c:
                    square(norms[6], 2 * c - 2)
                    square(norms[6], 2 * c - 1)
            square(norms[6], KC - 2)
            square(norms[6], KC - 1)
            norm(norms[6])
            for G in GROUPS[6:10]:
                hidden_up(G)
                hidden_down(G)
            norm(norms[7])

        @block.vector
        def _(dve):
            chain = [0]

            def link(ins):
                chain[0] += 1
                ins.then_inc(dve_chain, 1)
                dve.wait_ge(dve_chain, chain[0])

            def ada_products(k, w, rows, rows_done):
                for r in range(rows):
                    dve.wait_ge(ada_used, rows_done + r)
                    dve.scalar_tensor_tensor(out=ada_prod[:, :], in0=w, scalar=1.0, in1=cond_b[:, r * D:(r + 1) * D], op0=ALU.mult,
                                             op1=ALU.mult, accum_out=mods[:, ds(r * NMOD * KC + k, 1)]).then_inc(ada_used, 1)

            def ada_chunk(k, s, turn, rows, rows_done):
                dve.wait_ge(ada_ready[s], turn * 16)
                ada_products(k, ada_w[:, s * D:(s + 1) * D], rows, rows_done)

            def add_bias(parts, rows):
                n = (parts[1] - parts[0]) * KC
                for r in range(rows):
                    c = (r * NMOD + parts[0]) * KC
                    link(dve.tensor_tensor(mods[:, c:c + n], mods[:, c:c + n], vcol("ada_b", parts[0] * KC, n), ALU.add))

            def norm_scale(j, row, part, w):
                link(dve.scalar_tensor_tensor(scales[:, j * KC:(j + 1) * KC], mod(row, part), 1.0, vcol(w, 0, KC), ALU.add, ALU.mult))

            def add_squares(m, kc):
                dve.wait_ge(sq_ready, m.n * KC + kc + 1)
                if kc >= 2:
                    dve.wait_ge(sum_done, m.n * (KC - 1) + kc - 1)
                dve.tensor_tensor(act_a[:, 0:m.T], act_a[:, 0:m.T], squares[kc % 2][:, 0:m.T], ALU.add).then_inc(sum_done, 1)

            def token_factors(m):
                n = m.T // P
                dve.wait_ge(root_ready, m.n + 1)
                link(dve.reciprocal(rms[:, 0:n], rms[:, 0:n]))
                dst = rdiag[:, 0:m.T].rearrange("p (t i) -> p t i", i=P)
                eye = ident[:, :].rearrange("p (o i) -> p o i", o=1).broadcast_to([P, n, P])
                r = rms[:, 0:n].rearrange("p (t o) -> p t o", o=1).broadcast_to([P, n, P])
                dve.scalar_tensor_tensor(dst, eye, float(D), r, ALU.mult, ALU.mult).then_inc(diag_ready, 1)

            def norm(m):
                if m.n:
                    token_factors(m)
                dve.wait_ge(rstd_ready, m.n + 1)
                for kc in range(KC + 1):
                    if kc < KC:
                        b = (kc % 2) * TOK
                        for j, (xs, n, c0, _) in enumerate(m.segs()):
                            o = xs[:, kc * n:(kc + 1) * n] if m.last else prod[:, b + c0:b + c0 + n]
                            ins = dve.scalar_tensor_tensor(o, xs[:, kc * n:(kc + 1) * n], m.A[j](kc), bank(6 + j, n),
                                                           ALU.mult, ALU.mult)
                        ins.then_inc(xn_ready, 1)
                    if m.n == 3 and kc > 1:
                        add_squares(norms[4], kc - 1)
                    if kc > 0 and not m.last:
                        k = kc - 1
                        b = (k % 2) * TOK
                        dve.wait_ge(hhi_done, H_BEFORE[m.n] + k + 1)
                        dve.wait_ge(xn_ready, m.n * KC + k + 1)
                        for j, (_, n, c0, _) in enumerate(m.segs()):
                            sl = slice(h_at(k, c0), h_at(k, c0) + n)
                            src = prod[:, b + c0:b + c0 + n]
                            if m.B is None:
                                ins = dve.tensor_tensor(h_lo[:, sl], src, h_hi[:, sl].bitcast(f32), ALU.subtract)
                            else:
                                ins = dve.scalar_tensor_tensor(h_lo[:, sl], src, m.B[j](k), h_hi[:, sl].bitcast(f32),
                                                               ALU.add, ALU.subtract)
                        ins.then_inc(h_ready, 1)
                        dve.wait_ge(h_ready, H_BEFORE[m.n] + k + 1)

            def hidden_up(G):
                T, cols = G["T"], token_cols(G["T"])
                per_f = 2 if G["gated"] else 1
                f_per = RING // per_f
                with dve.Fori(0, G["g"] // f_per) as i:
                    for u in range(f_per):
                        if G["layer"] == 0 and (u == 0 or ADA_PER_PAIR[G["n"]] == 6):
                            npp = ADA_PER_PAIR[G["n"]]
                            for j in range(ADA_RING):
                                k = ada_before(G["n"]) + i * npp + u * ADA_RING + j
                                ada_chunk(k, j, ((ada_before(G["n"]) - ADA_FIRST) // ADA_RING) + i * (npp // ADA_RING) + u + 1, ADA_ROWS[G["n"]],
                                          ada_rows(G["n"], k))
                        f = G["f0"] + i * f_per + u
                        b = (u % 2) * TOK
                        dve.wait_ge(panel_done, done(G["p_up"] + i * RING + (u + 1) * per_f - 1))
                        dve.wait_ge(silu_done, f + 1)
                        dve.wait_ge(g_ready, f + 1)
                        if G["gated"]:
                            dve.tensor_tensor(prod[:, b:b + T], act_a[:, b:b + T], bank(4 * u + 2, T), ALU.mult).then_inc(up_evac, 1)
                        else:
                            dve.tensor_tensor(prod[:, b:b + T], act_a[:, b:b + T], act_a[:, b:b + T], ALU.mult).then_inc(up_evac, 1)
                        dve.wait_ge(ghi_done, f + 1)
                        fo = (i * f_per + u) * TOK
                        dve.tensor_tensor(g_lo[:, ds(fo, T)], prod[:, b:b + T], g_hi[:, ds(fo, T)].bitcast(f32), ALU.subtract)\
                            .then_inc(g_ready, 1)

            def hidden_down(G):
                T = G["T"]
                def add(dst, src, gate):
                    return dve.scalar_tensor_tensor(dst, src, gate, dst, ALU.mult, ALU.add)

                def output(o, c):
                    dve.wait_ge(panel_done, done(G["p_down"] + o))
                    dve.wait_ge(down_evac, G["o0"] + o + 1)
                    if T == TOK:
                        add(x_lat[:, ds(o * LAT, LAT)], bank(2 * c), gates[:, ds(o, 1)])
                        ins = add(x_ctx[:, ds(o * CTX, CTX)], bank(2 * c + 1, CTX), gates[:, ds(o + KC, 1)])
                    elif G["gated"]:
                        ins = add(x_lat[:, ds(o * LAT, LAT)], bank(2 * c), gates[:, ds(o + 3 * KC, 1)])
                    else:
                        dst = x_lat[:, ds(o * LAT, LAT)]
                        ins = dve.tensor_tensor(dst, bank(2 * c), dst, ALU.add)
                    ins.then_inc(down_evac, 1)

                if G["last"]:
                    for o in range(KC):
                        output(o, o % RING)
                        if o:
                            add_squares(norms[(1, 3, 7)[G["layer"]]], o)
                    return
                with dve.Fori(0, KC // RING) as i:
                    for c in range(RING):
                        output(i * RING + c, c)

            def log_sigmoids():
                z, w, w2, p = (ls_tmp[:, j * 16:(j + 1) * 16] for j in range(4))
                dve.wait_ge(ls_exp, 1)
                link(dve.tensor_scalar(w, z, 2.0, None, ALU.add))
                link(dve.reciprocal(w, w))
                link(dve.tensor_tensor(w, w, z, ALU.mult))
                link(dve.tensor_tensor(w2, w, w, ALU.mult))
                link(dve.tensor_scalar(p, w2, 1.0 / 17, 1.0 / 15, ALU.mult, ALU.add))
                for k in (13, 11, 9, 7, 5, 3, 1):
                    link(dve.tensor_tensor(p, p, w2, ALU.mult))
                    link(dve.tensor_scalar(p, p, 1.0 / k, None, ALU.add))
                link(dve.scalar_tensor_tensor(p, p, 2.0, w, ALU.mult, ALU.mult))
                link(dve.scalar_tensor_tensor(lsig[:, :], lsig[:, :], 0.0, p, ALU.min, ALU.subtract))
                dve.tensor_scalar(nlsig[:, :], lsig[:, 4:8], -1.0, None, ALU.mult).then_inc(lsig_ready, 1)

            def residual(p0, o0, gate, m):
                for o in range(KC):
                    dve.wait_ge(panel_done, done(p0 + o))
                    dve.wait_ge(down_evac, o0 + o + 1)
                    dst = x_lat[:, o * LAT:(o + 1) * LAT]
                    if gate is None:
                        ins = dve.tensor_tensor(dst, bank(2 * (o % RING)), dst, ALU.add)
                    else:
                        ins = dve.scalar_tensor_tensor(dst, bank(2 * (o % RING)), gates[:, gate * KC + o:gate * KC + o + 1], dst, ALU.mult, ALU.add)
                    ins.then_inc(down_evac, 1)
                    if o:
                        add_squares(m, o)

            def head_centre(j):
                dve.wait_ge(mean_ready, j + 1)
                dve.scalar_tensor_tensor(o_sb[:, :], bank(3), -float(D // P), o_sb[:, :], ALU.mult, ALU.add).then_inc(o_centred, 1)
                dve.wait_ge(o_centred, j + 1)

            def head_norm(j, w, gate):
                dve.wait_ge(oroot_ready, j + 1)
                link(dve.reciprocal(o_sq[:, :], o_sq[:, :]))
                link(dve.scalar_tensor_tensor(o_sb[:, :], o_sb[:, :], w, o_sq[:, :], ALU.mult, ALU.mult))
                dve.tensor_tensor(gate if j < HEADS else o_sb[:, :], o_sb[:, :], gate, ALU.mult).then_inc(o_scaled, 1)
                dve.wait_ge(o_scaled, j + 1)

            def head_lo(j):
                dve.wait_ge(ohi_done, j + 1)
                sl = slice(j * LAT, (j + 1) * LAT)
                src = rg[:, sl] if j < HEADS else o_sb[:, :]
                dve.tensor_tensor(o_lo[:, sl], src, o_hi[:, sl].bitcast(f32), ALU.subtract).then_inc(mix_ready, 1)

            def input_projection():
                dve.wait_ge(lr_split, 1)
                dve.tensor_tensor(lr_lo[:, :], lr_raw[:, :], lr_hi[:, :].bitcast(f32), ALU.subtract).then_inc(lr_lo_done, 1)
                for n in range(4):
                    d, hp = divmod(n, 2)
                    dve.wait_ge(gate_act, n + 1)
                    dst = (gf, gb)[d][:, hp * TOK:(hp + 1) * TOK]
                    link(dve.scalar_tensor_tensor(dst, gate_y[:, :], 0.0, gate_e[:, :], ALU.min, ALU.subtract))
                    dve.tensor_scalar(dst, dst, 1.0 / 16, None, ALU.mult).then_inc(gate_dve, 1)
                dve.wait_ge(rope_loaded, 16)
                for j in range(8):
                    dve.wait_ge(win_evac, j + 1 if j < 4 else j + 5)
                    dst = rq[:, j * LAT:(j + 1) * LAT] if j < 4 else rk[:, (j - 4) * TOK:(j - 4) * TOK + LAT]
                    if j:
                        dve.wait_ge(rope_done, j)
                    link(dve.stream_shuffle(rope_tmp[:, :], dst, SWAP16))
                    link(dve.tensor_tensor(rope_tmp[:, :], rope_tmp[:, :], rope_cs[:, LAT:2 * LAT], ALU.mult))
                    link(dve.tensor_tensor(dst, dst, rope_cs[:, 0:LAT], ALU.mult))
                    dve.tensor_tensor(dst, dst, rope_tmp[:, :], ALU.add).then_inc(rope_done, 1)

            def retention():
                dve.wait_ge(u_loaded, 16)
                dve.wait_ge(lsig_ready, 1)

                def exponents(j):
                    lg_f, nlg_b = lsig[:, j:j + 1], nlsig[:, j:j + 1]
                    if j:
                        dve.wait_ge(s_evac, 6 * j)
                    dve.tensor_scalar(decay_f[:, 0:UW], u_sb[:, :], 0.0, lg_f, ALU.max, ALU.mult)
                    dve.tensor_scalar(decay_b[:, 0:UW], u_sb[:, :], 0.0, nlg_b, ALU.min, ALU.mult)
                    dve.tensor_scalar(decay_f[:, UW:], u_sb[:, 256:], float(CTX), lg_f, ALU.add, ALU.mult)
                    dve.tensor_scalar(decay_b[:, UW:], u_sb[:, 256:], -float(LAT), nlg_b, ALU.add, ALU.mult).then_inc(arg_ready, 1)

                def decays_of(j):
                    dve.wait_ge(exp_ready, j + 1)
                    dve.scalar_tensor_tensor(decay_f[:, 0:UW], u_sb[:, :], 0.0, decay_f[:, 0:UW], ALU.is_ge, ALU.mult)
                    link(dve.scalar_tensor_tensor(decay_b[:, 0:UW], u_sb[:, :], 0.0, decay_b[:, 0:UW], ALU.is_le, ALU.mult))
                    link(dve.tensor_tensor(decay_f[:, :], decay_f[:, :], decay_b[:, :], ALU.add))

                exponents(0)
                decays_of(0)
                for j in range(HEADS):
                    for t in range(TILES):
                        n = j * TILES + t
                        dve.wait_ge(s_ready, n + 1)
                        if n >= 2:
                            dve.wait_ge(pv_done, n - 1)
                        c = 384 - P * t if t < LT else UW + P - P * (t - LT)
                        dve.tensor_tensor(s_ring[n % 2][:, :], bank(n % 2), decay_f[:, c:c + LAT], ALU.mult)\
                            .then_inc(s_evac, 1)
                    if j + 1 < HEADS:
                        exponents(j + 1)
                        decays_of(j + 1)
                    head_centre(j)
                    head_norm(j, vcol("ret_norm_w", j), rg[:, j * LAT:(j + 1) * LAT])
                for j in range(HEADS):
                    head_lo(j)

            def gla():
                dve.wait_ge(masks_loaded, 32)
                dve.wait_ge(win_evac, len(WIN))
                dve.wait_ge(mix_ready, HEADS)
                zero = zero_t[:, :].to_broadcast([P, LAT])
                C = [cum[:, j * LAT:(j + 1) * LAT] for j in range(4)]
                for hp in range(2):
                    q, k = gq[:, hp * LAT:(hp + 1) * LAT], gk[:, hp * TOK:(hp + 1) * TOK]
                    f, b = gf[:, hp * TOK:(hp + 1) * TOK], gb[:, hp * TOK:(hp + 1) * TOK]
                    if hp:
                        dve.wait_ge(o_ready, HEADS + 2)
                    def scan(dst, src, n):
                        return dve.tensor_tensor_scan(dst, src, zero_t[:, :].to_broadcast([P, n]), 0.0, ALU.add, ALU.add)
                    for t in range(LT):
                        sl = slice(t * P, (t + 1) * P)
                        scan(C[0][:, sl], f[:, sl], P)
                        scan(C[1][:, sl], b[:, sl], P)
                    scan(C[2], f[:, 0:LAT], LAT)
                    scan(C[3], b[:, 0:LAT], LAT)
                    scan(suf[:, ::-1], b[:, 0:LAT][:, ::-1], LAT)
                    kf, kb = ctx_k[:, 0:CTX], ctx_k[:, CTX:2 * CTX]
                    scan(kf[:, ::-1], f[:, LAT:TOK][:, ::-1], CTX)
                    link(scan(kb, b[:, LAT:TOK], CTX))
                    dve.tensor_tensor(C[1], C[1], b[:, 0:LAT], ALU.subtract)
                    dve.tensor_tensor(C[3], C[3], b[:, 0:LAT], ALU.subtract)
                    dve.tensor_tensor(kf, kf, f[:, LAT:TOK], ALU.subtract)
                    dve.tensor_tensor(kb, kb, b[:, LAT:TOK], ALU.subtract).then_inc(ctx_arg, 1)
                    dve.wait_ge(ctx_arg, hp + 1)
                    dve.wait_ge(ctx_exp, hp + 1)
                    link(dve.tensor_tensor(kf, kf, k[:, LAT:TOK], ALU.mult))
                    link(dve.tensor_tensor(kb, kb, k[:, LAT:TOK], ALU.mult))

                    def distances(u):
                        n = hp * (UNITS - 1) + u
                        if n > 2:
                            dve.wait_ge(qk_ready, hp * UNITS + u - 1 if u > 2 else hp * UNITS)
                        o = (u % 2) * 2 * LAT
                        if u == UNITS - 1:
                            dve.tensor_copy(d_lv[:, o:o + LAT], C[2])
                            dve.tensor_copy(d_lv[:, o + LAT:o + 2 * LAT], suf[:, :]).then_inc(d_ready, 1)
                            return
                        h = 2 ** (u - 1)
                        for d in range(2):
                            src = C[d if h < P else 2 + d].rearrange("p (n h) -> p n h", h=2 * h)
                            ref = src[:, :, h - 1 + d:h + d].broadcast_to([P, LAT // (2 * h), 2 * h])
                            dst = d_lv[:, o + d * LAT:o + (d + 1) * LAT].rearrange("p (n h) -> p n h", h=2 * h)
                            ins = dve.tensor_tensor(dst, src, ref, ALU.subtract)
                        ins.then_inc(d_ready, 1)

                    def scaled(u):
                        m = hp * UNITS + u
                        dve.wait_ge(x_ready, hp * (UNITS - 1) + u)
                        if m >= 2:
                            dve.wait_ge(unit_ready, m - 1)
                        o = (u % 2) * LAT
                        ql, kl = q_lv[:, o:o + LAT], k_lv[:, o:o + LAT]
                        xf, xb = d_lv[:, 2 * o:2 * o + LAT], d_lv[:, 2 * o + LAT:2 * o + 2 * LAT]
                        if u == UNITS - 1:
                            dve.tensor_tensor(ql, q, xf, ALU.mult)
                            dve.tensor_tensor(kl, q, xb, ALU.mult).then_inc(qk_ready, 1)
                            return
                        h = 2 ** (u - 1)
                        v = lambda a: a.rearrange("p (n t h) -> p n t h", t=2, h=h)
                        kk = k[:, 0:LAT]
                        dve.tensor_tensor(v(ql)[:, :, 0], v(q)[:, :, 0], v(xb)[:, :, 0], ALU.mult)
                        dve.tensor_tensor(v(ql)[:, :, 1], v(q)[:, :, 1], v(xf)[:, :, 1], ALU.mult)
                        dve.tensor_tensor(v(kl)[:, :, 0], v(kk)[:, :, 0], v(xf)[:, :, 0], ALU.mult)
                        dve.tensor_tensor(v(kl)[:, :, 1], v(kk)[:, :, 1], v(xb)[:, :, 1], ALU.mult).then_inc(qk_ready, 1)

                    def masked(u):
                        dve.wait_ge(unit_ready, hp * UNITS + u + 1)
                        if u:
                            dve.wait_ge(unit_dve, hp * (len(LEVELS) + 1) + u)
                        for a in range(2):
                            c0 = a * TILES * LAT
                            diagonal = [s_gla[:, c0 + t * (LAT + P):c0 + t * (LAT + P) + P] for t in range(LT)]
                            for t in range(LT):
                                src = bank(unit_bank(u, a), P, t * P)
                                if u == 0:
                                    ins = dve.tensor_tensor(diagonal[t], src, diag2_sb[:, :], ALU.mult)
                                else:
                                    ins = dve.copy_predicated(diagonal[t], masks[:, (u - 1) * P:u * P], src)
                        ins.then_inc(unit_dve, 1)

                    dve.tensor_copy(q_lv[:, 0:LAT], q)
                    dve.tensor_copy(k_lv[:, 0:LAT], k[:, 0:LAT]).then_inc(qk_ready, 1)
                    distances(1)
                    for u in range(1, UNITS):
                        if u + 1 < UNITS:
                            distances(u + 1)
                        scaled(u)
                        if u - 1 <= len(LEVELS):
                            masked(u - 1)
                    for a in range(2):
                        j = 2 * hp + a
                        head_norm(HEADS + j, vcol("gla_norm_w", j), gg[:, j * LAT:(j + 1) * LAT])
                        head_lo(HEADS + j)

            def input_projection2():
                dve.wait_ge(pos_loaded, 16)
                link(dve.tensor_copy(angle[:, :], pos_i[:, :]))
                link(dve.tensor_scalar(angle[:, :], angle[:, :], rope_pp[:, 0:1], None, ALU.mult))
                link(dve.tensor_scalar(turns[:, :], angle[:, :], 1.0 / (2 * math.pi), ROUND, ALU.mult, ALU.add))
                link(dve.tensor_scalar(turns[:, :], turns[:, :], ROUND, None, ALU.subtract))
                for part in TWO_PI:
                    link(dve.scalar_tensor_tensor(angle[:, :], turns[:, :], -part, angle[:, :], ALU.mult, ALU.add))
                cos_a, sin_a = cs2[:, 0:LAT], cs2[:, LAT:2 * LAT]
                link(dve.tensor_scalar(cos_a, angle[:, :], math.pi / 2, None, ALU.add))
                link(dve.tensor_scalar(turns[:, :], cos_a, math.pi, -2 * math.pi, ALU.is_gt, ALU.mult))
                link(dve.tensor_tensor(cos_a, cos_a, turns[:, :], ALU.add))
                link(dve.tensor_copy(sin_a, angle[:, :]))
                dve.tensor_scalar(cs2[:, :], cs2[:, :], PI_IN, -PI_IN, ALU.min, ALU.max).then_inc(cs_arg, 1)
                dve.wait_ge(cs_ready, 1)
                link(dve.tensor_scalar(sin_a, sin_a, rope_pp[:, 1:2], None, ALU.mult))
                rg_convolution()

                def rotate(j):
                    dve.wait_ge(win2_evac, 8 + j + 1)
                    dst = (aq if j < 4 else ak)[:, (j % 4) * LAT:(j % 4 + 1) * LAT]
                    if j:
                        dve.wait_ge(rope2_done, j)
                    link(dve.stream_shuffle(rope_tmp[:, :], dst, SWAP16))
                    link(dve.tensor_tensor(rope_tmp[:, :], rope_tmp[:, :], sin_a, ALU.mult))
                    link(dve.tensor_tensor(dst, dst, cos_a, ALU.mult))
                    dve.tensor_tensor(dst, dst, rope_tmp[:, :], ALU.add).then_inc(rope2_done, 1)

                rg_gated(0)
                rg_scans(0)
                rg_gated(1)
                rg_scans(1)
                for j in range(4):
                    rotate(j)
                rg_gated(2)
                rg_scans(2)
                rotate(4)
                rotate(5)
                rg_gated(3)
                rotate(6)
                rotate(7)
                rg_scans(3)

            def attention(A):
                if A is SELF:
                    dve.wait_ge(bias_loaded, 16)
                scale = float(A["dk"]) ** -0.5
                for n in range(A["n"] + 1):
                    N = A["n0"] + n
                    if n < A["n"]:
                        sl = N % P_BUFS
                        row = prob[:, sl * LAT:sl * LAT + A["keys"]]
                        top = stat[:, sl:sl + 1]
                        dve.wait_ge(a_scores, N + 1)
                        if N >= P_BUFS:
                            dve.wait_ge(a_trans, N - P_BUFS + 1)
                        if A is SELF:
                            it = n % LT
                            link(dve.tensor_tensor_reduce(out=row, in0=bank(n % 2), in1=bias_sb[:, it * LAT:(it + 1) * LAT], scale=1.0,
                                                          scalar=-3e38, op0=ALU.add, op1=ALU.max, accum_out=top))
                        else:
                            dve.tensor_copy(row, bank(n % 2, A["keys"]))
                            link(dve.tensor_reduce(out=top, in_=bank(n % 2, A["keys"]), axis=AX.X, op=ALU.max))
                        dve.tensor_scalar(top, top, -scale, None, ALU.mult).then_inc(a_max, 1)
                    if n >= 1:
                        sl = (N - 1) % P_BUFS
                        row = prob[:, sl * LAT:sl * LAT + A["keys"]]
                        total, inv = stat[:, P_BUFS + sl:P_BUFS + sl + 1], stat[:, 2 * P_BUFS + sl:2 * P_BUFS + sl + 1]
                        dve.wait_ge(a_exp, N)
                        link(dve.reciprocal(inv, total))
                        dve.tensor_scalar(row, row, inv, None, ALU.mult).then_inc(a_prob, 1)
                        hd, it = divmod(n - 1, LT)
                        if it == LT - 1 and (A["dk"] == P or hd % 2):
                            c = hd if A["dk"] == P else hd // 2
                            pending.append(c)
                    while pending and (n == A["n"] or n % LT == 3):
                        c = pending.pop(0)
                        dve.wait_ge(ohi_done, A["s0"] + c + 1)
                        sl = slice(c * LAT, (c + 1) * LAT)
                        dve.tensor_tensor(o_lo[:, sl], bank(4 + c % 2), o_hi[:, sl].bitcast(f32), ALU.subtract).then_inc(mix_ready, 1)

            pending = []

            def rg_convolution():
                link(dve.tensor_scalar(rg_c[:, :], lsig[:, 8:16], -8.0, None, ALU.mult))
                for c in range(4):
                    dve.wait_ge(win2_evac, c + 1)
                    u_in, o = ru[:, c * LAT:(c + 1) * LAT], uc[:, c * LAT:(c + 1) * LAT]
                    w = [vcol("conv_w_2", 4 * k + c) for k in range(4)]
                    link(dve.tensor_scalar(o, u_in, w[2], vcol("conv_b_2", c), ALU.mult, ALU.add))
                    link(dve.scalar_tensor_tensor(o[:, 1:], u_in[:, :LAT - 1], w[1], o[:, 1:], ALU.mult, ALU.add))
                    link(dve.scalar_tensor_tensor(o[:, 2:], u_in[:, :LAT - 2], w[0], o[:, 2:], ALU.mult, ALU.add))
                    dve.scalar_tensor_tensor(o[:, :LAT - 1], u_in[:, 1:], w[3], o[:, :LAT - 1], ALU.mult, ALU.add).then_inc(rg_conv, 1)
                dve.wait_ge(rg_conv, 4)

            def rg_gated(c):
                dve.wait_ge(rg_sig, c + 1)
                for z in range(2):
                    sl = slice(z * LAT, (z + 1) * LAT)
                    dve.tensor_tensor(rg_i[:, sl], rg_i[:, sl], uc[:, c * LAT:(c + 1) * LAT], ALU.mult)
                    ins = dve.tensor_scalar(rg_r[:, sl], rg_r[:, sl], rg_c[:, 4 * z + c:4 * z + c + 1], None, ALU.mult)
                ins.then_inc(rg_la, 1)
                dve.wait_ge(rg_la, c + 1)

            def rg_scans(c):
                dve.wait_ge(rg_exp, c + 1)
                link(dve.tensor_tensor(rg_h[:, :], rg_r[:, :], rg_r[:, :], ALU.mult))
                dve.scalar_tensor_tensor(rg_t[:, :], rg_h[:, :], 1.0, rg_t[:, :], ALU.add, ALU.mult).then_inc(rg_v, 1)
                dve.wait_ge(rg_v, c + 1)
                dve.wait_ge(rg_root, c + 1)
                link(dve.tensor_tensor(rg_i[:, :], rg_i[:, :], rg_t[:, :], ALU.mult))
                dve.tensor_tensor_scan(rg_h[:, 0:LAT], rg_r[:, 0:LAT], rg_i[:, 0:LAT], 0.0, ALU.mult, ALU.add)
                link(dve.tensor_tensor_scan(rg_h[:, LAT:][:, ::-1], rg_r[:, LAT:][:, ::-1], rg_i[:, LAT:][:, ::-1], 0.0, ALU.mult, ALU.add))
                link(dve.tensor_tensor(rg_h[:, 0:LAT], rg_h[:, 0:LAT], rg_h[:, LAT:], ALU.add))
                dve.wait_ge(win2_evac, 4 + c + 1)
                sl = slice(c * LAT, (c + 1) * LAT)
                dve.tensor_tensor(ru[:, sl], rg_h[:, 0:LAT], ry[:, sl], ALU.mult).then_inc(rg_hid, 1)
                dve.wait_ge(rg_hid, c + 1)

            def rg_split():
                for c in range(4):
                    dve.wait_ge(ohi_done, 8 + c + 1)
                    sl = slice((4 + c) * LAT, (5 + c) * LAT)
                    dve.tensor_tensor(o_lo[:, sl], ru[:, c * LAT:(c + 1) * LAT], o_hi[:, sl].bitcast(f32), ALU.subtract).then_inc(mix_ready, 1)

            dve.sem_inc(up_evac, 2)
            dve.sem_inc(g_ready, 2)
            dve.sem_inc(down_evac, KC)
            dve.wait_ge(vec_loaded, 16)
            dve.wait_ge(small_loaded, 80)
            log_sigmoids()
            dve.sem_inc(ada_used, 2 * ADA_PE)
            for kc in range(1, KC):
                add_squares(norms[0], kc)
            dve.wait_ge(cond_ready, 1)
            for k in range(ADA_PE, ADA_FIRST):
                if k == ADA_PE + 2:
                    token_factors(norms[0])
                dve.wait_ge(ada_loaded[k], 16)
                ada_products(k, ada_f[k][:, :], 2, 2 * k)
            dve.wait_ge(ada_used, 2 * ADA_FIRST)
            dve.wait_ge(ada_mods, 2)
            for r in range(2):
                c = r * NMOD * KC
                src = bank(5, 2 * ADA_PE).rearrange("p (k r) -> p k r", r=2)[:, :, r]
                link(dve.tensor_copy(mods[:, c:c + ADA_PE], src))
            add_bias((0, 2), 2)
            norm_scale(0, 0, 1, "norm1_w")
            norm_scale(1, 1, 1, "norm1_w")
            norm(norms[0])
            for G in GROUPS[0:3]:
                hidden_up(G)
                if G["n"] == 0:
                    dve.wait_ge(ada_used, ada_rows(0, ada_before(1)))
                    add_bias((2, 3), 2)
                    for r in range(2):
                        link(dve.tensor_scalar(gates[:, r * KC:(r + 1) * KC], mod(r, 2), 0.5, None, ALU.mult))
                hidden_down(G)
            dve.wait_ge(ada_used, ada_rows(2, ada_before(3)))
            add_bias((3, 9), 1)
            link(dve.tensor_tensor(mods[:, 72 + 24:72 + 40], mods[:, 72 + 24:72 + 40], vcol("ada_b", 24, 16), ALU.add))
            norm_scale(2, 0, 4, "norm2_w")
            norm_scale(3, 1, 4, "norm2_w")
            norm_scale(4, 0, 7, "norm3_w")
            link(dve.tensor_copy(gates[:, 2 * KC:3 * KC], mod(0, 5)))
            link(dve.tensor_scalar(gates[:, 3 * KC:4 * KC], mod(0, 8), 0.5, None, ALU.mult))
            norm(norms[1])
            input_projection()
            retention()
            gla()
            residual(P_WOUT, 3 * KC, 2, norms[2])
            norm(norms[2])
            for G in GROUPS[3:6]:
                hidden_up(G)
                hidden_down(G)
            norm(norms[3])
            norm(norms[4])
            input_projection2()
            rg_split()
            attention(SELF)
            residual(P_WOUT2, 7 * KC, None, norms[5])
            norm(norms[5])
            attention(CROSS)
            for o in range(KC):
                dve.wait_ge(panel_done, done(P_CO + o // 2))
                dve.wait_ge(down_evac, 8 * KC + o + 1)
                dst = x_lat[:, o * LAT:(o + 1) * LAT]
                dve.tensor_tensor(dst, bank(o), dst, ALU.add).then_inc(down_evac, 1)
                if o:
                    add_squares(norms[6], o)
            norm(norms[6])
            for G in GROUPS[6:10]:
                hidden_up(G)
                hidden_down(G)
            norm(norms[7])

        @block.tensor
        def _(pe):
            def product3(out, lhs, rhs, first, last):
                pe.matmul(out, lhs[0], rhs[0], start=first, stop=False)
                pe.matmul(out, lhs[0], rhs[1], start=False, stop=False)
                return pe.matmul(out, lhs[1], rhs[0], start=False, stop=last)

            def panel_product(s, banks, act_hi, act_lo, cols, n_k=KC, ready=None, off=0, at_=h_at):
                for kc in range(n_k):
                    if ready is not None:
                        pe.wait_ge(*ready(kc))
                    w = slice(s * PANEL + (off + kc) * P, s * PANEL + (off + kc + 1) * P)
                    order = ((whi, act_hi), (whi, act_lo), (wlo, act_hi))
                    for j, (wt, a) in enumerate(order):
                        for b, c0, n in cols:
                            ins = pe.matmul(bank(banks + b, n), wt[:, w], a[:, at_(kc, c0):at_(kc, c0) + n],
                                            start=kc == 0 and j == 0, stop=kc == n_k - 1 and j == 2)
                return ins

            def norm(m):
                if m.n == 0:
                    pe.wait_ge(consts, 3)
                pe.wait_ge(sum_done, (m.n + 1) * (KC - 1))
                for t in range(m.T // P):
                    ins = pe.matmul(bank(4, 1, t), act_a[:, t * P:(t + 1) * P], ones_k[:, 0:1], start=True, stop=True)
                ins.then_inc(stats_ready, 1)
                pe.wait_ge(diag_ready, m.n + 1)
                for j, (_, n, c0, _) in enumerate(m.segs()):
                    ins = pe.matmul(bank(6 + j, n), ones_k[:, :], rdiag[:, c0:c0 + n], start=True, stop=True)
                ins.then_inc(rstd_ready, 1)

            def first_modulation(k0, k1):
                pe.wait_ge(condt_ready, 1)
                for k in range(k0, k1):
                    pe.wait_ge(ada_loaded[k], 16)
                    for kc in range(KC):
                        ins = pe.matmul(bank(5, 2, 2 * k), ada_f[k][:, kc * P:(kc + 1) * P], cond_s[:, 2 * kc:2 * kc + 2],
                                        start=kc == 0, stop=kc == KC - 1)
                ins.then_inc(ada_mods, 1)

            def hidden_up(G, h_base):
                cols = token_cols(G["T"])
                per_f = 2 if G["gated"] else 1
                f_per = RING // per_f
                with pe.Fori(0, G["g"] // f_per) as i:
                    for u in range(f_per):
                        pe.wait_ge(up_evac, G["f0"] + i * f_per + u + 1)
                        pe.wait_ge(down_evac, G["o0"] + KC - (2 if u == 0 else 0))
                        for c in range(per_f):
                            s = u * per_f + c
                            pe.wait_ge(lo_done, G["p_up"] + i * RING + s + 1)
                            ready = (lambda kc: (h_ready, h_base + kc + 1)) if G["n"] == 0 and s == 0 else None
                            panel_product(s, 2 * s, h_hi, h_lo, cols, ready=ready).then_inc(panel_done, 1)

            def hidden_down(G):
                cols = token_cols(G["T"])
                f_end = G["f0"] + G["g"] + 2
                with pe.Fori(0, KC // RING) as i:
                    for c in range(RING):
                        pe.wait_ge(up_evac, f_end - (1 if c < 2 else 0))
                        pe.wait_ge(down_evac, G["o0"] + i * RING + c + RING + 1)
                        pe.wait_ge(lo_done, G["p_down"] + i * RING + c + 1)
                        ready = (lambda kc: (g_ready, G["f0"] + 2 + kc + 1)) if c == 0 else None
                        panel_product(c, 2 * c, g_hi, g_lo, cols, n_k=G["g"], ready=ready, at_=hidden_at).then_inc(panel_done, 1)

            def panel_rows(s, k, banks, tiles=TILES, t0=0, first=False, last=False):
                for c in range(2):
                    for t in range(tiles):
                        a = slice(h_at(k + c, (t0 + t) * P), h_at(k + c, (t0 + t) * P) + P)
                        w = slice(s * PANEL + c * 512, s * PANEL + (c + 1) * 512)
                        ins = product3(bank(banks[t]), (h_hi[:, a], h_lo[:, a]), (whi[:, w], wlo[:, w]),
                                       first and c == 0, last and c == 1)
                return ins

            def input_projection():
                last_use = {}
                for n in range(WIN_ALONE):
                    project(n, 2 * (WIN[n][1] % RING), last_use)
                    gate_step(n)

            def gate_step(n):
                if n == 0:
                    pe.wait_ge(lr_lo_done, 1)
                    for t in range(TILES):
                        for kc in range(KC):
                            a, w = slice(h_at(kc, t * P), h_at(kc, t * P) + P), slice(kc * 32, (kc + 1) * 32)
                            ins = product3(bank(7, 32, t * 32), (h_hi[:, a], h_lo[:, a]), (lr_hi[:, w], lr_lo[:, w]), kc == 0, kc == KC - 1)
                    ins.then_inc(lr_pe, 1)
                elif n == 1:
                    pe.wait_ge(lr_act, 1)
                    for d in range(2):
                        for t in range(TILES):
                            b = 1 + 4 * d + 2 * (t // 3)
                            ins = pe.transpose(ps[0:16, b * 512 + (t % 3) * P:b * 512 + (t % 3 + 1) * P],
                                               lr_sb[:, t * 32 + d * 16:t * 32 + d * 16 + 16], ident[:, :])
                    ins.then_inc(lr_pe, 1)
                elif n < 6:
                    d, hp = divmod(n - 2, 2)
                    pe.wait_ge(lr_act, 2)
                    if n >= 4:
                        pe.wait_ge(gate_act, n - 3)
                    for b in range(2):
                        ins = pe.matmul(bank(1 + 4 * hp + 2 * b, HALF), gate_sb[:, d * 256 + hp * P:d * 256 + (hp + 1) * P],
                                        lr_t[d][:, b * HALF:(b + 1) * HALF], start=True, stop=True)
                    ins.then_inc(lr_pe, 1)
                elif n == 7:
                    pe.wait_ge(gate_act, 4)

            def project(n, b0, last_use):
                kind, first, n_p = WIN[n]
                T = TOK if kind in ("rk", "gk") else LAT
                banks = V_BANKS[kind] if kind in V_BANKS else [b0 + b for b, _, _ in token_cols(T)]
                free = max(last_use.get(b, 0) for b in banks)
                if free:
                    pe.wait_ge(win_evac, free)
                for b in banks:
                    last_use[b] = n + 1
                for c in range(n_p):
                    p = P_WIN + first + c
                    pe.wait_ge(lo_done, p + 1)
                    if kind in V_BANKS:
                        panel_rows(p % RING, 2 * c, banks, first=c == 0, last=c == n_p - 1).then_inc(panel_done, 1)
                    else:
                        ready = (lambda kc: (h_ready, H_BEFORE[1] + kc + 1)) if n == 0 else None
                        panel_product(p % RING, b0, h_hi, h_lo, token_cols(T), ready=ready).then_inc(panel_done, 1)

            def head_mean(j):
                pe.wait_ge(o_copied, j + 1)
                pe.matmul(bank(3), ones_k[:, :], o_sb[:, :], start=True, stop=True).then_inc(mean_ready, 1)

            def head_square_mean(j):
                pe.wait_ge(osq_ready, j + 1)
                pe.matmul(bank(4), ones_k[:, :], o_sq[:, :], start=True, stop=True).then_inc(var_ready, 1)

            def retention():
                pe.wait_ge(win_evac, WIN_ALONE)
                pe.wait_ge(rope_done, 8)
                last_use = {}
                for j in range(HEADS):
                    def scores(t):
                        n = j * TILES + t
                        if n >= 2:
                            pe.wait_ge(s_evac, n - 1)
                        pe.matmul(bank(n % 2), rk[:, j * TOK + t * P:j * TOK + (t + 1) * P], rq[:, j * LAT:(j + 1) * LAT],
                                  start=True, stop=True).then_inc(s_ready, 1)

                    def values(t):
                        n = j * TILES + t
                        pe.wait_ge(s_evac, n + 1)
                        v = rv[:, t * 512 + j * P:t * 512 + (j + 1) * P] if t < LT else rv_c[:, (t - LT) * 512 + j * P:(t - LT) * 512 + (j + 1) * P]
                        return pe.matmul(bank(2), v, s_ring[n % 2][:, :], start=t == 0, stop=t == TILES - 1)
                    scores(0)
                    for t in range(1, TILES):
                        scores(t)
                        values(t - 1).then_inc(pv_done, 1)
                    values(TILES - 1).then_inc(pv_done, 1)
                    pe.wait_ge(pv_done, TILES * (j + 1))
                    pe.sem_inc(o_ready, 1)
                    for half, step in enumerate((head_mean, head_square_mean)):
                        if FILL[j][half]:
                            project(FILL[j][half], FILL_BANK, last_use)
                        step(j)

            def gla():
                pe.wait_ge(oroot_ready, HEADS)
                pe.wait_ge(win_evac, len(WIN))
                for hp in range(2):
                    if hp:
                        pe.wait_ge(oroot_ready, HEADS + 2)
                    for u in range(UNITS):
                        m = hp * UNITS + u
                        pe.wait_ge(qk_ready, m + 1)
                        if u >= 2:
                            v = u - 2
                            if v <= len(LEVELS):
                                pe.wait_ge(unit_dve, hp * (len(LEVELS) + 1) + v + 1)
                            else:
                                pe.wait_ge(unit_act, hp * 3 + v - len(LEVELS))
                        o = (u % 2) * LAT
                        for a in range(2):
                            r = slice(64 * a, 64 * a + 64)
                            b = unit_bank(u, a)
                            ql, kl = q_lv[r, o:o + LAT], k_lv[r, o:o + LAT]
                            if u <= len(LEVELS) + 1:
                                for t in range(LT):
                                    i = t if u <= len(LEVELS) else t ^ 1
                                    ins = pe.matmul(bank(b, P, t * P), kl[:, t * P:(t + 1) * P], ql[:, i * P:(i + 1) * P], start=True, stop=True)
                            elif u == UNITS - 2:
                                for t in range(LT):
                                    i = (1 - t // 2) * 256
                                    ins = pe.matmul(bank(b + t // 2, 256, (t % 2) * 256), kl[:, t * P:(t + 1) * P], ql[:, i:i + 256], start=True, stop=True)
                            else:
                                for t in range(2):
                                    for d, qq in enumerate((ql, kl)):
                                        ins = pe.matmul(bank(b + t), ctx_k[r, d * CTX + t * P:d * CTX + (t + 1) * P], qq, start=d == 0, stop=d == 1)
                        ins.then_inc(unit_ready, 1)
                    pe.wait_ge(unit_dve, (hp + 1) * (len(LEVELS) + 1))
                    pe.wait_ge(unit_act, 3 * (hp + 1))
                    for a in range(2):
                        j = 2 * hp + a
                        if a:
                            pe.wait_ge(o_copied, HEADS + j)
                        for t in range(TILES):
                            v = gv[:, t * 512 + j * P:t * 512 + (j + 1) * P] if t < LT else gv_c[:, (t - LT) * 512 + j * P:(t - LT) * 512 + (j + 1) * P]
                            S = s_gla[:, (a * TILES + t) * LAT:(a * TILES + t + 1) * LAT]
                            ins = pe.matmul(bank(2), v, S, start=t == 0, stop=t == TILES - 1)
                        ins.then_inc(o_ready, 1)
                        head_square_mean(HEADS + j)

            def input_projection2():
                last_use = {}
                for n, (kind, first, n_p) in enumerate(WIN2):
                    cols = [(0, LAT, CTX)] if kind == "ck" else token_cols(LAT)
                    b0 = 2 * (first % RING)
                    banks = V_BANKS[kind] if kind in V_BANKS else [b0]
                    free = max(last_use.get(b, 0) for b in banks)
                    if free:
                        pe.wait_ge(win2_evac, free)
                    for b in banks:
                        last_use[b] = n + 1
                    for c in range(n_p):
                        p = P_WIN2 + first + c
                        pe.wait_ge(lo_done, p + 1)
                        if kind in V_BANKS:
                            t0, tiles = (0, LT) if kind == "v" else (LT, 2)
                            panel_rows(p % RING, 2 * c, banks, tiles=tiles, t0=t0, first=c == 0, last=c == n_p - 1)\
                                .then_inc(panel_done, 1)
                        else:
                            ready = (lambda kc: (h_ready, H_BEFORE[4] + kc + 1)) if n == 0 else None
                            panel_product(p % RING, b0, h_hi, h_lo, cols, ready=ready).then_inc(panel_done, 1)
                    if n in RG_AFTER:
                        rg_products(RG_AFTER[n])

            def attention(A):
                if A is SELF:
                    pe.wait_ge(win2_evac, len(WIN2))
                    pe.wait_ge(rope2_done, 8)
                dk, kt = A["dk"], A["keys"] // P
                for n in range(A["n"] + 2):
                    if n < A["n"]:
                        hd, it = divmod(n, LT)
                        j, r = (hd // 2, slice(64 * (hd % 2), 64 * (hd % 2) + 64)) if dk == DH else (hd, slice(0, P))
                        if n >= 2:
                            pe.wait_ge(a_max, A["n0"] + n - 1)
                        pe.matmul(bank(n % 2, A["keys"]), A["q"][r, j * LAT + it * P:j * LAT + (it + 1) * P],
                                  A["k"][r, j * A["keys"]:(j + 1) * A["keys"]], start=True, stop=True).then_inc(a_scores, 1)
                    if n >= 2:
                        m = n - 2
                        hd, it = divmod(m, LT)
                        N = A["n0"] + m
                        pe.wait_ge(a_prob, N + 1)
                        if m >= 2:
                            pe.wait_ge(a_copied, N - 1)
                        for t in range(kt):
                            ins = pe.transpose(bank(2 + m % 2, P, t * P), prob[:, (N % P_BUFS) * LAT + t * P:(N % P_BUFS) * LAT + (t + 1) * P], ident[:, :])
                        ins.then_inc(a_trans, 1)
                        if it == LT - 1:
                            c = hd if dk == P else hd // 2
                            if c >= 2 or A is not SELF:
                                pe.wait_ge(mix_ready, max(A["s0"] + c - 1, A["s0"]))
                            pe.wait_ge(a_copied, N + 1)
                            r = slice(0, P) if dk == P else slice(64 * (hd % 2), 64 * (hd % 2) + 64)
                            o = ps[r, (4 + c % 2) * 512:(5 + c % 2) * 512]
                            for t in range(kt):
                                v = A["v"][:, t * 512 + hd * dk:t * 512 + (hd + 1) * dk]
                                ins = pe.matmul(o, v, prob_t[:, ((hd % 2) * LT + t) * LAT:((hd % 2) * LT + t + 1) * LAT], start=t == 0, stop=t == kt - 1)
                            ins.then_inc(a_values, 1)

            def rg_products(c):
                pe.wait_ge(rg_loaded, 16)
                pe.wait_ge(rg_conv, c + 1)
                if c:
                    pe.wait_ge(rg_sig, c)
                for z in range(2):
                    for g in range(2):
                        w = ((2 * z + g) * 4 + c) * P
                        ins = pe.matmul(bank(1 + 4 * z + 2 * g), rg_sb[:, w:w + P], uc[:, c * LAT:(c + 1) * LAT], start=True, stop=True)
                ins.then_inc(rg_gates, 1)

            def cross_queries():
                for j in range(4):
                    pe.wait_ge(lo_done, P_CQ + j + 1)
                    ready = (lambda kc: (h_ready, H_BEFORE[5] + kc + 1)) if j == 0 else None
                    panel_product(j, 2 * j, h_hi, h_lo, token_cols(LAT), ready=ready).then_inc(panel_done, 1)
                pe.wait_ge(cq_evac, 4)

            def cross_output():
                for c in range(RING):
                    pe.wait_ge(lo_done, P_CO + c + 1)
                    for e in range(2):
                        ready = (lambda kc: (mix_ready, 16 + kc + 1)) if c == 0 and e == 0 else None
                        ins = panel_product(c, 2 * c + e, o_hi, o_lo, token_cols(LAT), n_k=4, ready=ready, off=4 * e, at_=merged_at)
                    ins.then_inc(panel_done, 1)

            def residual(p0, o0, a_hi, a_lo, n_k, ready):
                with pe.Fori(0, KC // RING) as i:
                    for c in range(RING):
                        pe.wait_ge(down_evac, o0 + i * RING + c + RING + 1)
                        pe.wait_ge(lo_done, p0 + i * RING + c + 1)
                        panel_product(c, 2 * c, a_hi, a_lo, token_cols(LAT), n_k=n_k, ready=ready if c == 0 else None,
                                      at_=merged_at).then_inc(panel_done, 1)

            pe.sem_inc(panel_done, RING)
            first_modulation(0, 3)
            norm(norms[0])
            first_modulation(3, ADA_PE)
            for G in GROUPS[0:3]:
                hidden_up(G, 0)
                hidden_down(G)
            norm(norms[1])
            input_projection()
            retention()
            gla()
            residual(P_WOUT, 3 * KC, o_hi, o_lo, KC, lambda kc: (mix_ready, kc + 1))
            norm(norms[2])
            for G in GROUPS[3:6]:
                hidden_up(G, H_BEFORE[2])
                hidden_down(G)
            norm(norms[3])
            norm(norms[4])
            input_projection2()
            attention(SELF)
            residual(P_WOUT2, 7 * KC, o_hi, o_lo, KC, lambda kc: (mix_ready, min(13 + kc, 16)))
            norm(norms[5])
            cross_queries()
            attention(CROSS)
            cross_output()
            norm(norms[6])
            for G in GROUPS[6:10]:
                hidden_up(G, H_BEFORE[6])
                hidden_down(G)
            norm(norms[7])


def rotary_order(parts, n):
    order = []
    for part in range(parts):
        for f in range(0, n, 16):
            order += [part * 2 * n + f + j for j in range(16)] + [part * 2 * n + n + f + j for j in range(16)]
    return order


def shape_tables():
    tok = np.arange(LAT)
    freqs = 10000.0 ** (-np.arange(32) / 32)
    angle = np.zeros((P, LAT))
    sign = np.zeros((P, 1))
    for p, d in enumerate(rotary_order(2, 32)):
        pos = (tok // 64) if d < 64 else (tok % 64)
        angle[p] = pos * np.float32(freqs[d % 32])
        sign[p] = -1.0 if d % 64 < 32 else 1.0
    rope_grid = np.concatenate([np.cos(angle), sign * np.sin(angle)], axis=1)
    p = np.arange(P)[:, None]
    u_tab = np.arange(UW)[None, :] - 384 - p
    i = np.arange(P)[None, :]
    level_masks = np.concatenate([((p // (2 * h) == i // (2 * h)) & (p // h != i // h)) for h in LEVELS], axis=1)
    return {"rope_grid": rope_grid.astype(np.float32), "u_tab": u_tab.astype(np.float32),
            "level_masks": level_masks.astype(np.int32), "diag2": (2.0 * np.eye(P)).astype(np.float32),
            "ident": np.eye(P, dtype=np.float32)}


def window_tables():
    inv_freq = np.float32(10000.0) ** (-np.arange(32, dtype=np.float32) / np.float32(32))
    order = rotary_order(1, 32) * 2
    pp = np.array([[inv_freq[d % 32], -1.0 if d < 32 else 1.0] for d in order], np.float32)
    i, j = np.arange(LAT)[:, None], np.arange(LAT)[None, :]
    times = sum(((i - j) % dil == 0) & (abs(i - j) <= window // 2) for window, dil in ((128, 1), (512, 4), (2048, 16)))
    bias = np.where(times > 0, np.log(np.maximum(times, 1)) * DH ** 0.5, -1e30)
    bias = bias.reshape(LT, P, LAT).transpose(1, 0, 2).reshape(P, LT * LAT)
    return {"rope_pp_h": pp, "window_bias": bias.astype(np.float32)}


def kernel(**inputs):
    import concourse.bacc as bacc
    from concourse.bass_utils import run_bass_kernel_spmd

    def feature_major(a):
        return np.ascontiguousarray(a.reshape(a.shape[0], KC, P).transpose(2, 1, 0).reshape(P, -1))

    def columns(a):
        return a.reshape(-1, P).T

    a = {k: np.asarray(v) for k, v in inputs.items()}
    vecs = np.zeros((P, N_VEC), np.float32)
    for name, n in VEC_WIDTHS.items():
        v = a[name]
        if name == "conv_w_2":
            v = v.reshape(4, 4 * P)
        vecs[:, VEC_AT[name]:VEC_AT[name] + n] = columns(v)
    panels = np.zeros((N_PANELS, P, PANEL), np.float32)
    at = [0]

    def put(w, k0, n_k, c0):
        block = w[k0 * P:(k0 + n_k) * P, c0:c0 + P].reshape(n_k, P, P).transpose(1, 0, 2)
        panels[at[0], :, 0:n_k * P] = block.reshape(P, n_k * P)
        at[0] += 1

    def put_ffn(w1, w3, w2):
        f = 0
        for g in FF_GROUPS:
            for j in range(g):
                put(w1, 0, KC, (f + j) * P)
                put(w3, 0, KC, (f + j) * P)
            for o in range(KC):
                put(w2, f, g, o * P)
            f += g

    def put_rows(w, c0):
        for k in range(0, KC, 2):
            block = w[k * P:(k + 2) * P, c0:c0 + 512].reshape(2, P, 512).transpose(1, 0, 2)
            panels[at[0]] = block.reshape(P, PANEL)
            at[0] += 1

    put_ffn(a["ffn1_w1"][0], a["ffn1_w3"][0], a["ffn1_w2"][0])
    w = a["w_in"][0]
    assert at[0] == P_WIN
    rotated = [w[:, c0:c0 + 512].reshape(D, HEADS, P)[:, :, rotary_order(2, 32)].reshape(D, 512) for c0 in (0, 512)]
    for j in range(HEADS):
        put(rotated[0], 0, KC, j * P)
    for c0 in range(1536, 2048, P):
        put(w, 0, KC, c0)
    for j in range(HEADS):
        put(rotated[1], 0, KC, j * P)
    put_rows(w, 1024)
    put_rows(w, 2560)
    for c0 in (2304, 2304 + P, 2048, 2048 + P, *range(3072, 3584, P)):
        put(w, 0, KC, c0)
    assert at[0] == P_WOUT
    for o in range(KC):
        put(a["w_out"][0], 0, KC, o * P)
    put_ffn(a["ffn2_w1"][0], a["ffn2_w3"][0], a["ffn2_w2"][0])
    assert at[0] == P_WIN2
    w2 = a["w_in_2"][0]
    for c0 in range(1536, 2560, P):
        put(w2, 0, KC, c0)
    for c0 in (0, 512):
        rot = w2[:, c0:c0 + 512].reshape(D, 8, DH)[:, :, rotary_order(1, 32)].reshape(D, 512)
        for j in range(4):
            put(rot, 0, KC, j * P)
    put_rows(w2, 1024)
    for c0 in range(0, 512, P):
        put(a["w_ck_2"][0], 0, KC, c0)
    put_rows(a["w_cv_2"][0], 0)
    assert at[0] == P_WOUT2
    for o in range(KC):
        put(a["w_out_2"][0], 0, KC, o * P)
    for o in range(4):
        put(a["w_cq_2"][0], 0, KC, o * P)
    for o in range(0, KC, 2):
        for e in range(2):
            block = a["w_co_2"][0][:, (o + e) * P:(o + e + 1) * P].reshape(4, P, P).transpose(1, 0, 2)
            panels[at[0], :, e * 512:(e + 1) * 512] = block.reshape(P, 512)
        at[0] += 1
    assert at[0] == P_MLP
    for f in range(0, DFF2 // P, 8):
        for j in range(8):
            put(a["w_mlp_in_2"][0], 0, KC, (f + j) * P)
        for o in range(KC):
            put(a["w_mlp_out_2"][0], f, 8, o * P)
    assert at[0] == N_PANELS
    rg_w = np.zeros((P, 2, 2, 4, P), np.float32)
    for z in range(2):
        for g, name in enumerate(("rg_a_w_2", "rg_x_w_2")):
            for n in range(8):
                r = slice(64 * (n % 2), 64 * (n % 2) + 64)
                rg_w[r, z, g, n // 2, r] = a[name][0, z, n]
    cond = np.concatenate([a["c"][0], a["c_ctx"]])
    ada_p = np.stack([a["ada_w"][0][:, k * P:(k + 1) * P].reshape(KC, P, P).transpose(1, 0, 2).reshape(P, PANEL) for k in range(ADA_PE)])
    arrays = {
        "x_t": feature_major(a["x"][0]),
        "ctx_t": feature_major(a["ctx"][0]),
        "cond": cond,
        "ada_t": np.ascontiguousarray(a["ada_w"][0].T.reshape(NMOD * KC, P, D)),
        "vecs": vecs,
        "panels": panels,
        "lr_w": np.ascontiguousarray(w[:, 3584:3616].reshape(KC, P, 32).transpose(1, 0, 2).reshape(P, KC * 32)),
        "gate_w": np.concatenate([a["gla_gate_w_f"][0], a["gla_gate_w_b"][0]], axis=1),
        "decays": np.concatenate([a["ret_decay_f"][0], a["ret_decay_b"][0]]),
        **shape_tables(),
        "ada_p": ada_p,
        "cond_t": np.ascontiguousarray(cond.reshape(2, KC, P).transpose(2, 1, 0).reshape(P, 2 * KC)),
        "mem_t": feature_major(a["mem_2"][0]),
        "positions": np.ascontiguousarray(a["positions_2"][0]),
        **window_tables(),
        "rg_w": rg_w.reshape(P, 16 * P),
    }
    nc = bacc.Bacc("TRN2", target_bir_lowering=False, num_devices=1)
    args = [nc.dram_tensor(n, v.shape, mybir.dt.from_np(v.dtype), kind="ExternalInput").ap() for n, v in arrays.items()]
    out = nc.dram_tensor("out", (1, P, KC * LAT), mybir.dt.float32, kind="ExternalOutput").ap()
    build(nc, *args, out)
    r = run_bass_kernel_spmd(nc, [arrays], core_ids=[0])
    got = r.results[0]["out"]
    return np.ascontiguousarray(got.reshape(P, KC, LAT).transpose(2, 1, 0).reshape(1, LAT, D))
```

```python
import math
from contextlib import ExitStack

import numpy as np
import concourse.bass as bass
from concourse import mybir

P = 128
D = 1024
KC = D // P
LAT, CTX = 512, 256
TOK = LAT + CTX
HALF = TOK // 2
DFF = 2816
FF = DFF // P
FF_GROUPS = (8, 8, 6)
assert sum(FF_GROUPS) == FF
DFF2 = 4096
NMOD = 9
EPS = 1e-6
RING = 4
PANEL = KC * P
ADA_RING = 3
ADA_FIRST = 18
ADA_PER_PAIR = (3, 6, 6)
ADA_PE = 9
ADA_ROWS = (2, 2, 1)
assert ADA_FIRST + sum(n * g // 2 for n, g in zip(ADA_PER_PAIR, FF_GROUPS)) == NMOD * KC

N_FFN = sum(2 * g + KC for g in FF_GROUPS)
P_FFN1 = 0
P_WIN = P_FFN1 + N_FFN
P_WOUT = P_WIN + 28
P_FFN2 = P_WOUT + 8
P_WIN2 = P_FFN2 + N_FFN
P_WOUT2 = P_WIN2 + 28
P_CQ = P_WOUT2 + 8
P_CO = P_CQ + 4
P_MLP = P_CO + 4
N_PANELS = P_MLP + 2 * DFF2 // P
assert all(p % RING == 0 for p in (P_WIN, P_WOUT, P_FFN2, P_WIN2, P_WOUT2, P_CQ, P_CO, P_MLP, N_PANELS))

VEC_WIDTHS = dict(norm1_w=8, norm2_w=8, norm3_w=8, final_norm_w=8, norm_mix_g_2=8, norm_cross_g_2=8, norm_mem_g_2=8,
                  norm_mlp_g_2=8, norm_final_g_2=8, ada_b=72, ret_norm_w=4, gla_norm_w=4, gla_gate_b_f=2,
                  gla_gate_b_b=2, conv_b_2=4, conv_w_2=16, rg_a_b_2=8, rg_x_b_2=8, rg_lambda_2=8)
VEC_AT, _n = {}, 0
for _k, _w in VEC_WIDTHS.items():
    VEC_AT[_k] = _n
    _n += _w
N_VEC = _n


WIN = [("rq", 0, 1), ("rq", 1, 1), ("rq", 2, 1), ("rq", 3, 1), ("rg", 4, 1), ("rg", 5, 1), ("rg", 6, 1), ("rg", 7, 1),
       ("rk", 8, 1), ("rk", 9, 1), ("rk", 10, 1), ("rk", 11, 1), ("rv", 12, 4), ("gv", 16, 4), ("gk", 20, 1), ("gk", 21, 1),
       ("gq", 22, 1), ("gq", 23, 1), ("gg", 24, 1), ("gg", 25, 1), ("gg", 26, 1), ("gg", 27, 1)]
WIN_ALONE = 18
WIN_CONTEXT = 16
FILL = (18, 19, 20, 21)
WIN2 = [("u", 0, 1), ("u", 1, 1), ("u", 2, 1), ("u", 3, 1), ("y", 4, 1), ("y", 5, 1), ("y", 6, 1), ("y", 7, 1),
        ("q", 8, 1), ("q", 9, 1), ("q", 10, 1), ("q", 11, 1), ("k", 12, 1), ("k", 13, 1), ("k", 14, 1), ("k", 15, 1), ("v", 16, 4),
        ("ck", 20, 1), ("ck", 21, 1), ("ck", 22, 1), ("ck", 23, 1), ("cv", 24, 4)]
RG_AFTER = {5: 0, 8: 1, 11: 2, 14: 3}
DH = 64
P_BUFS = 4
LAG = 3
SCORE_BANKS = (0, 1, 6, 7)
TWO_PI = (6.28125, round((2 * math.pi - 6.28125) * 2 ** 21) / 2 ** 21, 2 * math.pi - 6.28125 - round((2 * math.pi - 6.28125) * 2 ** 21) / 2 ** 21)
PI_IN = 3.1415925
ROUND = 1.5 * 2 ** 23
TILES = TOK // P
LT = LAT // P
HEADS = 4
LR_COLS = 48
UW = 896
LEVELS = (1, 2, 4, 8, 16, 32, 64)
MASKED = len(LEVELS)
TOP = MASKED + 2
UNITS = TOP + 2
assert 2 ** TOP == LAT
SWAP16 = [(i + 16) % 32 for i in range(32)]


def build(nc, x_t, ctx_t, cond, ada_t, vecs, panels, lr_w, gate_w, decays, rope_grid, u_tab, level_masks, diag2, ident_h,
          ada_p, cond_t, mem_t, positions, rope_pp_h, window_bias, rg_w, out):
    f32, f32r, bf16, i32 = mybir.dt.float32, mybir.dt.float32r, mybir.dt.bfloat16, mybir.dt.int32
    ACT, ALU, AX = mybir.ActivationFunctionType, mybir.AluOpType, mybir.AxisListType
    ds = bass.ds

    with ExitStack() as stack:
        KB = 1024
        origin = -(-nc.sbuf_base // 64) * 64

        def at(name, cols, offset, dt=f32, rows=P):
            return nc.alloc_sbuf_tensor_at(name, [rows, cols], dt, offset=origin + offset)

        R_RAW, R_HI, R_LO, R_XL, R_XC, R_H, R_G = 0, 16 * KB, 32 * KB, 48 * KB, 64 * KB, 72 * KB, 120 * KB
        R_TMP, R_ADA, R_VEC = 168 * KB, 180 * KB, 202 * KB

        raw = at("raw", RING * PANEL, R_RAW)
        whi = at("whi", RING * PANEL, R_HI, f32r)
        wlo = at("wlo", RING * PANEL, R_LO, f32r)
        x_lat = at("x_lat", KC * LAT, R_XL)
        x_ctx = at("x_ctx", KC * CTX, R_XC)
        h_hi = at("h_hi", KC * TOK, R_H, f32r)
        h_lo = at("h_lo", KC * TOK, R_H + 24 * KB, f32r)
        g_hi = at("g_hi", KC * TOK, R_G, f32r)
        g_lo = at("g_lo", KC * TOK, R_G + 24 * KB, f32r)
        rdiag = at("rdiag", TOK, R_G)
        rdiag_x = at("rdiag_x", LAT, R_G + 3 * KB)
        act_a = at("act_a", 2 * TOK, R_TMP)
        prod = at("prod", 2 * TOK, R_TMP + 6 * KB)
        ada_f = [at(f"ada_f{k}", PANEL, R_H + 4 * k * KB if k < 12 else R_G + (24 + 4 * (k - 12)) * KB) for k in range(ADA_FIRST)]
        ada_w = at("ada_w", ADA_RING * D, R_ADA)
        cond_b = at("cond_b", 2 * D, R_ADA + 12 * KB)
        cond_s = at("cond_s", 2 * KC, R_TMP + 10 * KB)
        ada_prod = at("ada_prod", D, R_ADA + 20 * KB, bf16)
        vec = at("vec", N_VEC, R_VEC)
        mods = at("mods", 2 * NMOD * KC, R_VEC + 800)
        scales = at("scales", 5 * KC, R_VEC + 1408)
        gates = at("gates", 4 * KC, R_VEC + 1664)
        eps_zero = at("eps_zero", 2, R_VEC + 1792)
        eps_t, zero_t = eps_zero[:, 0:1], eps_zero[:, 1:2]
        head_rms = at("head_rms", 2 * LT, R_VEC + 2336)
        rms = at("rms", LT + TILES, R_VEC + 5952)
        ones_k = at("ones_k", P, R_VEC + 1824)

        lr_raw = at("lr_raw", KC * LR_COLS, R_VEC + 2368)
        gate_sb = at("gate_sb", 256, R_VEC + 3904, rows=LR_COLS)
        ident = at("ident", P, R_VEC + 5440)
        rq = at("rq", HEADS * LAT, R_G)
        rk = at("rk", HEADS * TOK, R_G + 8 * KB)
        rg = at("rg", HEADS * LAT, R_G + 20 * KB)
        gg = at("gg", HEADS * LAT, R_G + 28 * KB)
        gf = at("gf", 2 * TOK, R_G + 36 * KB)
        gb = at("gb", 2 * TOK, R_G + 42 * KB)
        rv = at("rv", LT * 512, R_ADA)
        gv = at("gv", LT * 512, R_ADA + 8 * KB)
        gq = at("gq", 2 * LAT, R_ADA + 16 * KB)
        rv_c = at("rv_c", 2 * 512, R_XC)
        gv_c = at("gv_c", 2 * 512, R_XC + 4 * KB)
        gk = at("gk", 2 * TOK, R_TMP)
        rope_tmp = at("rope_tmp", LAT, R_TMP + 6 * KB)
        rope_cs = at("rope_cs", 2 * LAT, R_TMP + 8 * KB)
        lr_hi = at("lr_hi", KC * LR_COLS, R_ADA, f32r)
        lr_lo = at("lr_lo", KC * LR_COLS, R_ADA + 2 * KB, f32r)
        lr_t = at("lr_t", TOK, R_ADA + 4 * KB, rows=LR_COLS)
        gate_y = at("gate_y", TOK, R_ADA + 9 * KB)
        gate_e = at("gate_e", TOK, R_ADA + 12 * KB)
        o_hi = at("o_hi", KC * LAT, R_H, f32r)
        o_lo = at("o_lo", KC * LAT, R_H + 16 * KB, f32r)
        decay_f = at("decay_f", UW + 640, R_H + 16 * KB)
        decay_b = at("decay_b", UW + 640, R_H + 40 * KB)
        s_ring = [at(f"s_ring{b}", LAT, R_H + (22 + 24 * b) * KB) for b in range(2)]
        u_sb = at("u_sb", UW, R_TMP + 8 * KB)
        o_sb = at("o_sb", LAT, R_TMP + 6 * KB)
        o_sq = at("o_sq", LAT, R_ADA + 20 * KB)
        o_pair = [o_sb, at("o_pair1", LAT, R_TMP + 10 * KB)]
        f_pair = [o_sq, at("f_pair1", LAT, R_ADA + 16 * KB)]
        s_gla = at("s_gla", 2 * TILES * LAT, R_G)
        ctx_k = [at(f"ctx_k{hp}", 2 * CTX, R_G + (12 + 12 * hp) * KB) for hp in range(2)]
        q_lv = at("q_lv", 2 * LAT, R_ADA)
        k_lv = at("k_lv", 2 * LAT, R_ADA + 4 * KB)
        d_lv = at("d_lv", 4 * LAT, R_H + 32 * KB)
        cum = at("cum", 4 * LAT, R_H + 40 * KB)
        suf = at("suf", LAT, R_TMP + 8 * KB)
        masks = at("masks", 7 * P, R_XC, i32)
        diag2_sb = at("diag2_sb", P, R_XC + 3584)
        lsig = at("lsig", 16, R_VEC + 1568)
        nlsig = at("nlsig", 4, R_VEC + 1632)
        ls_tmp = at("ls_tmp", 4 * 16, R_TMP + 11 * KB)

        aq = at("aq", 4 * LAT, R_G)
        ak = at("ak", 4 * LAT, R_G + 8 * KB)
        av = at("av", LT * 512, R_G + 16 * KB)
        ru = at("ru", 4 * LAT, R_G + 24 * KB)
        ry = at("ry", 4 * LAT, R_G + 32 * KB)
        ck = at("ck", HEADS * CTX, R_G + 40 * KB)
        cv = at("cv", 2 * 512, R_G + 44 * KB)
        pos_i = at("pos_i", LAT, R_TMP, i32)
        angle = at("angle", LAT, R_TMP + 2 * KB)
        turns = at("turns", LAT, R_TMP + 4 * KB)
        cs2 = at("cs2", 2 * LAT, R_TMP + 8 * KB)
        rope_pp = at("rope_pp", 2, R_VEC + 1376)
        bias_sb = at("bias_sb", LT * LAT, R_ADA)
        prob = at("prob", P_BUFS * LAT, R_ADA + 8 * KB)
        stat = at("stat", 3 * P_BUFS, R_ADA + 16 * KB)
        prob_t = at("prob_t", 2 * LT * LAT, R_H + 32 * KB)
        uc = at("uc", 4 * LAT, R_ADA)
        rg_sb = at("rg_sb", 16 * P, R_ADA + 8 * KB)
        rg_c = at("rg_c", 8, R_ADA + 16 * KB + 64)
        rg_r = at("rg_r", 2 * LAT, R_XC)
        rg_i = at("rg_i", 2 * LAT, R_XC + 4 * KB)
        rg_t = at("rg_t", 2 * LAT, R_ADA + 17 * KB)
        rg_h = at("rg_h", 2 * LAT, R_TMP)

        ps = stack.enter_context(nc.psum_tensor("ps", [P, 8 * 512], f32))

        def bank(b, n=512, c0=0):
            return ps[:, b * 512 + c0:b * 512 + c0 + n]

        sems = {}

        def sem(name):
            sems[name] = stack.enter_context(nc.semaphore(name))
            return sems[name]

        raw_ready = [sem(f"raw_ready{s}") for s in range(RING)]
        hi_done, lo_done, panel_done = sem("hi_done"), sem("lo_done"), sem("panel_done")
        ada_ready = [sem(f"ada_ready{s}") for s in range(ADA_RING)]
        ada_used = sem("ada_used")
        x_loaded, vec_loaded, cond_loaded, consts = sem("x_loaded"), sem("vec_loaded"), sem("cond_loaded"), sem("consts")
        cond_ready = sem("cond_ready")
        ada_loaded = [sem(f"ada_loaded{g}") for g in range(ADA_FIRST)]
        condt_loaded, condt_ready, ada_mods = sem("condt_loaded"), sem("condt_ready"), sem("ada_mods")
        act_chain, dve_chain = sem("act_chain"), sem("dve_chain")
        mods_ready = sem("mods_ready")
        silu_done, up_evac, ghi_done, g_ready, down_evac = (sem(n) for n in ("silu_done", "up_evac", "ghi_done", "g_ready", "down_evac"))
        sq_ready, sum_done, stats_ready, root_ready, diag_ready, rstd_ready, xn_ready, hhi_done, h_ready = (
            sem(n) for n in ("sq_ready", "sum_done", "stats_ready", "root_ready", "diag_ready", "rstd_ready", "xn_ready", "hhi_done",
                             "h_ready"))
        out_done = sem("out_done")
        small_loaded = sem("small_loaded")
        mem_loaded, pos_loaded, win2_evac, cs_arg, cs_ready, rope2_done, bias_loaded, rg_loaded, cq_evac = (
            sem(n) for n in ("mem_loaded", "pos_loaded", "win2_evac", "cs_arg", "cs_ready", "rope2_done", "bias_loaded", "rg_loaded", "cq_evac"))
        a_scores, a_max, a_exp, a_prob, a_trans, a_copied, a_values = (
            sem(n) for n in ("a_scores", "a_max", "a_exp", "a_prob", "a_trans", "a_copied", "a_values"))
        rg_conv, rg_gates, rg_sig, rg_la, rg_exp, rg_v, rg_root, rg_hid = (
            sem(n) for n in ("rg_conv", "rg_gates", "rg_sig", "rg_la", "rg_exp", "rg_v", "rg_root", "rg_hid"))
        ls_exp, lsig_ready = sem("ls_exp"), sem("lsig_ready")
        lr_lo_done = sem("lr_lo_done")
        lr_split, lr_pe, lr_act, gate_act, gate_dve = (sem(n) for n in ("lr_split", "lr_pe", "lr_act", "gate_act", "gate_dve"))
        win_evac, rope_loaded, rope_done, u_loaded, masks_loaded = (
            sem(n) for n in ("win_evac", "rope_loaded", "rope_done", "u_loaded", "masks_loaded"))
        arg_ready, exp_ready, s_ready, s_evac, pv_done = (sem(n) for n in ("arg_ready", "exp_ready", "s_ready", "s_evac", "pv_done"))
        o_ready, o_copied, mean_ready, o_centred, osq_ready, var_ready, oroot_ready, o_scaled, ohi_done, mix_ready = (
            sem(n) for n in ("o_ready", "o_copied", "mean_ready", "o_centred", "osq_ready", "var_ready", "oroot_ready",
                             "o_scaled", "ohi_done", "mix_ready"))
        means_ready = sem("means_ready")
        cum_ready, hdiag_ready, spread_ready = sem("cum_ready"), sem("hdiag_ready"), sem("spread_ready")
        d_ready, x_ready, qk_ready, unit_ready, unit_dve, unit_act, ctx_arg, ctx_exp = (
            sem(n) for n in ("d_ready", "x_ready", "qk_ready", "unit_ready", "unit_dve", "unit_act", "ctx_arg", "ctx_exp"))
        block = stack.enter_context(nc.Block())

        def done(p):
            return p + RING + 1

        def token_cols(T):
            return [(0, 0, LAT), (1, LAT, CTX)] if T == TOK else [(0, 0, T)]

        def h_at(kc, token):
            return kc * LAT + token if token < LAT else KC * LAT + kc * CTX + token - LAT

        def merged_at(kc, token):
            return kc * LAT + token

        def hidden_at(kc, token):
            return kc * TOK + token

        def vcol(name, j=0, n=1):
            return vec[:, VEC_AT[name] + j:VEC_AT[name] + j + n]

        def mod(row, part):
            c = (row * NMOD + part) * KC
            return mods[:, c:c + KC]

        class Norm:
            def __init__(self, n, T, A, B, last=False):
                self.n, self.T, self.A, self.B, self.last = n, T, A, B, last
                self.xn0 = (3 if n == 4 else n) * KC

            def segs(self):
                s = [(x_lat, LAT, 0, 0)]
                return s + [(x_ctx, CTX, LAT, 1)] if self.T == TOK else s

        def sc(j):
            return lambda kc: scales[:, j * KC + kc:j * KC + kc + 1]

        def md(row, part):
            return lambda kc: mods[:, (row * NMOD + part) * KC + kc:(row * NMOD + part) * KC + kc + 1]

        def vc(name):
            return lambda kc: vcol(name, kc)

        norms = [Norm(0, TOK, (sc(0), sc(1)), (md(0, 0), md(1, 0))),
                 Norm(1, TOK, (sc(2), sc(3)), (md(0, 3), md(1, 3))),
                 Norm(2, LAT, (sc(4),), (md(0, 6),)),
                 Norm(3, LAT, (vc("final_norm_w"),), None, True),
                 Norm(4, TOK, (sc(0), vc("norm_mem_g_2")), None),
                 Norm(5, LAT, (vc("norm_cross_g_2"),), None),
                 Norm(6, LAT, (vc("norm_mlp_g_2"),), None),
                 Norm(7, LAT, (vc("norm_final_g_2"),), None, True)]
        H_BEFORE = [sum(8 for m in norms[:n] if not m.last) for n in range(9)]

        def hidden_groups():
            f, rows = 0, []
            for layer, (p0, T, sizes, gated) in enumerate(((P_FFN1, TOK, FF_GROUPS, True), (P_FFN2, LAT, FF_GROUPS, True),
                                                        (P_MLP, LAT, (8,) * 4, False))):
                p, o = p0, (0, 4 * KC, 9 * KC)[layer]
                for n, g in enumerate(sizes):
                    n_up = (2 if gated else 1) * g
                    rows.append(dict(layer=layer, n=n, T=T, g=g, gated=gated, p_up=p, p_down=p + n_up, f0=f, o0=o, last=n == len(sizes) - 1))
                    p += n_up + KC
                    f += g
                    o += KC
            return rows

        GROUPS = hidden_groups()
        squares = [prod[:, 0:TOK], act_a[:, TOK:2 * TOK]]

        def ada_before(n):
            return ADA_FIRST + sum(ADA_PER_PAIR[m] * FF_GROUPS[m] // 2 for m in range(n))

        def ada_rows(n, k):
            k0 = ada_before(n)
            return sum(r * (ada_before(m + 1) - ada_before(m)) for m, r in enumerate(ADA_ROWS[:n])) + 2 * ADA_FIRST + ADA_ROWS[n] * (k - k0)

        def x_final(n):
            return {1: 3, 2: 4, 3: 7, 5: 8, 6: 9, 7: 13}[n] * KC

        def attention_items(heads, q, k, v, dk, keys, n0, p0, s0):
            return dict(heads=heads, q=q, k=k, v=v, dk=dk, keys=keys, n0=n0, h0=p0, s0=s0, n=heads * LT)

        SELF = attention_items(8, aq, ak, av, DH, LAT, 0, 0, 12)
        CROSS = attention_items(HEADS, aq, ck, cv, P, CTX, 8 * LT, 8, 16)

        V_BANKS = {"v": (0, 2, 4, 6), "cv": (0, 2), "rv": (0, 1, 2, 3, 4, 5), "gv": (0, 1, 2, 3, 4, 5)}

        FILL_BANK = 5

        def n_scaled(hp, u):
            return hp * (TOP + 1) + u + 1

        def n_unit(hp, u):
            return hp * UNITS + u + 2

        def unit_bank(u, a):
            return 4 * ((u + 1) % 2) + 2 * a

        def scores_of(a):
            return s_gla[:, a * TILES * LAT:(a + 1) * TILES * LAT].rearrange("p (j i) -> p j i", j=TILES)

        @block.sync
        def _(sp):
            sp.dma_start(vec[:, :], vecs).then_inc(vec_loaded, 16)
            sp.dma_start(cond_s[:, :], cond_t).then_inc(condt_loaded, 16)
            sp.dma_start(cond_b[:, :], cond.partition_broadcast(P)).then_inc(cond_loaded, 16)
            sp.dma_start(lsig[:, 0:8], decays.partition_broadcast(P)).then_inc(small_loaded, 16)
            sp.dma_start(lr_raw[:, :], lr_w).then_inc(small_loaded, 16)
            sp.dma_start(gate_sb[:, :], gate_w).then_inc(small_loaded, 16)
            sp.dma_start(ident[:, :], ident_h).then_inc(small_loaded, 16)
            sp.dma_start(rope_pp[:, :], rope_pp_h).then_inc(small_loaded, 16)
            sp.dma_start(x_lat[:, :], x_t).then_inc(x_loaded, 16)
            sp.dma_start(x_ctx[:, :], ctx_t).then_inc(x_loaded, 16)
            for k in range(ADA_PE):
                sp.dma_start(ada_f[k][:, :], ada_p[k]).then_inc(ada_loaded[k], 16)
                sp.dma_start(ada_f[ADA_PE + k][:, :], ada_t[ADA_PE + k]).then_inc(ada_loaded[ADA_PE + k], 16)
            for s in range(RING):
                sp.dma_start(raw[:, s * PANEL:(s + 1) * PANEL], panels[s]).then_inc(raw_ready[s], 16)
            with sp.Fori(1, N_PANELS // RING) as i:
                for s in range(RING):
                    sp.wait_ge(lo_done, (i - 1) * RING + s + 1)
                    sp.dma_start(raw[:, s * PANEL:(s + 1) * PANEL],
                                 panels[ds(i * RING + s, 1)].rearrange("a p n -> (a p) n")).then_inc(raw_ready[s], 16)
            for kc in range(KC):
                sp.wait_ge(xn_ready, 7 * KC + kc + 1)
                sp.dma_start(out[0, :, kc * LAT:(kc + 1) * LAT], x_lat[:, kc * LAT:(kc + 1) * LAT]).then_inc(out_done, 16)
            sp.wait_ge(out_done, 16 * KC)

        @block.gpsimd
        def _(pool):
            def gla_distances():
                for hp in range(2):
                    pool.wait_ge(cum_ready, hp + 1)
                    for u in range(1, TOP + 1):
                        n = n_scaled(hp, u - 2) if u > 1 else hp * (TOP + 1)
                        if n:
                            pool.wait_ge(qk_ready, n)
                        h = 2 ** (u - 1)
                        for d in range(2):
                            c = (d if h < P else 2 + d) * LAT
                            src = cum[:, c:c + LAT].rearrange("p (n h) -> p n h", h=2 * h)
                            ref = src[:, :, h - 1 + d:h + d].broadcast_to([P, LAT // (2 * h), 2 * h])
                            o = (2 * (u % 2) + d) * LAT
                            ins = pool.tensor_tensor(d_lv[:, o:o + LAT].rearrange("p (n h) -> p n h", h=2 * h), src, ref, ALU.subtract)
                        ins.then_inc(d_ready, 1)

            pool.memset(ones_k[:, :], 1.0 / D).then_inc(consts, 1)
            pool.memset(eps_t, EPS).then_inc(consts, 1)
            pool.memset(zero_t, 0.0).then_inc(consts, 1)
            def low_part(s, p):
                pool.wait_ge(hi_done, p + 1)
                sl = slice(s * PANEL, (s + 1) * PANEL)
                pool.tensor_tensor(wlo[:, sl], raw[:, sl], whi[:, sl].bitcast(f32), ALU.subtract).then_inc(lo_done, 1)

            with pool.Fori(0, P_WOUT // RING) as i:
                for s in range(RING):
                    low_part(s, i * RING + s)
            low_part(0, P_WOUT)
            low_part(1, P_WOUT + 1)
            gla_distances()
            low_part(2, P_WOUT + 2)
            low_part(3, P_WOUT + 3)
            with pool.Fori(P_WOUT // RING + 1, N_PANELS // RING) as i:
                for s in range(RING):
                    low_part(s, i * RING + s)

        @block.scalar
        def _(act):
            chain = [0]

            def link(ins):
                chain[0] += 1
                ins.then_inc(act_chain, 1)
                act.wait_ge(act_chain, chain[0])

            def round_panel(s, turn, p_done=None):
                act.wait_ge(raw_ready[s], turn * 16)
                if p_done is not None:
                    act.wait_ge(panel_done, done(p_done))
                sl = slice(s * PANEL, (s + 1) * PANEL)
                act.activation(whi[:, sl], raw[:, sl], ACT.Copy).then_inc(hi_done, 1)

            def round_ahead(p0, i, c):
                q = p0 + c + 2
                round_panel(q % RING, i + (q // RING + 1), i * RING + (q - RING))

            def square(m, kc):
                if m.n == 0:
                    act.wait_ge(x_loaded, 32)
                else:
                    act.wait_ge(down_evac, x_final(m.n) + kc + 1)
                if kc >= 3:
                    act.wait_ge(sum_done, m.n * (KC - 1) + kc - 2)
                buf = act_a[:, 0:TOK] if kc == 0 else squares[kc % 2]
                for xs, n, c0, _ in m.segs():
                    ins = act.activation(buf[:, c0:c0 + n], xs[:, kc * n:(kc + 1) * n], ACT.Square)
                ins.then_inc(sq_ready, 1)

            def square_both(kc):
                act.wait_ge(down_evac, x_final(3) + kc + 1)
                if kc == 0:
                    act.wait_ge(mem_loaded, 16)
                if kc >= 2:
                    act.wait_ge(sum_done, 3 * (KC - 1) + 2 * (kc - 1))
                x, mem = x_lat[:, kc * LAT:(kc + 1) * LAT], x_ctx[:, kc * CTX:(kc + 1) * CTX]
                plain, scaled = (act_a[:, 0:TOK], prod[:, TOK:2 * TOK]) if kc == 0 else squares
                act.activation(plain[:, 0:LAT], x, ACT.Square).then_inc(sq_ready, 1)
                act.activation(scaled[:, 0:LAT], x, ACT.Square, scale=vcol("final_norm_w", kc))
                act.activation(scaled[:, LAT:TOK], mem, ACT.Square).then_inc(sq_ready, 1)

            def norm(m):
                if m.n == 4:
                    act.wait_ge(means_ready, 1)
                    act.activation(rms[:, :], rms[:, :], ACT.Sqrt).then_inc(root_ready, 2)
                else:
                    act.wait_ge(stats_ready, m.n + 1)
                    act.activation(rms[:, 0:m.T // P], bank(4, m.T // P), ACT.Sqrt, bias=eps_t).then_inc(root_ready, 1)
                if m.n == 0:
                    round_panel(0, 1)
                    round_panel(1, 1)
                if m.last:
                    return
                for kc in range(KC):
                    act.wait_ge(xn_ready, m.xn0 + kc + 1)
                    b = (kc % 2) * TOK
                    for j, (_, n, c0, _) in enumerate(m.segs()):
                        o = h_hi[:, h_at(kc, c0):h_at(kc, c0) + n]
                        if m.B is None:
                            ins = act.activation(o, prod[:, b + c0:b + c0 + n], ACT.Copy)
                        else:
                            ins = act.activation(o, prod[:, b + c0:b + c0 + n], ACT.Identity, bias=m.B[j](kc))
                    ins.then_inc(hhi_done, 1)

            def hidden_up(G):
                T, cols = G["T"], token_cols(G["T"])
                per_f = 2 if G["gated"] else 1
                f_per = RING // per_f
                with act.Fori(0, G["g"] // f_per) as i:
                    for u in range(f_per):
                        if G["layer"] == 0 and (u == 0 or ADA_PER_PAIR[G["n"]] == 6):
                            for j in range(ADA_RING):
                                k = ada_before(G["n"]) + i * ADA_PER_PAIR[G["n"]] + u * ADA_RING + j
                                act.wait_ge(ada_used, ada_rows(G["n"], k - ADA_RING + 1))
                                act.dma_start(ada_w[:, j * D:(j + 1) * D],
                                              ada_t[ds(k, 1)].rearrange("a p n -> (a p) n")).then_inc(ada_ready[j], 16)
                        for c in range(per_f):
                            round_ahead(G["p_up"], i, u * per_f + c)
                        f = G["f0"] + i * f_per + u
                        b = (u % 2) * TOK
                        act.wait_ge(panel_done, done(G["p_up"] + i * RING + u * per_f))
                        act.wait_ge(up_evac, f + 1)
                        b0 = 2 * u * per_f
                        src, dst = bank(b0, T), act_a[:, b:b + T]
                        act.activation(dst, src, ACT.Silu if G["gated"] else ACT.Relu).then_inc(silu_done, 1)
                        act.wait_ge(up_evac, f + 3)
                        fo = (i * f_per + u) * TOK
                        act.activation(g_hi[:, ds(fo, T)], prod[:, b:b + T], ACT.Copy).then_inc(ghi_done, 1)

            def hidden_down(G):
                if G["last"]:
                    outputs_and_squares(G["p_down"], norms[(1, 3, 7)[G["layer"]]])
                    return
                with act.Fori(0, KC // RING) as i:
                    for c in range(RING):
                        round_ahead(G["p_down"], i, c)

            def outputs_and_squares(p0, m):
                def follow(o):
                    square_both(o) if m.n == 3 else square(m, o)

                for o in range(KC):
                    q = p0 + o + 2
                    if q < N_PANELS:
                        round_panel(q % RING, q // RING + 1, q - RING)
                    if o >= 2:
                        follow(o - 2)
                follow(KC - 2)
                follow(KC - 1)

            def head_out(j):
                act.wait_ge(o_ready, j + 1)
                if j:
                    act.wait_ge(o_scaled, j)
                act.activation(o_sb[:, :], bank(2), ACT.Copy).then_inc(o_copied, 1)

            def head_squares(j):
                act.wait_ge(o_centred, j + 1)
                act.activation(o_sq[:, :], o_sb[:, :], ACT.Square).then_inc(osq_ready, 1)

            def head_root(j):
                act.wait_ge(var_ready, j + 1)
                act.activation(o_sq[:, :], bank(4), ACT.Sqrt, bias=eps_t, scale=float(D // P)).then_inc(oroot_ready, 1)

            def head_hi(j):
                act.wait_ge(o_scaled, j + 1)
                act.wait_ge(pv_done, 6 * HEADS)
                act.wait_ge(panel_done, done(P_WOUT - 1))
                src = rg[:, j * LAT:(j + 1) * LAT]
                act.activation(o_hi[:, j * LAT:(j + 1) * LAT], src, ACT.Copy).then_inc(ohi_done, 1)

            def gate_step(n):
                if n == 0:
                    act.wait_ge(lr_pe, 1)
                    for b, c0, nn in token_cols(TOK):
                        ins = act.activation(lr_t[:, c0:c0 + nn], ps[0:LR_COLS, (5 + 2 * b) * 512:(5 + 2 * b) * 512 + nn], ACT.Copy)
                    ins.then_inc(lr_act, 1)
                elif 2 <= n < 6:
                    d, hp = divmod(n - 2, 2)
                    act.wait_ge(lr_pe, n)
                    if n > 2:
                        act.wait_ge(gate_dve, n - 2)
                    for b in range(2):
                        ins = act.activation(gate_y[:, b * HALF:(b + 1) * HALF], bank(1 + 4 * hp + 2 * b, HALF), ACT.Identity,
                                             bias=vcol(("gla_gate_b_f", "gla_gate_b_b")[d], hp))
                    link(ins)
                    link(act.activation(gate_e[:, :], gate_y[:, :], ACT.Abs))
                    link(act.activation(gate_e[:, :], gate_e[:, :], ACT.Exp, scale=-1.0))
                    act.activation(gate_e[:, :], gate_e[:, :], ACT.Ln, bias=1.0).then_inc(gate_act, 1)

            def round_for(p0, p1, first, n_p):
                for q in range(p0 + first + (2 if first == 0 else 3), min(p0 + first + n_p + 3, p1 + 2)):
                    round_panel(q % RING, q // RING + 1, q - RING)

            def projected(n, b):
                kind, first, n_p = WIN[n]
                round_for(P_WIN, P_WOUT, first, n_p)
                act.wait_ge(panel_done, done(P_WIN + first + n_p - 1))
                j = first % 4
                if kind == "rq":
                    act.activation(rq[:, j * LAT:(j + 1) * LAT], bank(b), ACT.Copy, scale=P ** -0.5).then_inc(win_evac, 1)
                elif kind in ("rk", "gk"):
                    j = first - 20 if kind == "gk" else j
                    dst = (rk if kind == "rk" else gk)[:, j * TOK:(j + 1) * TOK]
                    act.activation(dst, bank(b, TOK), ACT.Copy).then_inc(win_evac, 1)
                elif kind == "gq":
                    j = first - 22
                    act.activation(gq[:, j * LAT:(j + 1) * LAT], bank(b), ACT.Copy, scale=64 ** -0.5).then_inc(win_evac, 1)
                elif kind in ("rg", "gg"):
                    dst = (rg if kind == "rg" else gg)[:, j * LAT:(j + 1) * LAT]
                    act.activation(dst, bank(b), ACT.Silu).then_inc(win_evac, 1)
                else:
                    if kind == "rv":
                        act.wait_ge(gate_dve, 4)
                    lat, ctx = (rv, rv_c) if kind == "rv" else (gv, gv_c)
                    for t in range(TILES):
                        dst = lat[:, t * 512:(t + 1) * 512] if t < LT else ctx[:, (t - LT) * 512:(t - LT + 1) * 512]
                        ins = act.activation(dst, bank(V_BANKS[kind][t]), ACT.Copy)
                    ins.then_inc(win_evac, 1)

            def input_projection():
                act.wait_ge(h_ready, H_BEFORE[2])
                act.dma_start(rope_cs[:, :], rope_grid).then_inc(rope_loaded, 16)
                act.wait_ge(small_loaded, 80)
                act.activation(lr_hi[:, :], lr_raw[:, :], ACT.Copy).then_inc(lr_split, 1)
                for n in range(WIN_ALONE):
                    projected(n, 2 * (WIN[n][1] % RING))
                    gate_step(n)
                    if n == WIN_CONTEXT - 1:
                        act.wait_ge(rope_done, 8)
                        act.dma_start(u_sb[:, :], u_tab).then_inc(u_loaded, 16)
                    if n == WIN_CONTEXT:
                        exponentials(0)

            def exponentials(j):
                act.wait_ge(arg_ready, j + 1)
                act.activation(decay_f[:, :], decay_f[:, :], ACT.Exp)
                act.activation(decay_b[:, :], decay_b[:, :], ACT.Exp).then_inc(exp_ready, 1)

            def retention():
                for j in range(HEADS):
                    head_out(j)
                    if j + 1 < HEADS:
                        exponentials(j + 1)
                    projected(FILL[j], FILL_BANK)
                    head_squares(j)
                    head_root(j)
                act.wait_ge(pv_done, 6 * HEADS)
                act.dma_start(masks[:, :], level_masks).then_inc(masks_loaded, 16)
                act.dma_start(diag2_sb[:, :], diag2).then_inc(masks_loaded, 16)
                context_factors(0)
                for j in range(HEADS):
                    head_hi(j)

            def gla():
                for u in range(1, TOP + 1):
                    factors(0, u)
                    unit_copy(0, u)
                context_factors(1)
                pair_out(0)
                for u in range(1, TOP + 1):
                    factors(1, u)
                    unit_copy(1, u)
                    if u == 2:
                        pair_root(0)
                    if u == 6:
                        pair_hi(0)
                pair_out(1)
                pair_root(1)
                pair_hi(1)

            def context_factors(hp):
                act.wait_ge(ctx_arg, hp + 1)
                act.activation(ctx_k[hp][:, :], ctx_k[hp][:, :], ACT.Exp).then_inc(ctx_exp, 1)
                if hp:
                    act.wait_ge(qk_ready, hp * (TOP + 1))
                act.activation(d_lv[:, 0:LAT], cum[:, 2 * LAT:3 * LAT], ACT.Exp)
                act.activation(d_lv[:, LAT:2 * LAT], suf[:, :], ACT.Exp).then_inc(x_ready, 1)

            def factors(hp, u):
                act.wait_ge(d_ready, hp * TOP + u)
                b, h = (u % 2) * 2 * LAT, 2 ** (u - 1)
                v = d_lv[:, b:b + 2 * LAT].rearrange("p (n t h) -> p n t h", t=2, h=h)
                act.activation(v[:, :, 0, :], v[:, :, 0, :], ACT.Exp, scale=-1.0)
                act.activation(v[:, :, 1, :], v[:, :, 1, :], ACT.Exp).then_inc(x_ready, 1)

            def unit_copy(hp, u):
                for m in ((-1,) if u == 2 else (TOP - 1,) if u == TOP else ()) + ((TOP,) if u == TOP else ()):
                    act.wait_ge(unit_ready, n_unit(hp, m))
                    if hp:
                        act.wait_ge(o_ready, HEADS + 2)
                    else:
                        act.wait_ge(mix_ready, HEADS)
                    for a in range(2):
                        S, b = scores_of(a), unit_bank(m, a)
                        if m == -1:
                            ins = act.activation(S[:, LT:TILES, :], ps[:, b * 512:(b + 2) * 512].rearrange("p (j i) -> p j i", j=2), ACT.Copy)
                        elif m == TOP:
                            for half in range(2):
                                ins = act.activation(S[:, 2 * half:2 * half + 2, (1 - half) * 256:(2 - half) * 256],
                                                     bank(b + half).rearrange("p (j i) -> p j i", j=2), ACT.Copy)
                        else:
                            for t in range(LT):
                                o = (t ^ 1) * P
                                ins = act.activation(S[:, t, o:o + P], bank(b, P, t * P), ACT.Copy)
                    ins.then_inc(unit_act, 1)

            def pair_out(hp):
                for a in range(2):
                    act.wait_ge(o_ready, HEADS + 2 * hp + a + 1)
                    if hp:
                        act.wait_ge(mix_ready, HEADS + a + 1)
                    else:
                        act.wait_ge(mix_ready, HEADS)
                    act.activation(o_pair[a][:, :], bank(5 + 2 * a), ACT.Copy).then_inc(o_copied, 1)
                    act.activation(f_pair[a][:, :], bank(5 + 2 * a), ACT.Square).then_inc(osq_ready, 1)

            def pair_root(hp):
                act.wait_ge(var_ready, HEADS + hp + 1)
                act.activation(head_rms[:, :], bank(5, 2 * LT), ACT.Sqrt, bias=eps_t, scale=float(D // P)).then_inc(oroot_ready, 1)

            def pair_hi(hp):
                for a in range(2):
                    j = HEADS + 2 * hp + a
                    act.wait_ge(o_scaled, j + 1)
                    act.activation(o_hi[:, j * LAT:(j + 1) * LAT], o_pair[a][:, :], ACT.Copy).then_inc(ohi_done, 1)

            def input_projection2():
                act.wait_ge(h_ready, H_BEFORE[5])
                act.dma_start(pos_i[:, :], positions.partition_broadcast(P)).then_inc(pos_loaded, 16)
                act.dma_start(rg_sb[:, :], rg_w).then_inc(rg_loaded, 16)
                for n, (kind, first, n_p) in enumerate(WIN2):
                    round_for(P_WIN2, P_WOUT2, first, n_p)
                    act.wait_ge(panel_done, done(P_WIN2 + first + n_p - 1))
                    j = first % 4
                    b = 2 * (first % RING)
                    if kind in ("q", "k", "u"):
                        dst = {"q": aq, "k": ak, "u": ru}[kind]
                        act.activation(dst[:, j * LAT:(j + 1) * LAT], bank(b), ACT.Copy).then_inc(win2_evac, 1)
                    elif kind == "y":
                        act.activation(ry[:, j * LAT:(j + 1) * LAT], bank(b), ACT.Gelu_apprx_tanh).then_inc(win2_evac, 1)
                    elif kind == "ck":
                        act.activation(ck[:, j * CTX:(j + 1) * CTX], bank(b, CTX), ACT.Copy).then_inc(win2_evac, 1)
                    else:
                        dst = av if kind == "v" else cv
                        for t, vb in enumerate(V_BANKS[kind]):
                            ins = act.activation(dst[:, t * 512:(t + 1) * 512], bank(vb), ACT.Copy)
                        ins.then_inc(win2_evac, 1)
                    if n == 1:
                        act.wait_ge(cs_arg, 1)
                        act.activation(cs2[:, :], cs2[:, :], ACT.Sin).then_inc(cs_ready, 1)
                    for step, m in enumerate((n, n - 1, n - 2)):
                        if m in RG_AFTER:
                            rg_step(RG_AFTER[m], step)
                    if kind == "v":
                        act.wait_ge(rg_hid, 4)
                        act.dma_start(bias_sb[:, :], window_bias).then_inc(bias_loaded, 16)

            def rg_step(c, step):
                if step == 0:
                    act.wait_ge(rg_gates, c + 1)
                    if c:
                        act.wait_ge(rg_hid, c)
                    for z in range(2):
                        sl = slice(z * LAT, (z + 1) * LAT)
                        act.activation(rg_r[:, sl], bank(1 + 4 * z), ACT.Sigmoid, bias=vcol("rg_a_b_2", 4 * z + c))
                        ins = act.activation(rg_i[:, sl], bank(3 + 4 * z), ACT.Sigmoid, bias=vcol("rg_x_b_2", 4 * z + c))
                    ins.then_inc(rg_sig, 1)
                elif step == 1:
                    act.wait_ge(rg_la, c + 1)
                    link(act.activation(rg_t[:, :], rg_r[:, :], ACT.Tanh))
                    act.activation(rg_r[:, :], rg_r[:, :], ACT.Exp, scale=-1.0).then_inc(rg_exp, 1)
                else:
                    act.wait_ge(rg_v, c + 1)
                    act.activation(rg_t[:, :], rg_t[:, :], ACT.Sqrt).then_inc(rg_root, 1)

            def rg_split():
                act.wait_ge(panel_done, done(P_WOUT2 - 1))
                for c in range(4):
                    act.activation(o_hi[:, (4 + c) * LAT:(5 + c) * LAT], ru[:, c * LAT:(c + 1) * LAT], ACT.Copy).then_inc(ohi_done, 1)

            def attention(A):
                def merged(hd):
                    if A["dk"] == P or hd % 2:
                        act.wait_ge(a_values, A["h0"] + hd + 1)
                        c = hd if A["dk"] == P else hd // 2
                        act.activation(o_hi[:, c * LAT:(c + 1) * LAT], bank(4 + c % 2), ACT.Copy).then_inc(ohi_done, 1)

                for n in range(A["n"] + LAG):
                    if n < A["n"]:
                        N = A["n0"] + n
                        sl = N % P_BUFS
                        act.wait_ge(a_max, N + 1)
                        if A is CROSS and N >= P_BUFS:
                            act.wait_ge(a_trans, N - P_BUFS + 1)
                        row = prob[:, sl * LAT:sl * LAT + A["keys"]]
                        src = row if A is SELF else bank(SCORE_BANKS[n % 4], A["keys"])
                        act.activation(row, src, ACT.Exp, bias=stat[:, sl:sl + 1], scale=float(A["dk"]) ** -0.5,
                                       accum_out=stat[:, P_BUFS + sl:P_BUFS + sl + 1]).then_inc(a_exp, 1)
                    if n >= LAG:
                        m = n - LAG
                        hd, it = divmod(m, LT)
                        act.wait_ge(a_trans, A["n0"] + m + 1)
                        H = A["h0"] + hd
                        if it == 0 and H >= 2:
                            act.wait_ge(a_values, H - 1)
                        kt = A["keys"] // P
                        dst = prob_t[:, (hd % 2) * LT * LAT:(hd % 2 + 1) * LT * LAT].rearrange("p (j i) -> p j i", j=LT)
                        act.activation(dst[:, 0:kt, it * P:(it + 1) * P], bank(2 + m % 2, kt * P).rearrange("p (j i) -> p j i", j=kt),
                                       ACT.Copy).then_inc(a_copied, 1)
                        if it == 0 and hd:
                            merged(hd - 1)
                merged(A["n"] // LT - 1)

            def cross_queries():
                for j in range(4):
                    q = P_CQ + j + 2
                    round_panel(q % RING, q // RING + 1, q - RING)
                    act.wait_ge(panel_done, done(P_CQ + j))
                    act.activation(aq[:, j * LAT:(j + 1) * LAT], bank(2 * j), ACT.Copy).then_inc(cq_evac, 1)

            act.wait_ge(vec_loaded, 16)
            act.wait_ge(small_loaded, 80)
            link(act.activation(lsig[:, 8:16], vcol("rg_lambda_2", 0, 8), ACT.Copy))
            link(act.activation(ls_tmp[:, 0:16], lsig[:, :], ACT.Abs))
            act.activation(ls_tmp[:, 0:16], ls_tmp[:, 0:16], ACT.Exp, scale=-1.0).then_inc(ls_exp, 1)
            act.wait_ge(condt_loaded, 16)
            act.activation(cond_s[:, :], cond_s[:, :], ACT.Silu).then_inc(condt_ready, 1)
            act.wait_ge(cond_loaded, 16)
            act.activation(cond_b[:, :], cond_b[:, :], ACT.Silu).then_inc(cond_ready, 1)
            act.wait_ge(consts, 3)
            for kc in range(KC):
                square(norms[0], kc)
            norm(norms[0])
            for G in GROUPS[0:3]:
                hidden_up(G)
                hidden_down(G)
            norm(norms[1])
            input_projection()
            retention()
            gla()
            outputs_and_squares(P_WOUT, norms[2])
            norm(norms[2])
            act.wait_ge(o_ready, 2 * HEADS)
            act.dma_start(x_ctx[:, :], mem_t).then_inc(mem_loaded, 16)
            for G in GROUPS[3:6]:
                hidden_up(G)
                hidden_down(G)
            norm(norms[4])
            input_projection2()
            rg_split()
            attention(SELF)
            outputs_and_squares(P_WOUT2, norms[5])
            norm(norms[5])
            cross_queries()
            attention(CROSS)
            for c, q in enumerate(range(P_CO + 2, P_CO + 6)):
                round_panel(q % RING, q // RING + 1, q - RING)
                if c:
                    square(norms[6], 2 * c - 2)
                    square(norms[6], 2 * c - 1)
            square(norms[6], KC - 2)
            square(norms[6], KC - 1)
            norm(norms[6])
            for G in GROUPS[6:10]:
                hidden_up(G)
                hidden_down(G)
            norm(norms[7])

        @block.vector
        def _(dve):
            chain = [0]

            def link(ins):
                chain[0] += 1
                ins.then_inc(dve_chain, 1)
                dve.wait_ge(dve_chain, chain[0])

            def ada_products(k, w, rows, rows_done):
                for r in range(rows):
                    dve.wait_ge(ada_used, rows_done + r)
                    dve.scalar_tensor_tensor(out=ada_prod[:, :], in0=w, scalar=1.0, in1=cond_b[:, r * D:(r + 1) * D], op0=ALU.mult,
                                             op1=ALU.mult, accum_out=mods[:, ds(r * NMOD * KC + k, 1)]).then_inc(ada_used, 1)

            def ada_chunk(k, s, turn, rows, rows_done):
                dve.wait_ge(ada_ready[s], turn * 16)
                ada_products(k, ada_w[:, s * D:(s + 1) * D], rows, rows_done)

            def add_bias(parts, rows):
                n = (parts[1] - parts[0]) * KC
                for r in range(rows):
                    c = (r * NMOD + parts[0]) * KC
                    link(dve.tensor_tensor(mods[:, c:c + n], mods[:, c:c + n], vcol("ada_b", parts[0] * KC, n), ALU.add))

            def norm_scale(j, row, part, w):
                link(dve.scalar_tensor_tensor(scales[:, j * KC:(j + 1) * KC], mod(row, part), 1.0, vcol(w, 0, KC), ALU.add, ALU.mult))

            def add_squares(m, kc):
                dve.wait_ge(sq_ready, m.n * KC + kc + 1)
                if kc >= 2:
                    dve.wait_ge(sum_done, m.n * (KC - 1) + kc - 1)
                dve.tensor_tensor(act_a[:, 0:m.T], act_a[:, 0:m.T], squares[kc % 2][:, 0:m.T], ALU.add).then_inc(sum_done, 1)

            def add_both(kc):
                dve.wait_ge(sq_ready, 3 * KC + 2 * kc + 2)
                if kc >= 2:
                    dve.wait_ge(sum_done, 3 * (KC - 1) + 2 * (kc - 1))
                dve.tensor_tensor(act_a[:, 0:LAT], act_a[:, 0:LAT], squares[0][:, 0:LAT], ALU.add).then_inc(sum_done, 1)
                dve.tensor_tensor(prod[:, TOK:2 * TOK], prod[:, TOK:2 * TOK], squares[1], ALU.add).then_inc(sum_done, 1)

            def diagonal_of(dst, c0, n):
                eye = ident[:, :].rearrange("p (o i) -> p o i", o=1).broadcast_to([P, n, P])
                r = rms[:, c0:c0 + n].rearrange("p (t o) -> p t o", o=1).broadcast_to([P, n, P])
                return dve.scalar_tensor_tensor(dst[:, 0:n * P].rearrange("p (t i) -> p t i", i=P), eye, float(D), r, ALU.mult, ALU.mult)

            def token_factors(m):
                if m.n == 4:
                    link(dve.tensor_tensor(scales[:, 0:KC], vcol("final_norm_w", 0, KC), vcol("norm_mix_g_2", 0, KC), ALU.mult))
                    dve.wait_ge(stats_ready, 5)
                    link(dve.tensor_scalar(rms[:, 0:LT], bank(4, LT), EPS, None, ALU.add))
                    dve.scalar_tensor_tensor(rms[:, LT:2 * LT], rms[:, 0:LT], EPS, bank(4, LT, LT), ALU.mult, ALU.add)
                    dve.tensor_scalar(rms[:, 2 * LT:LT + TILES], bank(4, 2, 2 * LT), EPS, None, ALU.add).then_inc(means_ready, 1)
                    dve.wait_ge(root_ready, 5)
                    link(dve.reciprocal(rms[:, :], rms[:, :]))
                    diagonal_of(rdiag, LT, TILES).then_inc(diag_ready, 1)
                    diagonal_of(rdiag_x, 0, LT).then_inc(diag_ready, 1)
                    return
                n = m.T // P
                dve.wait_ge(root_ready, m.n + 1)
                link(dve.reciprocal(rms[:, 0:n], rms[:, 0:n]))
                diagonal_of(rdiag, 0, n).then_inc(diag_ready, 1)

            def norm(m):
                if m.n:
                    token_factors(m)
                dve.wait_ge(rstd_ready, 4 if m.n == 4 else m.n + 1)
                for kc in range(KC + 1):
                    if kc < KC:
                        b = (kc % 2) * TOK
                        for j, (xs, n, c0, _) in enumerate(m.segs()):
                            o = xs[:, kc * n:(kc + 1) * n] if m.last else prod[:, b + c0:b + c0 + n]
                            ins = dve.scalar_tensor_tensor(o, xs[:, kc * n:(kc + 1) * n], m.A[j](kc), bank(6 + j, n),
                                                           ALU.mult, ALU.mult)
                        ins.then_inc(xn_ready, 1)
                    if kc > 0 and not m.last:
                        k = kc - 1
                        b = (k % 2) * TOK
                        dve.wait_ge(hhi_done, H_BEFORE[m.n] + k + 1)
                        dve.wait_ge(xn_ready, m.xn0 + k + 1)
                        for j, (_, n, c0, _) in enumerate(m.segs()):
                            sl = slice(h_at(k, c0), h_at(k, c0) + n)
                            src = prod[:, b + c0:b + c0 + n]
                            if m.B is None:
                                ins = dve.tensor_tensor(h_lo[:, sl], src, h_hi[:, sl].bitcast(f32), ALU.subtract)
                            else:
                                ins = dve.scalar_tensor_tensor(h_lo[:, sl], src, m.B[j](k), h_hi[:, sl].bitcast(f32),
                                                               ALU.add, ALU.subtract)
                        ins.then_inc(h_ready, 1)
                        dve.wait_ge(h_ready, H_BEFORE[m.n] + k + 1)
                if m.n == 4:
                    dve.wait_ge(rstd_ready, 5)
                    for kc in range(KC):
                        x = x_lat[:, kc * LAT:(kc + 1) * LAT]
                        dve.scalar_tensor_tensor(x, x, vcol("final_norm_w", kc), bank(5), ALU.mult, ALU.mult).then_inc(xn_ready, 1)

            def hidden_up(G):
                T, cols = G["T"], token_cols(G["T"])
                per_f = 2 if G["gated"] else 1
                f_per = RING // per_f
                with dve.Fori(0, G["g"] // f_per) as i:
                    for u in range(f_per):
                        if G["layer"] == 0 and (u == 0 or ADA_PER_PAIR[G["n"]] == 6):
                            npp = ADA_PER_PAIR[G["n"]]
                            for j in range(ADA_RING):
                                k = ada_before(G["n"]) + i * npp + u * ADA_RING + j
                                ada_chunk(k, j, ((ada_before(G["n"]) - ADA_FIRST) // ADA_RING) + i * (npp // ADA_RING) + u + 1, ADA_ROWS[G["n"]],
                                          ada_rows(G["n"], k))
                        f = G["f0"] + i * f_per + u
                        b = (u % 2) * TOK
                        dve.wait_ge(panel_done, done(G["p_up"] + i * RING + (u + 1) * per_f - 1))
                        dve.wait_ge(silu_done, f + 1)
                        dve.wait_ge(g_ready, f + 1)
                        if G["gated"]:
                            dve.tensor_tensor(prod[:, b:b + T], act_a[:, b:b + T], bank(4 * u + 2, T), ALU.mult).then_inc(up_evac, 1)
                        else:
                            dve.tensor_tensor(prod[:, b:b + T], act_a[:, b:b + T], act_a[:, b:b + T], ALU.mult).then_inc(up_evac, 1)
                        dve.wait_ge(ghi_done, f + 1)
                        fo = (i * f_per + u) * TOK
                        dve.tensor_tensor(g_lo[:, ds(fo, T)], prod[:, b:b + T], g_hi[:, ds(fo, T)].bitcast(f32), ALU.subtract)\
                            .then_inc(g_ready, 1)

            def hidden_down(G):
                T = G["T"]
                def add(dst, src, gate):
                    return dve.scalar_tensor_tensor(dst, src, gate, dst, ALU.mult, ALU.add)

                def output(o, c):
                    dve.wait_ge(panel_done, done(G["p_down"] + o))
                    dve.wait_ge(down_evac, G["o0"] + o + 1)
                    if T == TOK:
                        add(x_lat[:, ds(o * LAT, LAT)], bank(2 * c), gates[:, ds(o, 1)])
                        ins = add(x_ctx[:, ds(o * CTX, CTX)], bank(2 * c + 1, CTX), gates[:, ds(o + KC, 1)])
                    elif G["gated"]:
                        ins = add(x_lat[:, ds(o * LAT, LAT)], bank(2 * c), gates[:, ds(o + 3 * KC, 1)])
                    else:
                        dst = x_lat[:, ds(o * LAT, LAT)]
                        ins = dve.tensor_tensor(dst, bank(2 * c), dst, ALU.add)
                    ins.then_inc(down_evac, 1)

                if G["last"]:
                    for o in range(KC):
                        output(o, o % RING)
                        if o and G["layer"] == 1:
                            add_both(o)
                        elif o:
                            add_squares(norms[(1, 3, 7)[G["layer"]]], o)
                    return
                with dve.Fori(0, KC // RING) as i:
                    for c in range(RING):
                        output(i * RING + c, c)

            def log_sigmoids():
                z, w, w2, p = (ls_tmp[:, j * 16:(j + 1) * 16] for j in range(4))
                dve.wait_ge(ls_exp, 1)
                link(dve.tensor_scalar(w, z, 2.0, None, ALU.add))
                link(dve.reciprocal(w, w))
                link(dve.tensor_tensor(w, w, z, ALU.mult))
                link(dve.tensor_tensor(w2, w, w, ALU.mult))
                link(dve.tensor_scalar(p, w2, 1.0 / 17, 1.0 / 15, ALU.mult, ALU.add))
                for k in (13, 11, 9, 7, 5, 3, 1):
                    link(dve.tensor_tensor(p, p, w2, ALU.mult))
                    link(dve.tensor_scalar(p, p, 1.0 / k, None, ALU.add))
                link(dve.scalar_tensor_tensor(p, p, 2.0, w, ALU.mult, ALU.mult))
                link(dve.scalar_tensor_tensor(lsig[:, :], lsig[:, :], 0.0, p, ALU.min, ALU.subtract))
                dve.tensor_scalar(nlsig[:, :], lsig[:, 4:8], -1.0, None, ALU.mult).then_inc(lsig_ready, 1)

            def residual(p0, o0, gate, m):
                for o in range(KC):
                    dve.wait_ge(panel_done, done(p0 + o))
                    dve.wait_ge(down_evac, o0 + o + 1)
                    dst = x_lat[:, o * LAT:(o + 1) * LAT]
                    if gate is None:
                        ins = dve.tensor_tensor(dst, bank(2 * (o % RING)), dst, ALU.add)
                    else:
                        ins = dve.scalar_tensor_tensor(dst, bank(2 * (o % RING)), gates[:, gate * KC + o:gate * KC + o + 1], dst, ALU.mult, ALU.add)
                    ins.then_inc(down_evac, 1)
                    if o:
                        add_squares(m, o)

            def head_centre(j):
                dve.wait_ge(mean_ready, j + 1)
                dve.scalar_tensor_tensor(o_sb[:, :], bank(3), -float(D // P), o_sb[:, :], ALU.mult, ALU.add).then_inc(o_centred, 1)
                dve.wait_ge(o_centred, j + 1)

            def head_norm_step(j, t):
                if t < LT:
                    if t == 0:
                        dve.wait_ge(oroot_ready, j + 1)
                    sl = slice(t * P, (t + 1) * P)
                    link(dve.reciprocal(o_sq[:, sl], o_sq[:, sl]))
                elif t == LT:
                    link(dve.scalar_tensor_tensor(o_sb[:, :], o_sb[:, :], vcol("ret_norm_w", j), o_sq[:, :], ALU.mult, ALU.mult))
                else:
                    gate = rg[:, j * LAT:(j + 1) * LAT]
                    dve.tensor_tensor(gate, o_sb[:, :], gate, ALU.mult).then_inc(o_scaled, 1)
                    dve.wait_ge(o_scaled, j + 1)

            def head_lo(j):
                dve.wait_ge(ohi_done, j + 1)
                sl = slice(j * LAT, (j + 1) * LAT)
                src = rg[:, sl] if j < HEADS else o_pair[j % 2][:, :]
                dve.tensor_tensor(o_lo[:, sl], src, o_hi[:, sl].bitcast(f32), ALU.subtract).then_inc(mix_ready, 1)

            def input_projection():
                dve.wait_ge(lr_split, 1)
                dve.tensor_tensor(lr_lo[:, :], lr_raw[:, :], lr_hi[:, :].bitcast(f32), ALU.subtract).then_inc(lr_lo_done, 1)
                for n in range(4):
                    d, hp = divmod(n, 2)
                    dve.wait_ge(gate_act, n + 1)
                    dst = (gf, gb)[d][:, hp * TOK:(hp + 1) * TOK]
                    link(dve.scalar_tensor_tensor(dst, gate_y[:, :], 0.0, gate_e[:, :], ALU.min, ALU.subtract))
                    dve.tensor_scalar(dst, dst, 1.0 / 16, None, ALU.mult).then_inc(gate_dve, 1)
                dve.wait_ge(rope_loaded, 16)
                for j in range(8):
                    dve.wait_ge(win_evac, j + 1 if j < 4 else j + 5)
                    dst = rq[:, j * LAT:(j + 1) * LAT] if j < 4 else rk[:, (j - 4) * TOK:(j - 4) * TOK + LAT]
                    if j:
                        dve.wait_ge(rope_done, j)
                    link(dve.stream_shuffle(rope_tmp[:, :], dst, SWAP16))
                    link(dve.tensor_tensor(rope_tmp[:, :], rope_tmp[:, :], rope_cs[:, LAT:2 * LAT], ALU.mult))
                    link(dve.tensor_tensor(dst, dst, rope_cs[:, 0:LAT], ALU.mult))
                    dve.tensor_tensor(dst, dst, rope_tmp[:, :], ALU.add).then_inc(rope_done, 1)

            def scan(dst, src, n):
                return dve.tensor_tensor_scan(dst, src, zero_t.to_broadcast([P, n]), 0.0, ALU.add, ALU.add)

            def pair_sums(hp):
                C = [cum[:, j * LAT:(j + 1) * LAT] for j in range(4)]
                f, b = gf[:, hp * TOK:(hp + 1) * TOK], gb[:, hp * TOK:(hp + 1) * TOK]
                if hp == 0:
                    dve.wait_ge(pv_done, 6 * HEADS)
                    dve.wait_ge(o_centred, HEADS)
                else:
                    dve.wait_ge(d_ready, TOP)
                    dve.wait_ge(x_ready, TOP + 1)
                    dve.wait_ge(unit_ready, n_unit(0, TOP - 1))
                kf, kb = ctx_k[hp][:, 0:CTX], ctx_k[hp][:, CTX:2 * CTX]
                scan(C[2], f[:, 0:LAT], LAT)
                scan(suf[:, ::-1], b[:, 0:LAT][:, ::-1], LAT)
                scan(kf[:, ::-1], f[:, LAT:TOK][:, ::-1], CTX)
                link(scan(kb, b[:, LAT:TOK], CTX))
                dve.tensor_tensor(kf, kf, f[:, LAT:TOK], ALU.subtract)
                dve.tensor_tensor(kb, kb, b[:, LAT:TOK], ALU.subtract).then_inc(ctx_arg, 1)
                for t in range(LT):
                    sl = slice(t * P, (t + 1) * P)
                    scan(C[0][:, sl], f[:, sl], P)
                    scan(C[1][:, sl], b[:, sl], P)
                link(scan(C[3], b[:, 0:LAT], LAT))
                dve.tensor_tensor(C[1], C[1], b[:, 0:LAT], ALU.subtract)
                dve.tensor_tensor(C[3], C[3], b[:, 0:LAT], ALU.subtract).then_inc(cum_ready, 1)

            def context_scaled(hp):
                q, k = gq[:, hp * LAT:(hp + 1) * LAT], gk[:, hp * TOK:(hp + 1) * TOK]
                kf, kb = ctx_k[hp][:, 0:CTX], ctx_k[hp][:, CTX:2 * CTX]
                dve.wait_ge(ctx_arg, hp + 1)
                dve.wait_ge(ctx_exp, hp + 1)
                dve.tensor_tensor(kf, kf, k[:, LAT:TOK], ALU.mult)
                dve.tensor_tensor(kb, kb, k[:, LAT:TOK], ALU.mult)
                dve.wait_ge(x_ready, n_scaled(hp, 0))
                dve.tensor_tensor(q_lv[:, 0:LAT], q, d_lv[:, 0:LAT], ALU.mult)
                dve.tensor_tensor(k_lv[:, 0:LAT], q, d_lv[:, LAT:2 * LAT], ALU.mult).then_inc(qk_ready, 1)

            def retention():
                dve.wait_ge(u_loaded, 16)
                dve.wait_ge(lsig_ready, 1)
                dve.wait_ge(panel_done, done(P_WIN + WIN[WIN_CONTEXT - 1][1]))

                def exponents(j):
                    lg_f, nlg_b = lsig[:, j:j + 1], nlsig[:, j:j + 1]
                    if j:
                        dve.wait_ge(s_evac, 6 * j)
                    dve.tensor_scalar(decay_f[:, 0:UW], u_sb[:, :], 0.0, lg_f, ALU.max, ALU.mult)
                    dve.tensor_scalar(decay_b[:, 0:UW], u_sb[:, :], 0.0, nlg_b, ALU.min, ALU.mult)
                    dve.tensor_scalar(decay_f[:, UW:], u_sb[:, 256:], float(CTX), lg_f, ALU.add, ALU.mult)
                    dve.tensor_scalar(decay_b[:, UW:], u_sb[:, 256:], -float(LAT), nlg_b, ALU.add, ALU.mult).then_inc(arg_ready, 1)

                def decays_of(j):
                    dve.wait_ge(exp_ready, j + 1)
                    dve.scalar_tensor_tensor(decay_f[:, 0:UW], u_sb[:, :], 0.0, decay_f[:, 0:UW], ALU.is_ge, ALU.mult)
                    link(dve.scalar_tensor_tensor(decay_b[:, 0:UW], u_sb[:, :], 0.0, decay_b[:, 0:UW], ALU.is_le, ALU.mult))
                    link(dve.tensor_tensor(decay_f[:, :], decay_f[:, :], decay_b[:, :], ALU.add))

                exponents(0)
                decays_of(0)
                for j in range(HEADS):
                    for t in range(TILES):
                        n = j * TILES + t
                        dve.wait_ge(s_ready, n + 1)
                        if n >= 2:
                            dve.wait_ge(pv_done, n - 1)
                        c = 384 - P * t if t < LT else UW + P - P * (t - LT)
                        dve.tensor_tensor(s_ring[n % 2][:, :], bank(n % 2), decay_f[:, c:c + LAT], ALU.mult)\
                            .then_inc(s_evac, 1)
                        if j:
                            head_norm_step(j - 1, t)
                    if j + 1 < HEADS:
                        exponents(j + 1)
                        decays_of(j + 1)
                    head_centre(j)
                pair_sums(0)
                context_scaled(0)
                for t in range(TILES):
                    head_norm_step(HEADS - 1, t)
                for j in range(HEADS):
                    head_lo(j)

            def gla():
                dve.wait_ge(masks_loaded, 32)
                dve.wait_ge(win_evac, len(WIN))
                dve.wait_ge(mix_ready, HEADS)
                def scaled(hp, u):
                    dve.wait_ge(x_ready, n_scaled(hp, u))
                    n = n_unit(hp, u - 2) if u > 2 else n_unit(hp, -1) if u == 2 else hp * UNITS
                    if n:
                        dve.wait_ge(unit_ready, n)
                    q, k = gq[:, hp * LAT:(hp + 1) * LAT], gk[:, hp * TOK:hp * TOK + LAT]
                    o, h = (u % 2) * LAT, 2 ** (u - 1)
                    ql, kl, xf, xb, q, k = (a.rearrange("p (n t h) -> p n t h", t=2, h=h) for a in
                                            (q_lv[:, o:o + LAT], k_lv[:, o:o + LAT], d_lv[:, 2 * o:2 * o + LAT],
                                             d_lv[:, 2 * o + LAT:2 * o + 2 * LAT], q, k))
                    dve.tensor_tensor(ql[:, :, 0], q[:, :, 0], xb[:, :, 0], ALU.mult)
                    dve.tensor_tensor(ql[:, :, 1], q[:, :, 1], xf[:, :, 1], ALU.mult)
                    dve.tensor_tensor(kl[:, :, 0], k[:, :, 0], xf[:, :, 0], ALU.mult)
                    dve.tensor_tensor(kl[:, :, 1], k[:, :, 1], xb[:, :, 1], ALU.mult).then_inc(qk_ready, 1)

                def masked(hp, u):
                    dve.wait_ge(unit_ready, n_unit(hp, u))
                    if hp:
                        dve.wait_ge(o_ready, HEADS + 2)
                    if u:
                        dve.wait_ge(unit_dve, hp * (MASKED + 1) + u)
                    for a in range(2):
                        c0 = a * TILES * LAT
                        dst = s_gla[:, c0:c0 + LT * (LAT + P)].rearrange("p (t i) -> p t i", t=LT)[:, :, 0:P]
                        src = bank(unit_bank(u, a)).rearrange("p (t i) -> p t i", t=LT)
                        which = diag2_sb[:, :] if u == 0 else masks[:, (u - 1) * P:u * P]
                        which = which.rearrange("p (o i) -> p o i", o=1).broadcast_to([P, LT, P])
                        ins = dve.tensor_tensor(dst, src, which, ALU.mult) if u == 0 else dve.copy_predicated(dst, which, src)
                    ins.then_inc(unit_dve, 1)

                def pair_factors(hp):
                    dve.wait_ge(oroot_ready, HEADS + hp + 1)
                    link(dve.reciprocal(head_rms[:, :], head_rms[:, :]))
                    for a in range(2):
                        dst = f_pair[a][:, :].rearrange("p (t i) -> p t i", i=P)
                        eye = ident[:, :].rearrange("p (o i) -> p o i", o=1).broadcast_to([P, LT, P])
                        r = head_rms[:, a * LT:(a + 1) * LT].rearrange("p (t o) -> p t o", o=1).broadcast_to([P, LT, P])
                        ins = dve.scalar_tensor_tensor(dst, eye, float(D), r, ALU.mult, ALU.mult)
                    ins.then_inc(hdiag_ready, 1)

                def pair_scaled(hp):
                    dve.wait_ge(spread_ready, hp + 1)
                    for a in range(2):
                        j = 2 * hp + a
                        o = o_pair[a][:, :]
                        link(dve.scalar_tensor_tensor(o, o, vcol("gla_norm_w", j), bank(5 + 2 * a), ALU.mult, ALU.mult))
                        dve.tensor_tensor(o, o, gg[:, j * LAT:(j + 1) * LAT], ALU.mult).then_inc(o_scaled, 1)
                        dve.wait_ge(o_scaled, HEADS + j + 1)

                for u in range(1, TOP + 1):
                    scaled(0, u)
                    if u - 1 <= MASKED:
                        masked(0, u - 1)
                pair_sums(1)
                context_scaled(1)
                for u in range(1, TOP + 1):
                    scaled(1, u)
                    if u == 2:
                        pair_factors(0)
                    if u - 1 <= MASKED:
                        masked(1, u - 1)
                    if u == 4:
                        pair_scaled(0)
                    if u == 6:
                        head_lo(HEADS)
                        head_lo(HEADS + 1)
                pair_factors(1)
                pair_scaled(1)
                head_lo(HEADS + 2)
                head_lo(HEADS + 3)

            def input_projection2():
                dve.wait_ge(pos_loaded, 16)
                link(dve.tensor_copy(angle[:, :], pos_i[:, :]))
                link(dve.tensor_scalar(angle[:, :], angle[:, :], rope_pp[:, 0:1], None, ALU.mult))
                link(dve.tensor_scalar(turns[:, :], angle[:, :], 1.0 / (2 * math.pi), ROUND, ALU.mult, ALU.add))
                link(dve.tensor_scalar(turns[:, :], turns[:, :], ROUND, None, ALU.subtract))
                for part in TWO_PI:
                    link(dve.scalar_tensor_tensor(angle[:, :], turns[:, :], -part, angle[:, :], ALU.mult, ALU.add))
                cos_a, sin_a = cs2[:, 0:LAT], cs2[:, LAT:2 * LAT]
                link(dve.tensor_scalar(cos_a, angle[:, :], math.pi / 2, None, ALU.add))
                link(dve.tensor_scalar(turns[:, :], cos_a, math.pi, -2 * math.pi, ALU.is_gt, ALU.mult))
                link(dve.tensor_tensor(cos_a, cos_a, turns[:, :], ALU.add))
                link(dve.tensor_copy(sin_a, angle[:, :]))
                dve.tensor_scalar(cs2[:, :], cs2[:, :], PI_IN, -PI_IN, ALU.min, ALU.max).then_inc(cs_arg, 1)
                dve.wait_ge(cs_ready, 1)
                link(dve.tensor_scalar(sin_a, sin_a, rope_pp[:, 1:2], None, ALU.mult))
                rg_convolution()

                def rotate(j):
                    dve.wait_ge(win2_evac, 8 + j + 1)
                    dst = (aq if j < 4 else ak)[:, (j % 4) * LAT:(j % 4 + 1) * LAT]
                    if j:
                        dve.wait_ge(rope2_done, j)
                    link(dve.stream_shuffle(rope_tmp[:, :], dst, SWAP16))
                    link(dve.tensor_tensor(rope_tmp[:, :], rope_tmp[:, :], sin_a, ALU.mult))
                    link(dve.tensor_tensor(dst, dst, cos_a, ALU.mult))
                    dve.tensor_tensor(dst, dst, rope_tmp[:, :], ALU.add).then_inc(rope2_done, 1)

                rg_gated(0)
                rg_scans(0)
                rg_gated(1)
                rg_scans(1)
                for j in range(4):
                    rotate(j)
                rg_gated(2)
                rg_scans(2)
                rotate(4)
                rotate(5)
                rg_gated(3)
                rotate(6)
                rotate(7)
                rg_scans(3)

            def attention(A):
                if A is SELF:
                    dve.wait_ge(bias_loaded, 16)
                scale = float(A["dk"]) ** -0.5
                for n in range(A["n"] + 1):
                    N = A["n0"] + n
                    if n < A["n"]:
                        sl = N % P_BUFS
                        row = prob[:, sl * LAT:sl * LAT + A["keys"]]
                        top = stat[:, sl:sl + 1]
                        dve.wait_ge(a_scores, N + 1)
                        if N >= P_BUFS:
                            dve.wait_ge(a_trans, N - P_BUFS + 1)
                        if A is SELF:
                            it = n % LT
                            link(dve.tensor_tensor_reduce(out=row, in0=bank(SCORE_BANKS[n % 4]), in1=bias_sb[:, it * LAT:(it + 1) * LAT], scale=1.0,
                                                          scalar=-3e38, op0=ALU.add, op1=ALU.max, accum_out=top))
                        else:
                            link(dve.tensor_reduce(out=top, in_=bank(SCORE_BANKS[n % 4], A["keys"]), axis=AX.X, op=ALU.max))
                        dve.tensor_scalar(top, top, -scale, None, ALU.mult).then_inc(a_max, 1)
                    if n >= 1:
                        sl = (N - 1) % P_BUFS
                        row = prob[:, sl * LAT:sl * LAT + A["keys"]]
                        total, inv = stat[:, P_BUFS + sl:P_BUFS + sl + 1], stat[:, 2 * P_BUFS + sl:2 * P_BUFS + sl + 1]
                        dve.wait_ge(a_exp, N)
                        link(dve.reciprocal(inv, total))
                        dve.tensor_scalar(row, row, inv, None, ALU.mult).then_inc(a_prob, 1)
                        hd, it = divmod(n - 1, LT)
                        if it == LT - 1 and (A["dk"] == P or hd % 2):
                            c = hd if A["dk"] == P else hd // 2
                            pending.append(c)
                    while pending and (n == A["n"] or n % LT == 3):
                        c = pending.pop(0)
                        dve.wait_ge(ohi_done, A["s0"] + c + 1)
                        sl = slice(c * LAT, (c + 1) * LAT)
                        dve.tensor_tensor(o_lo[:, sl], bank(4 + c % 2), o_hi[:, sl].bitcast(f32), ALU.subtract).then_inc(mix_ready, 1)

            pending = []

            def rg_convolution():
                link(dve.tensor_scalar(rg_c[:, :], lsig[:, 8:16], -8.0, None, ALU.mult))
                for c in range(4):
                    dve.wait_ge(win2_evac, c + 1)
                    u_in, o = ru[:, c * LAT:(c + 1) * LAT], uc[:, c * LAT:(c + 1) * LAT]
                    w = [vcol("conv_w_2", 4 * k + c) for k in range(4)]
                    link(dve.tensor_scalar(o, u_in, w[2], vcol("conv_b_2", c), ALU.mult, ALU.add))
                    link(dve.scalar_tensor_tensor(o[:, 1:], u_in[:, :LAT - 1], w[1], o[:, 1:], ALU.mult, ALU.add))
                    link(dve.scalar_tensor_tensor(o[:, 2:], u_in[:, :LAT - 2], w[0], o[:, 2:], ALU.mult, ALU.add))
                    dve.scalar_tensor_tensor(o[:, :LAT - 1], u_in[:, 1:], w[3], o[:, :LAT - 1], ALU.mult, ALU.add).then_inc(rg_conv, 1)
                dve.wait_ge(rg_conv, 4)

            def rg_gated(c):
                dve.wait_ge(rg_sig, c + 1)
                for z in range(2):
                    sl = slice(z * LAT, (z + 1) * LAT)
                    dve.tensor_tensor(rg_i[:, sl], rg_i[:, sl], uc[:, c * LAT:(c + 1) * LAT], ALU.mult)
                    ins = dve.tensor_scalar(rg_r[:, sl], rg_r[:, sl], rg_c[:, 4 * z + c:4 * z + c + 1], None, ALU.mult)
                ins.then_inc(rg_la, 1)
                dve.wait_ge(rg_la, c + 1)

            def rg_scans(c):
                dve.wait_ge(rg_exp, c + 1)
                link(dve.tensor_tensor(rg_h[:, :], rg_r[:, :], rg_r[:, :], ALU.mult))
                dve.scalar_tensor_tensor(rg_t[:, :], rg_h[:, :], 1.0, rg_t[:, :], ALU.add, ALU.mult).then_inc(rg_v, 1)
                dve.wait_ge(rg_v, c + 1)
                dve.wait_ge(rg_root, c + 1)
                link(dve.tensor_tensor(rg_i[:, :], rg_i[:, :], rg_t[:, :], ALU.mult))
                dve.tensor_tensor_scan(rg_h[:, 0:LAT], rg_r[:, 0:LAT], rg_i[:, 0:LAT], 0.0, ALU.mult, ALU.add)
                link(dve.tensor_tensor_scan(rg_h[:, LAT:][:, ::-1], rg_r[:, LAT:][:, ::-1], rg_i[:, LAT:][:, ::-1], 0.0, ALU.mult, ALU.add))
                link(dve.tensor_tensor(rg_h[:, 0:LAT], rg_h[:, 0:LAT], rg_h[:, LAT:], ALU.add))
                dve.wait_ge(win2_evac, 4 + c + 1)
                sl = slice(c * LAT, (c + 1) * LAT)
                dve.tensor_tensor(ru[:, sl], rg_h[:, 0:LAT], ry[:, sl], ALU.mult).then_inc(rg_hid, 1)
                dve.wait_ge(rg_hid, c + 1)

            def rg_split():
                for c in range(4):
                    dve.wait_ge(ohi_done, 8 + c + 1)
                    sl = slice((4 + c) * LAT, (5 + c) * LAT)
                    dve.tensor_tensor(o_lo[:, sl], ru[:, c * LAT:(c + 1) * LAT], o_hi[:, sl].bitcast(f32), ALU.subtract).then_inc(mix_ready, 1)

            dve.sem_inc(up_evac, 2)
            dve.sem_inc(g_ready, 2)
            dve.sem_inc(down_evac, KC)
            dve.wait_ge(vec_loaded, 16)
            dve.wait_ge(small_loaded, 80)
            log_sigmoids()
            dve.sem_inc(ada_used, 2 * ADA_PE)
            for kc in range(1, KC):
                add_squares(norms[0], kc)
            dve.wait_ge(cond_ready, 1)
            for k in range(ADA_PE, ADA_FIRST):
                if k == ADA_PE + 2:
                    token_factors(norms[0])
                dve.wait_ge(ada_loaded[k], 16)
                ada_products(k, ada_f[k][:, :], 2, 2 * k)
            dve.wait_ge(ada_used, 2 * ADA_FIRST)
            dve.wait_ge(ada_mods, 2)
            for r in range(2):
                c = r * NMOD * KC
                src = bank(5, 2 * ADA_PE).rearrange("p (k r) -> p k r", r=2)[:, :, r]
                link(dve.tensor_copy(mods[:, c:c + ADA_PE], src))
            add_bias((0, 2), 2)
            norm_scale(0, 0, 1, "norm1_w")
            norm_scale(1, 1, 1, "norm1_w")
            norm(norms[0])
            for G in GROUPS[0:3]:
                hidden_up(G)
                if G["n"] == 0:
                    dve.wait_ge(ada_used, ada_rows(0, ada_before(1)))
                    add_bias((2, 3), 2)
                    for r in range(2):
                        link(dve.tensor_scalar(gates[:, r * KC:(r + 1) * KC], mod(r, 2), 0.5, None, ALU.mult))
                hidden_down(G)
            dve.wait_ge(ada_used, ada_rows(2, ada_before(3)))
            add_bias((3, 9), 1)
            link(dve.tensor_tensor(mods[:, 72 + 24:72 + 40], mods[:, 72 + 24:72 + 40], vcol("ada_b", 24, 16), ALU.add))
            norm_scale(2, 0, 4, "norm2_w")
            norm_scale(3, 1, 4, "norm2_w")
            norm_scale(4, 0, 7, "norm3_w")
            link(dve.tensor_copy(gates[:, 2 * KC:3 * KC], mod(0, 5)))
            link(dve.tensor_scalar(gates[:, 3 * KC:4 * KC], mod(0, 8), 0.5, None, ALU.mult))
            norm(norms[1])
            input_projection()
            retention()
            gla()
            residual(P_WOUT, 3 * KC, 2, norms[2])
            norm(norms[2])
            for G in GROUPS[3:6]:
                hidden_up(G)
                hidden_down(G)
            norm(norms[4])
            input_projection2()
            rg_split()
            attention(SELF)
            dve.wait_ge(xn_ready, 5 * KC)
            residual(P_WOUT2, 7 * KC, None, norms[5])
            norm(norms[5])
            attention(CROSS)
            for o in range(KC):
                dve.wait_ge(panel_done, done(P_CO + o // 2))
                dve.wait_ge(down_evac, 8 * KC + o + 1)
                dst = x_lat[:, o * LAT:(o + 1) * LAT]
                dve.tensor_tensor(dst, bank(o), dst, ALU.add).then_inc(down_evac, 1)
                if o:
                    add_squares(norms[6], o)
            norm(norms[6])
            for G in GROUPS[6:10]:
                hidden_up(G)
                hidden_down(G)
            norm(norms[7])

        @block.tensor
        def _(pe):
            def product3(out, lhs, rhs, first, last):
                pe.matmul(out, lhs[0], rhs[0], start=first, stop=False)
                pe.matmul(out, lhs[0], rhs[1], start=False, stop=False)
                return pe.matmul(out, lhs[1], rhs[0], start=False, stop=last)

            def panel_product(s, banks, act_hi, act_lo, cols, n_k=KC, ready=None, off=0, at_=h_at):
                for kc in range(n_k):
                    if ready is not None:
                        pe.wait_ge(*ready(kc))
                    w = slice(s * PANEL + (off + kc) * P, s * PANEL + (off + kc + 1) * P)
                    order = ((whi, act_hi), (whi, act_lo), (wlo, act_hi))
                    for j, (wt, a) in enumerate(order):
                        for b, c0, n in cols:
                            ins = pe.matmul(bank(banks + b, n), wt[:, w], a[:, at_(kc, c0):at_(kc, c0) + n],
                                            start=kc == 0 and j == 0, stop=kc == n_k - 1 and j == 2)
                return ins

            def first_pair(p0, banks, h_base, cols):
                for c in range(2):
                    pe.wait_ge(lo_done, p0 + c + 1)
                for kc in range(KC):
                    pe.wait_ge(h_ready, h_base + kc + 1)
                    for c in range(2):
                        w = slice(c * PANEL + kc * P, c * PANEL + (kc + 1) * P)
                        for j, (wt, a) in enumerate(((whi, h_hi), (whi, h_lo), (wlo, h_hi))):
                            for b, c0, n in cols:
                                ins = pe.matmul(bank(banks[c] + b, n), wt[:, w], a[:, h_at(kc, c0):h_at(kc, c0) + n],
                                                start=kc == 0 and j == 0, stop=kc == KC - 1 and j == 2)
                        if kc == KC - 1:
                            ins.then_inc(panel_done, 1)

            def norm(m):
                if m.n == 0:
                    pe.wait_ge(consts, 3)
                pe.wait_ge(sum_done, (m.n + 1) * (KC - 1))
                if m.n == 4:
                    for t in range(LT + TILES):
                        src = act_a[:, t * P:(t + 1) * P] if t < LT else prod[:, TOK + (t - LT) * P:TOK + (t - LT + 1) * P]
                        ins = pe.matmul(bank(4, 1, t), src, ones_k[:, 0:1], start=True, stop=True)
                    ins.then_inc(stats_ready, 2)
                    pe.wait_ge(diag_ready, 4)
                    pe.matmul(bank(6), ones_k[:, :], rdiag[:, 0:LAT], start=True, stop=True)
                    pe.matmul(bank(7, CTX), ones_k[:, :], rdiag[:, LAT:TOK], start=True, stop=True).then_inc(rstd_ready, 1)
                    pe.wait_ge(diag_ready, 5)
                    pe.matmul(bank(5), ones_k[:, :], rdiag_x[:, :], start=True, stop=True).then_inc(rstd_ready, 1)
                    return
                for t in range(m.T // P):
                    ins = pe.matmul(bank(4, 1, t), act_a[:, t * P:(t + 1) * P], ones_k[:, 0:1], start=True, stop=True)
                ins.then_inc(stats_ready, 1)
                pe.wait_ge(diag_ready, m.n + 1)
                for j, (_, n, c0, _) in enumerate(m.segs()):
                    ins = pe.matmul(bank(6 + j, n), ones_k[:, :], rdiag[:, c0:c0 + n], start=True, stop=True)
                ins.then_inc(rstd_ready, 1)

            def first_modulation(k0, k1):
                pe.wait_ge(condt_ready, 1)
                for k in range(k0, k1):
                    pe.wait_ge(ada_loaded[k], 16)
                    for kc in range(KC):
                        ins = pe.matmul(bank(5, 2, 2 * k), ada_f[k][:, kc * P:(kc + 1) * P], cond_s[:, 2 * kc:2 * kc + 2],
                                        start=kc == 0, stop=kc == KC - 1)
                ins.then_inc(ada_mods, 1)

            def hidden_up(G, h_base):
                cols = token_cols(G["T"])
                per_f = 2 if G["gated"] else 1
                f_per = RING // per_f

                def panel(i, s):
                    u = s // per_f
                    if s % per_f == 0:
                        pe.wait_ge(up_evac, G["f0"] + i * f_per + u + 1)
                        pe.wait_ge(down_evac, G["o0"] + KC - (2 if u == 0 else 0))
                    pe.wait_ge(lo_done, G["p_up"] + i * RING + s + 1)
                    panel_product(s, 2 * s, h_hi, h_lo, cols).then_inc(panel_done, 1)

                if G["n"] == 0:
                    first_pair(G["p_up"], (0, 2), h_base, cols)
                    for s in range(2, RING):
                        panel(0, s)
                with pe.Fori(1 if G["n"] == 0 else 0, G["g"] // f_per) as i:
                    for s in range(RING):
                        panel(i, s)

            def hidden_down(G):
                cols = token_cols(G["T"])
                f_end = G["f0"] + G["g"] + 2
                with pe.Fori(0, KC // RING) as i:
                    for c in range(RING):
                        pe.wait_ge(up_evac, f_end - (1 if c < 2 else 0))
                        pe.wait_ge(down_evac, G["o0"] + i * RING + c + RING + 1)
                        pe.wait_ge(lo_done, G["p_down"] + i * RING + c + 1)
                        ready = (lambda kc: (g_ready, G["f0"] + 2 + kc + 1)) if c == 0 else None
                        panel_product(c, 2 * c, g_hi, g_lo, cols, n_k=G["g"], ready=ready, at_=hidden_at).then_inc(panel_done, 1)

            def panel_rows(s, k, banks, tiles=TILES, t0=0, first=False, last=False):
                for c in range(2):
                    for t in range(tiles):
                        a = slice(h_at(k + c, (t0 + t) * P), h_at(k + c, (t0 + t) * P) + P)
                        w = slice(s * PANEL + c * 512, s * PANEL + (c + 1) * 512)
                        ins = product3(bank(banks[t]), (h_hi[:, a], h_lo[:, a]), (whi[:, w], wlo[:, w]),
                                       first and c == 0, last and c == 1)
                return ins

            def input_projection():
                first_pair(P_WIN, (0, 2), H_BEFORE[1], token_cols(LAT))
                last_use = {0: 1, 2: 2}
                gate_step(1)
                for n in range(2, WIN_ALONE):
                    project(n, 2 * (WIN[n][1] % RING), last_use)
                    gate_step(n)

            def gate_step(n):
                if n == 1:
                    pe.wait_ge(lr_lo_done, 1)
                    for kc in range(KC):
                        w = slice(kc * LR_COLS, (kc + 1) * LR_COLS)
                        for j, (wt, a) in enumerate(((lr_hi, h_hi), (lr_hi, h_lo), (lr_lo, h_hi))):
                            for b, c0, nn in token_cols(TOK):
                                ins = pe.matmul(ps[0:LR_COLS, (5 + 2 * b) * 512:(5 + 2 * b) * 512 + nn], wt[:, w],
                                                a[:, h_at(kc, c0):h_at(kc, c0) + nn], start=kc == 0 and j == 0, stop=kc == KC - 1 and j == 2)
                    ins.then_inc(lr_pe, 1)
                elif 2 <= n < 6:
                    d, hp = divmod(n - 2, 2)
                    pe.wait_ge(lr_act, 1)
                    if n >= 4:
                        pe.wait_ge(gate_act, n - 3)
                    r = slice(32 * d, 32 * d + 16)
                    for b in range(2):
                        ins = pe.matmul(bank(1 + 4 * hp + 2 * b, HALF), gate_sb[r, hp * P:(hp + 1) * P],
                                        lr_t[r, b * HALF:(b + 1) * HALF], start=True, stop=True)
                    ins.then_inc(lr_pe, 1)
                elif n == 7:
                    pe.wait_ge(gate_act, 4)

            def project(n, b0, last_use):
                kind, first, n_p = WIN[n]
                T = TOK if kind in ("rk", "gk") else LAT
                banks = V_BANKS[kind] if kind in V_BANKS else [b0 + b for b, _, _ in token_cols(T)]
                free = max(last_use.get(b, 0) for b in banks)
                if free:
                    pe.wait_ge(win_evac, free)
                for b in banks:
                    last_use[b] = n + 1
                for c in range(n_p):
                    p = P_WIN + first + c
                    pe.wait_ge(lo_done, p + 1)
                    if kind in V_BANKS:
                        panel_rows(p % RING, 2 * c, banks, first=c == 0, last=c == n_p - 1).then_inc(panel_done, 1)
                    else:
                        panel_product(p % RING, b0, h_hi, h_lo, token_cols(T)).then_inc(panel_done, 1)

            def head_mean(j):
                pe.wait_ge(o_copied, j + 1)
                pe.matmul(bank(3), ones_k[:, :], o_sb[:, :], start=True, stop=True).then_inc(mean_ready, 1)

            def head_square_mean(j):
                pe.wait_ge(osq_ready, j + 1)
                pe.matmul(bank(4), ones_k[:, :], o_sq[:, :], start=True, stop=True).then_inc(var_ready, 1)

            def retention():
                pe.wait_ge(win_evac, WIN_ALONE)
                pe.wait_ge(rope_done, 8)
                last_use = {}
                for j in range(HEADS):
                    def scores(j, t):
                        n = j * TILES + t
                        if n >= 2:
                            pe.wait_ge(s_evac, n - 1)
                        pe.matmul(bank(n % 2), rk[:, j * TOK + t * P:j * TOK + (t + 1) * P], rq[:, j * LAT:(j + 1) * LAT],
                                  start=True, stop=True).then_inc(s_ready, 1)

                    def values(t):
                        n = j * TILES + t
                        pe.wait_ge(s_evac, n + 1)
                        v = rv[:, t * 512 + j * P:t * 512 + (j + 1) * P] if t < LT else rv_c[:, (t - LT) * 512 + j * P:(t - LT) * 512 + (j + 1) * P]
                        return pe.matmul(bank(2), v, s_ring[n % 2][:, :], start=t == 0, stop=t == TILES - 1)
                    if j == 0:
                        scores(0, 0)
                    for t in range(1, TILES):
                        scores(j, t)
                        values(t - 1).then_inc(pv_done, 1)
                    values(TILES - 1).then_inc(pv_done, 1)
                    pe.wait_ge(pv_done, TILES * (j + 1))
                    pe.sem_inc(o_ready, 1)
                    project(FILL[j], FILL_BANK, last_use)
                    head_mean(j)
                    if j + 1 < HEADS:
                        scores(j + 1, 0)
                    head_square_mean(j)

            def gla():
                pe.wait_ge(win_evac, len(WIN))

                def unit(hp, u):
                    if hp == 0 and u == 0:
                        pe.wait_ge(oroot_ready, HEADS)
                    if u == -1:
                        pe.wait_ge(qk_ready, n_scaled(hp, 0))
                    if u > 0:
                        pe.wait_ge(qk_ready, n_scaled(hp, u))
                    v = u - 2
                    if u == -1 or u == 0:
                        if hp:
                            pe.wait_ge(unit_act, 3 if u == -1 else 2)
                    elif v == -1:
                        pe.wait_ge(unit_act, 3 * hp + 1)
                    elif v <= MASKED:
                        pe.wait_ge(unit_dve, hp * (MASKED + 1) + v + 1)
                    o = (u % 2) * LAT
                    for a in range(2):
                        r = slice(64 * a, 64 * a + 64)
                        b = unit_bank(u, a)
                        if u == -1:
                            for t in range(2):
                                for d, qq in enumerate((q_lv, k_lv)):
                                    ins = pe.matmul(bank(b + t), ctx_k[hp][r, d * CTX + t * P:d * CTX + (t + 1) * P], qq[r, 0:LAT],
                                                    start=d == 0, stop=d == 1)
                            continue
                        ql, kl = (q_lv[r, o:o + LAT], k_lv[r, o:o + LAT]) if u else \
                            (gq[r, hp * LAT:(hp + 1) * LAT], gk[r, hp * TOK:hp * TOK + LAT])
                        for t in range(LT):
                            if u == TOP:
                                i = (1 - t // 2) * 256
                                ins = pe.matmul(bank(b + t // 2, 256, (t % 2) * 256), kl[:, t * P:(t + 1) * P], ql[:, i:i + 256],
                                                start=True, stop=True)
                            else:
                                i = t if u <= MASKED else t ^ 1
                                ins = pe.matmul(bank(b, P, t * P), kl[:, t * P:(t + 1) * P], ql[:, i * P:(i + 1) * P], start=True, stop=True)
                    ins.then_inc(unit_ready, 1)

                def values(hp):
                    pe.wait_ge(unit_dve, (hp + 1) * (MASKED + 1))
                    pe.wait_ge(unit_act, 3 * (hp + 1))
                    for a in range(2):
                        j = 2 * hp + a
                        if hp:
                            pe.wait_ge(o_scaled, HEADS + a + 1)
                        for t in range(TILES):
                            v = gv[:, t * 512 + j * P:t * 512 + (j + 1) * P] if t < LT else gv_c[:, (t - LT) * 512 + j * P:(t - LT) * 512 + (j + 1) * P]
                            ins = pe.matmul(bank(5 + 2 * a), v, s_gla[:, (a * TILES + t) * LAT:(a * TILES + t + 1) * LAT],
                                            start=t == 0, stop=t == TILES - 1)
                        ins.then_inc(o_ready, 1)

                def pair_stats(hp):
                    pe.wait_ge(osq_ready, HEADS + 2 * hp + 2)
                    for a in range(2):
                        for t in range(LT):
                            ins = pe.matmul(bank(5, 1, a * LT + t), f_pair[a][:, t * P:(t + 1) * P], ones_k[:, 0:1], start=True, stop=True)
                    ins.then_inc(var_ready, 1)

                def pair_spread(hp):
                    pe.wait_ge(hdiag_ready, hp + 1)
                    for a in range(2):
                        ins = pe.matmul(bank(5 + 2 * a), ones_k[:, :], f_pair[a][:, :], start=True, stop=True)
                    ins.then_inc(spread_ready, 1)

                for u in range(-1, TOP + 1):
                    unit(0, u)
                values(0)
                for u in range(-1, TOP + 1):
                    unit(1, u)
                    if u == 0:
                        pair_stats(0)
                    if u == 2:
                        pair_spread(0)
                values(1)
                pair_stats(1)
                pair_spread(1)

            def input_projection2():
                first_pair(P_WIN2, (0, 2), H_BEFORE[4], token_cols(LAT))
                last_use = {0: 1, 2: 2}
                for n, (kind, first, n_p) in enumerate(WIN2[2:], 2):
                    cols = [(0, LAT, CTX)] if kind == "ck" else token_cols(LAT)
                    b0 = 2 * (first % RING)
                    banks = V_BANKS[kind] if kind in V_BANKS else [b0]
                    free = max(last_use.get(b, 0) for b in banks)
                    if free:
                        pe.wait_ge(win2_evac, free)
                    for b in banks:
                        last_use[b] = n + 1
                    for c in range(n_p):
                        p = P_WIN2 + first + c
                        pe.wait_ge(lo_done, p + 1)
                        if kind in V_BANKS:
                            t0, tiles = (0, LT) if kind == "v" else (LT, 2)
                            panel_rows(p % RING, 2 * c, banks, tiles=tiles, t0=t0, first=c == 0, last=c == n_p - 1)\
                                .then_inc(panel_done, 1)
                        else:
                            panel_product(p % RING, b0, h_hi, h_lo, cols).then_inc(panel_done, 1)
                    if n in RG_AFTER:
                        rg_products(RG_AFTER[n])

            def attention(A):
                if A is SELF:
                    pe.wait_ge(win2_evac, len(WIN2))
                    pe.wait_ge(rope2_done, 8)
                dk, kt = A["dk"], A["keys"] // P

                def values(hd):
                    c = hd if dk == P else hd // 2
                    if c >= 2 or A is not SELF:
                        pe.wait_ge(mix_ready, max(A["s0"] + c - 1, A["s0"]))
                    pe.wait_ge(a_copied, A["n0"] + (hd + 1) * LT)
                    r = slice(0, P) if dk == P else slice(64 * (hd % 2), 64 * (hd % 2) + 64)
                    o = ps[r, (4 + c % 2) * 512:(5 + c % 2) * 512]
                    for t in range(kt):
                        v = A["v"][:, t * 512 + hd * dk:t * 512 + (hd + 1) * dk]
                        ins = pe.matmul(o, v, prob_t[:, ((hd % 2) * LT + t) * LAT:((hd % 2) * LT + t + 1) * LAT], start=t == 0, stop=t == kt - 1)
                    ins.then_inc(a_values, 1)

                for n in range(A["n"] + LAG):
                    if n < A["n"]:
                        hd, it = divmod(n, LT)
                        j, r = (hd // 2, slice(64 * (hd % 2), 64 * (hd % 2) + 64)) if dk == DH else (hd, slice(0, P))
                        if n >= 4:
                            pe.wait_ge(a_max if A is SELF else a_exp, A["n0"] + n - 3)
                        pe.matmul(bank(SCORE_BANKS[n % 4], A["keys"]), A["q"][r, j * LAT + it * P:j * LAT + (it + 1) * P],
                                  A["k"][r, j * A["keys"]:(j + 1) * A["keys"]], start=True, stop=True).then_inc(a_scores, 1)
                    if n >= LAG:
                        m = n - LAG
                        hd, it = divmod(m, LT)
                        N = A["n0"] + m
                        pe.wait_ge(a_prob, N + 1)
                        if m >= 2:
                            pe.wait_ge(a_copied, N - 1)
                        for t in range(kt):
                            ins = pe.transpose(bank(2 + m % 2, P, t * P), prob[:, (N % P_BUFS) * LAT + t * P:(N % P_BUFS) * LAT + (t + 1) * P], ident[:, :])
                        ins.then_inc(a_trans, 1)
                        if it == 0 and hd:
                            values(hd - 1)
                values(A["n"] // LT - 1)

            def rg_products(c):
                pe.wait_ge(rg_loaded, 16)
                pe.wait_ge(rg_conv, c + 1)
                if c:
                    pe.wait_ge(rg_sig, c)
                for z in range(2):
                    for g in range(2):
                        w = ((2 * z + g) * 4 + c) * P
                        ins = pe.matmul(bank(1 + 4 * z + 2 * g), rg_sb[:, w:w + P], uc[:, c * LAT:(c + 1) * LAT], start=True, stop=True)
                ins.then_inc(rg_gates, 1)

            def cross_queries():
                first_pair(P_CQ, (0, 2), H_BEFORE[5], token_cols(LAT))
                for j in range(2, 4):
                    pe.wait_ge(lo_done, P_CQ + j + 1)
                    panel_product(j, 2 * j, h_hi, h_lo, token_cols(LAT)).then_inc(panel_done, 1)
                pe.wait_ge(cq_evac, 4)

            def cross_output():
                for c in range(RING):
                    pe.wait_ge(lo_done, P_CO + c + 1)
                    for e in range(2):
                        ready = (lambda kc: (mix_ready, 16 + kc + 1)) if c == 0 and e == 0 else None
                        ins = panel_product(c, 2 * c + e, o_hi, o_lo, token_cols(LAT), n_k=4, ready=ready, off=4 * e, at_=merged_at)
                    ins.then_inc(panel_done, 1)

            def residual(p0, o0, a_hi, a_lo, n_k, ready):
                with pe.Fori(0, KC // RING) as i:
                    for c in range(RING):
                        pe.wait_ge(down_evac, o0 + i * RING + c + RING + 1)
                        pe.wait_ge(lo_done, p0 + i * RING + c + 1)
                        panel_product(c, 2 * c, a_hi, a_lo, token_cols(LAT), n_k=n_k, ready=ready if c == 0 else None,
                                      at_=merged_at).then_inc(panel_done, 1)

            pe.sem_inc(panel_done, RING)
            first_modulation(0, 3)
            norm(norms[0])
            first_modulation(3, ADA_PE)
            for G in GROUPS[0:3]:
                hidden_up(G, 0)
                hidden_down(G)
            norm(norms[1])
            input_projection()
            retention()
            gla()
            residual(P_WOUT, 3 * KC, o_hi, o_lo, KC, lambda kc: (mix_ready, kc + 1))
            norm(norms[2])
            for G in GROUPS[3:6]:
                hidden_up(G, H_BEFORE[2])
                hidden_down(G)
            norm(norms[4])
            input_projection2()
            attention(SELF)
            residual(P_WOUT2, 7 * KC, o_hi, o_lo, KC, lambda kc: (mix_ready, min(13 + kc, 16)))
            norm(norms[5])
            cross_queries()
            attention(CROSS)
            cross_output()
            norm(norms[6])
            for G in GROUPS[6:10]:
                hidden_up(G, H_BEFORE[6])
                hidden_down(G)
            norm(norms[7])


def rotary_order(parts, n):
    order = []
    for part in range(parts):
        for f in range(0, n, 16):
            order += [part * 2 * n + f + j for j in range(16)] + [part * 2 * n + n + f + j for j in range(16)]
    return order


def shape_tables():
    tok = np.arange(LAT)
    freqs = 10000.0 ** (-np.arange(32) / 32)
    angle = np.zeros((P, LAT))
    sign = np.zeros((P, 1))
    for p, d in enumerate(rotary_order(2, 32)):
        pos = (tok // 64) if d < 64 else (tok % 64)
        angle[p] = pos * np.float32(freqs[d % 32])
        sign[p] = -1.0 if d % 64 < 32 else 1.0
    rope_grid = np.concatenate([np.cos(angle), sign * np.sin(angle)], axis=1)
    p = np.arange(P)[:, None]
    u_tab = np.arange(UW)[None, :] - 384 - p
    i = np.arange(P)[None, :]
    level_masks = np.concatenate([((p // (2 * h) == i // (2 * h)) & (p // h != i // h)) for h in LEVELS], axis=1)
    return {"rope_grid": rope_grid.astype(np.float32), "u_tab": u_tab.astype(np.float32),
            "level_masks": level_masks.astype(np.int32), "diag2": (2.0 * np.eye(P)).astype(np.float32),
            "ident": np.eye(P, dtype=np.float32)}


def window_tables():
    inv_freq = np.float32(10000.0) ** (-np.arange(32, dtype=np.float32) / np.float32(32))
    order = rotary_order(1, 32) * 2
    pp = np.array([[inv_freq[d % 32], -1.0 if d < 32 else 1.0] for d in order], np.float32)
    i, j = np.arange(LAT)[:, None], np.arange(LAT)[None, :]
    times = sum(((i - j) % dil == 0) & (abs(i - j) <= window // 2) for window, dil in ((128, 1), (512, 4), (2048, 16)))
    bias = np.where(times > 0, np.log(np.maximum(times, 1)) * DH ** 0.5, -1e30)
    bias = bias.reshape(LT, P, LAT).transpose(1, 0, 2).reshape(P, LT * LAT)
    return {"rope_pp_h": pp, "window_bias": bias.astype(np.float32)}


def kernel(**inputs):
    import concourse.bacc as bacc
    from concourse.bass_utils import run_bass_kernel_spmd

    def feature_major(a):
        return np.ascontiguousarray(a.reshape(a.shape[0], KC, P).transpose(2, 1, 0).reshape(P, -1))

    def columns(a):
        return a.reshape(-1, P).T

    a = {k: np.asarray(v) for k, v in inputs.items()}
    vecs = np.zeros((P, N_VEC), np.float32)
    for name, n in VEC_WIDTHS.items():
        v = a[name]
        if name == "conv_w_2":
            v = v.reshape(4, 4 * P)
        vecs[:, VEC_AT[name]:VEC_AT[name] + n] = columns(v)
    panels = np.zeros((N_PANELS, P, PANEL), np.float32)
    at = [0]

    def put(w, k0, n_k, c0):
        block = w[k0 * P:(k0 + n_k) * P, c0:c0 + P].reshape(n_k, P, P).transpose(1, 0, 2)
        panels[at[0], :, 0:n_k * P] = block.reshape(P, n_k * P)
        at[0] += 1

    def put_ffn(w1, w3, w2):
        f = 0
        for g in FF_GROUPS:
            for j in range(g):
                put(w1, 0, KC, (f + j) * P)
                put(w3, 0, KC, (f + j) * P)
            for o in range(KC):
                put(w2, f, g, o * P)
            f += g

    def put_rows(w, c0):
        for k in range(0, KC, 2):
            block = w[k * P:(k + 2) * P, c0:c0 + 512].reshape(2, P, 512).transpose(1, 0, 2)
            panels[at[0]] = block.reshape(P, PANEL)
            at[0] += 1

    put_ffn(a["ffn1_w1"][0], a["ffn1_w3"][0], a["ffn1_w2"][0])
    w = a["w_in"][0]
    assert at[0] == P_WIN
    rotated = [w[:, c0:c0 + 512].reshape(D, HEADS, P)[:, :, rotary_order(2, 32)].reshape(D, 512) for c0 in (0, 512)]
    for j in range(HEADS):
        put(rotated[0], 0, KC, j * P)
    for c0 in range(1536, 2048, P):
        put(w, 0, KC, c0)
    for j in range(HEADS):
        put(rotated[1], 0, KC, j * P)
    put_rows(w, 1024)
    put_rows(w, 2560)
    for c0 in (2304, 2304 + P, 2048, 2048 + P, *range(3072, 3584, P)):
        put(w, 0, KC, c0)
    assert at[0] == P_WOUT
    for o in range(KC):
        put(a["w_out"][0], 0, KC, o * P)
    put_ffn(a["ffn2_w1"][0], a["ffn2_w3"][0], a["ffn2_w2"][0])
    assert at[0] == P_WIN2
    w2 = a["w_in_2"][0]
    for c0 in range(1536, 2560, P):
        put(w2, 0, KC, c0)
    for c0 in (0, 512):
        rot = w2[:, c0:c0 + 512].reshape(D, 8, DH)[:, :, rotary_order(1, 32)].reshape(D, 512)
        for j in range(4):
            put(rot, 0, KC, j * P)
    put_rows(w2, 1024)
    for c0 in range(0, 512, P):
        put(a["w_ck_2"][0], 0, KC, c0)
    put_rows(a["w_cv_2"][0], 0)
    assert at[0] == P_WOUT2
    for o in range(KC):
        put(a["w_out_2"][0], 0, KC, o * P)
    for o in range(4):
        put(a["w_cq_2"][0], 0, KC, o * P)
    for o in range(0, KC, 2):
        for e in range(2):
            block = a["w_co_2"][0][:, (o + e) * P:(o + e + 1) * P].reshape(4, P, P).transpose(1, 0, 2)
            panels[at[0], :, e * 512:(e + 1) * 512] = block.reshape(P, 512)
        at[0] += 1
    assert at[0] == P_MLP
    for f in range(0, DFF2 // P, 8):
        for j in range(8):
            put(a["w_mlp_in_2"][0], 0, KC, (f + j) * P)
        for o in range(KC):
            put(a["w_mlp_out_2"][0], f, 8, o * P)
    assert at[0] == N_PANELS
    rg_w = np.zeros((P, 2, 2, 4, P), np.float32)
    for z in range(2):
        for g, name in enumerate(("rg_a_w_2", "rg_x_w_2")):
            for n in range(8):
                r = slice(64 * (n % 2), 64 * (n % 2) + 64)
                rg_w[r, z, g, n // 2, r] = a[name][0, z, n]
    cond = np.concatenate([a["c"][0], a["c_ctx"]])
    lr_w, gate_w = np.zeros((P, KC, LR_COLS), np.float32), np.zeros((LR_COLS, 256), np.float32)
    for d, name in enumerate(("gla_gate_w_f", "gla_gate_w_b")):
        lr_w[:, :, 32 * d:32 * d + 16] = w[:, 3584 + 16 * d:3600 + 16 * d].reshape(KC, P, 16).transpose(1, 0, 2)
        gate_w[32 * d:32 * d + 16] = a[name][0]
    ada_p = np.stack([a["ada_w"][0][:, k * P:(k + 1) * P].reshape(KC, P, P).transpose(1, 0, 2).reshape(P, PANEL) for k in range(ADA_PE)])
    arrays = {
        "x_t": feature_major(a["x"][0]),
        "ctx_t": feature_major(a["ctx"][0]),
        "cond": cond,
        "ada_t": np.ascontiguousarray(a["ada_w"][0].T.reshape(NMOD * KC, P, D)),
        "vecs": vecs,
        "panels": panels,
        "lr_w": lr_w.reshape(P, KC * LR_COLS),
        "gate_w": gate_w,
        "decays": np.concatenate([a["ret_decay_f"][0], a["ret_decay_b"][0]]),
        **shape_tables(),
        "ada_p": ada_p,
        "cond_t": np.ascontiguousarray(cond.reshape(2, KC, P).transpose(2, 1, 0).reshape(P, 2 * KC)),
        "mem_t": feature_major(a["mem_2"][0]),
        "positions": np.ascontiguousarray(a["positions_2"][0]),
        **window_tables(),
        "rg_w": rg_w.reshape(P, 16 * P),
    }
    nc = bacc.Bacc("TRN2", target_bir_lowering=False, num_devices=1)
    args = [nc.dram_tensor(n, v.shape, mybir.dt.from_np(v.dtype), kind="ExternalInput").ap() for n, v in arrays.items()]
    out = nc.dram_tensor("out", (1, P, KC * LAT), mybir.dt.float32, kind="ExternalOutput").ap()
    build(nc, *args, out)
    r = run_bass_kernel_spmd(nc, [arrays], core_ids=[0])
    got = r.results[0]["out"]
    return np.ascontiguousarray(got.reshape(P, KC, LAT).transpose(2, 1, 0).reshape(1, LAT, D))
```
